# Optimizing a Trainium2 kernel written in Bass

```python
import jax, jax.numpy as jnp
from jax import lax
import numpy as np

D_MODEL = 1024
BATCH = 1
SEQ = 256
DEPTH = 2

HEAD_DIM = 64
N_MEM = 256
MEM_HEADS = 4
CROSS_WIDTH = MEM_HEADS * HEAD_DIM
MIX_WIDTH = 12 * HEAD_DIM
ATTN_WIDTH = MIX_WIDTH + CROSS_WIDTH
EPS = 1e-6
NEG = -1e30
MLA_HEADS = 12
MLA_Q_RANK = 384
MLA_KV_RANK = 256
MLA_NOPE = 64
MLA_ROPE = 32
MLA_V = 64
MLA_QK = MLA_NOPE + MLA_ROPE
ROPE_THETA = 10000.0
Q_BLOCK = 128
MLA_IN = MLA_Q_RANK + MLA_KV_RANK + MLA_ROPE + CROSS_WIDTH
SWA_Q_HEADS = 12
SWA_KV_HEADS = 4
SWA_GROUP = SWA_Q_HEADS // SWA_KV_HEADS
WINDOW = 128
SWA_IN = (SWA_Q_HEADS + 2 * SWA_KV_HEADS) * HEAD_DIM + CROSS_WIDTH
D_FF = 4 * D_MODEL
N_MLA_LAYERS = (DEPTH + 1) // 2
N_SWA_LAYERS = DEPTH // 2


def rmsnorm(x, g):
    xf = x.astype(jnp.float32)
    y = xf * lax.rsqrt(jnp.mean(xf * xf, axis=-1, keepdims=True) + EPS)
    return (y * g.astype(jnp.float32)).astype(x.dtype)

def rope(x, positions):
    r = x.shape[-1]
    half = r // 2
    inv = ROPE_THETA ** (-(jnp.arange(half, dtype=jnp.float32) * 2.0) / r)
    ang = positions.astype(jnp.float32)[..., None] * inv
    cos = jnp.cos(ang)[:, :, None, :]
    sin = jnp.sin(ang)[:, :, None, :]
    xf = x.astype(jnp.float32)
    x1, x2 = xf[..., :half], xf[..., half:]
    out = jnp.concatenate([x1 * cos - x2 * sin, x1 * sin + x2 * cos], axis=-1)
    return out.astype(x.dtype)

def alibi_slopes(n_heads):
    return 2.0 ** (-8.0 * (jnp.arange(n_heads, dtype=jnp.float32) + 1.0) / n_heads)

def causal_dense_attention(q, k, v):
    b, s, h, dk = q.shape
    dv = v.shape[-1]
    nb = s // Q_BLOCK
    scale = dk ** -0.5
    qb = q.reshape(b, nb, Q_BLOCK, h, dk).transpose(1, 0, 2, 3, 4)
    k_idx = jnp.arange(s)

    def one_block(args):
        q_blk, n = args
        t_idx = n * Q_BLOCK + jnp.arange(Q_BLOCK)
        sc = jnp.einsum('bqhd,bkhd->bhqk', q_blk, k,
                        preferred_element_type=jnp.float32) * scale
        mask = k_idx[None, :] <= t_idx[:, None]
        sc = jnp.where(mask[None, None], sc, NEG)
        p = jax.nn.softmax(sc, axis=-1).astype(v.dtype)
        return jnp.einsum('bhqk,bkhd->bqhd', p, v)

    out = lax.map(one_block, (qb, jnp.arange(nb)))
    return out.transpose(1, 0, 2, 3, 4).reshape(b, s, h, dv)

def mla_mixer(hn, positions, w_in, q_norm_g, kv_norm_g, w_uq, w_ukv):
    b, s, _ = hn.shape
    proj = hn @ w_in
    c_q = proj[..., :MLA_Q_RANK]
    c_kv = proj[..., MLA_Q_RANK:MLA_Q_RANK + MLA_KV_RANK]
    k_r = proj[..., MLA_Q_RANK + MLA_KV_RANK:MLA_Q_RANK + MLA_KV_RANK + MLA_ROPE]
    q_cross = proj[..., MLA_Q_RANK + MLA_KV_RANK + MLA_ROPE:]
    q = (rmsnorm(c_q, q_norm_g) @ w_uq).reshape(b, s, MLA_HEADS, MLA_QK)
    q = jnp.concatenate([q[..., :MLA_NOPE], rope(q[..., MLA_NOPE:], positions)], axis=-1)
    kv = (rmsnorm(c_kv, kv_norm_g) @ w_ukv).reshape(b, s, MLA_HEADS, MLA_NOPE + MLA_V)
    k_nope, v = kv[..., :MLA_NOPE], kv[..., MLA_NOPE:]
    k_rope = jnp.broadcast_to(rope(k_r[:, :, None, :], positions),
                              (b, s, MLA_HEADS, MLA_ROPE))
    k = jnp.concatenate([k_nope, k_rope], axis=-1)
    o = causal_dense_attention(q, k, v)
    return o.reshape(b, s, MLA_HEADS * MLA_V), q_cross

def _with_prev_block(a):
    pad = [(0, 0), (1, 0)] + [(0, 0)] * (a.ndim - 2)
    prev = jnp.pad(a[:, :-1], pad)
    return jnp.concatenate([prev, a], axis=2)

def swa_mixer(hn, positions, w_in, sinks):
    b, s, _ = hn.shape
    nb = s // WINDOW
    proj = hn @ w_in
    nq = SWA_Q_HEADS * HEAD_DIM
    nk = SWA_KV_HEADS * HEAD_DIM
    q = proj[..., :nq].reshape(b, nb, WINDOW, SWA_KV_HEADS, SWA_GROUP, HEAD_DIM)
    k = proj[..., nq:nq + nk].reshape(b, nb, WINDOW, SWA_KV_HEADS, HEAD_DIM)
    v = proj[..., nq + nk:nq + 2 * nk].reshape(b, nb, WINDOW, SWA_KV_HEADS, HEAD_DIM)
    q_cross = proj[..., nq + 2 * nk:]
    kk = _with_prev_block(k)
    vv = _with_prev_block(v)
    pos_q = positions.reshape(b, nb, WINDOW)
    pos_k = _with_prev_block(pos_q)
    sc = jnp.einsum('bnqhgd,bnkhd->bnhgqk', q, kk,
                    preferred_element_type=jnp.float32) * (HEAD_DIM ** -0.5)
    dist = (pos_q[..., :, None] - pos_k[..., None, :]).astype(jnp.float32)
    slopes = alibi_slopes(SWA_Q_HEADS).reshape(SWA_KV_HEADS, SWA_GROUP)
    sc = sc - slopes[None, None, :, :, None, None] * dist[:, :, None, None]
    qi = jnp.arange(WINDOW)[:, None]
    kj = jnp.arange(2 * WINDOW)[None, :]
    rel = WINDOW + qi - kj
    band = (rel >= 0) & (rel < WINDOW)
    valid = band[None] & ((jnp.arange(nb)[:, None, None] > 0) | (kj >= WINDOW)[None])
    sc = jnp.where(valid[None, :, None, None], sc, NEG)
    sink = sinks.astype(jnp.float32).reshape(SWA_KV_HEADS, SWA_GROUP)[None, None, :, :, None, None]
    sink = jnp.broadcast_to(sink, sc.shape[:-1] + (1,))
    p = jax.nn.softmax(jnp.concatenate([sc, sink], axis=-1), axis=-1)[..., :-1]
    o = jnp.einsum('bnhgqk,bnkhd->bnqhgd', p.astype(vv.dtype), vv)
    return o.reshape(b, s, SWA_Q_HEADS * HEAD_DIM), q_cross

def memory_cross_attention(q_cross, mem_n, w_mem_kv):
    b, s, _ = q_cross.shape
    kv = (mem_n @ w_mem_kv).reshape(b, N_MEM, 2, MEM_HEADS, HEAD_DIM)
    k, v = kv[:, :, 0], kv[:, :, 1]
    q = q_cross.reshape(b, s, MEM_HEADS, HEAD_DIM)
    sc = jnp.einsum('bshd,bmhd->bhsm', q, k,
                    preferred_element_type=jnp.float32) * (HEAD_DIM ** -0.5)
    p = jax.nn.softmax(sc, axis=-1).astype(v.dtype)
    return jnp.einsum('bhsm,bmhd->bshd', p, v).reshape(b, s, CROSS_WIDTH)

def squared_relu_mlp(h, w_up, w_down):
    a = jax.nn.relu(h @ w_up)
    return (a * a) @ w_down

def first_inputs(seed: int = 0) -> dict:
    key = jax.random.key(seed)
    ks = jax.random.split(key, 20)

    def w(k, shape, fan_in):
        return jax.random.normal(k, shape, jnp.float32) * (fan_in ** -0.5)

    def gain(k, shape):
        return 1.0 + 0.02 * jax.random.normal(k, shape, jnp.float32)

    x = jax.random.normal(ks[0], (BATCH, SEQ, D_MODEL), jnp.float32)
    mem = jax.random.normal(ks[1], (BATCH, N_MEM, D_MODEL), jnp.float32)
    offsets = jax.random.randint(ks[2], (BATCH, 1), 0, 1024, dtype=jnp.int32)
    positions = (offsets + jnp.arange(SEQ, dtype=jnp.int32)[None, :]).astype(jnp.int32)
    return {
        "x": x,
        "mem": mem,
        "positions": positions,
        "attn_norm_g": gain(ks[3], (DEPTH, D_MODEL)),
        "mlp_norm_g": gain(ks[4], (DEPTH, D_MODEL)),
        "mem_norm_g": gain(ks[5], (D_MODEL,)),
        "final_norm_g": gain(ks[6], (D_MODEL,)),
        "mla_w_in": w(ks[7], (N_MLA_LAYERS, D_MODEL, MLA_IN), D_MODEL),
        "mla_q_norm_g": gain(ks[8], (N_MLA_LAYERS, MLA_Q_RANK)),
        "mla_kv_norm_g": gain(ks[9], (N_MLA_LAYERS, MLA_KV_RANK)),
        "mla_w_uq": w(ks[10], (N_MLA_LAYERS, MLA_Q_RANK, MLA_HEADS * MLA_QK), MLA_Q_RANK),
        "mla_w_ukv": w(ks[11], (N_MLA_LAYERS, MLA_KV_RANK, MLA_HEADS * (MLA_NOPE + MLA_V)), MLA_KV_RANK),
        "swa_w_in": w(ks[12], (N_SWA_LAYERS, D_MODEL, SWA_IN), D_MODEL),
        "swa_sinks": 0.5 * jax.random.normal(ks[13], (N_SWA_LAYERS, SWA_Q_HEADS), jnp.float32),
        "w_mem_kv": w(ks[14], (DEPTH, D_MODEL, 2 * CROSS_WIDTH), D_MODEL),
        "w_o": w(ks[15], (DEPTH, ATTN_WIDTH, D_MODEL), ATTN_WIDTH),
        "mlp_w_up": w(ks[16], (DEPTH, D_MODEL, D_FF), D_MODEL),
        "mlp_w_down": w(ks[17], (DEPTH, D_FF, D_MODEL), D_FF),
    }

def first_block(x, mem, positions, attn_norm_g, mlp_norm_g, mem_norm_g, final_norm_g,
              mla_w_in, mla_q_norm_g, mla_kv_norm_g, mla_w_uq, mla_w_ukv,
              swa_w_in, swa_sinks, w_mem_kv, w_o, mlp_w_up, mlp_w_down):
    mem_n = rmsnorm(mem, mem_norm_g)
    for i in range(DEPTH):
        j = i // 2
        hn = rmsnorm(x, attn_norm_g[i])
        if i % 2 == 0:
            mix, q_cross = mla_mixer(hn, positions, mla_w_in[j], mla_q_norm_g[j],
                                     mla_kv_norm_g[j], mla_w_uq[j], mla_w_ukv[j])
        else:
            mix, q_cross = swa_mixer(hn, positions, swa_w_in[j], swa_sinks[j])
        cross = memory_cross_attention(q_cross, mem_n, w_mem_kv[i])
        x = x + jnp.concatenate([mix, cross], axis=-1) @ w_o[i]
        x = x + squared_relu_mlp(rmsnorm(x, mlp_norm_g[i]), mlp_w_up[i], mlp_w_down[i])
    return rmsnorm(x, final_norm_g)


CHUNK = 64
CONV_WIDTH = D_MODEL // 2
LRU_WIDTH = D_MODEL // 2
CONV_GROUPS = CONV_WIDTH // HEAD_DIM
LRU_HEADS = LRU_WIDTH // HEAD_DIM
SHORT_CONV_K = 3
LRU_CONV_K = 4
RG_C = 8.0
SB_HEADS = D_MODEL // HEAD_DIM
D_FF_2 = ((8 * D_MODEL // 3 + 255) // 256) * 256
N_MOD = 6


def rms_norm(x, g):
    x32 = x.astype(jnp.float32)
    y = x32 * lax.rsqrt(jnp.mean(x32 * x32, axis=-1, keepdims=True) + EPS)
    return (y * g.astype(jnp.float32)).astype(x.dtype)

def ada_modulation(c, ada_w, ada_b):
    m = jax.nn.silu(c) @ ada_w + ada_b
    return jnp.split(m, N_MOD, axis=-1)

def modulate(h, shift, scale):
    return h * (1.0 + scale[:, None, :]) + shift[:, None, :]

def causal_depthwise_conv(x, w):
    k_width = w.shape[0]
    seq = x.shape[1]
    xp = jnp.pad(x, ((0, 0), (k_width - 1, 0), (0, 0)))
    y = xp[:, 0:seq] * w[0]
    for k in range(1, k_width):
        y = y + xp[:, k:k + seq] * w[k]
    return y

def rg_lru(xr, w_a, b_a, w_x, b_x, lam):
    bsz, seq, width = xr.shape
    n_blk, blk = w_a.shape[0], w_a.shape[1]
    x32 = xr.astype(jnp.float32)
    xh = x32.reshape(bsz, seq, n_blk, blk)
    r = jax.nn.sigmoid(jnp.einsum('bshi,hij->bshj', xh, w_a.astype(jnp.float32)) + b_a).reshape(bsz, seq, width)
    i = jax.nn.sigmoid(jnp.einsum('bshi,hij->bshj', xh, w_x.astype(jnp.float32)) + b_x).reshape(bsz, seq, width)
    log_a = -RG_C * r * jax.nn.softplus(-lam.astype(jnp.float32))
    a = jnp.exp(log_a)
    b = jnp.sqrt(-jnp.expm1(2.0 * log_a)) * (i * x32)
    n_chunks = seq // CHUNK
    a_c = a.reshape(bsz, n_chunks, CHUNK, width).transpose(1, 0, 2, 3)
    b_c = b.reshape(bsz, n_chunks, CHUNK, width).transpose(1, 0, 2, 3)

    def combine(lhs, rhs):
        al, bl = lhs
        ar, br = rhs
        return al * ar, ar * bl + br

    def chunk_step(h0, ab):
        a_k, b_k = ab
        a_cum, b_cum = lax.associative_scan(combine, (a_k, b_k), axis=1)
        h = a_cum * h0[:, None, :] + b_cum
        return h[:, -1], h

    h_init = jnp.zeros((bsz, width), jnp.float32)
    _, hs = lax.scan(chunk_step, h_init, (a_c, b_c))
    return hs.transpose(1, 0, 2, 3).reshape(bsz, seq, width)

def stick_breaking_attention(q, k, v):
    seq, dh = q.shape[2], q.shape[3]
    scale = dh ** -0.5
    outs = []
    for blk in range(seq // Q_BLOCK):
        q0, q1 = blk * Q_BLOCK, (blk + 1) * Q_BLOCK
        qb = q[:, :, q0:q1].astype(jnp.float32)
        kb = k[:, :, :q1].astype(jnp.float32)
        vb = v[:, :, :q1].astype(jnp.float32)
        z = jnp.einsum('bhqd,bhkd->bhqk', qb, kb) * scale
        q_pos = jnp.arange(q0, q1)[:, None]
        k_pos = jnp.arange(q1)[None, :]
        strict = k_pos < q_pos
        log_keep = jnp.where(strict, jax.nn.log_sigmoid(-z), 0.0)
        prefix = jnp.cumsum(log_keep, axis=-1)
        after = prefix[..., -1:] - prefix
        w = jnp.where(strict, jnp.exp(jax.nn.log_sigmoid(z) + after), 0.0)
        outs.append(jnp.einsum('bhqk,bhkd->bhqd', w, vb))
    return jnp.concatenate(outs, axis=2)

def swiglu(h, w_gate, w_up, w_down):
    return (jax.nn.silu(h @ w_gate) * (h @ w_up)) @ w_down

def even_layer(x, c, ada_w, ada_b, mix_norm, w_in, conv_a_w, conv_b_w, conv_b_b,
               rg_a_w, rg_a_b, rg_x_w, rg_x_b, rg_lambda, w_out,
               ffn_norm, ffn_w_gate, ffn_w_up, ffn_w_down):
    sh_m, sc_m, g_m, sh_f, sc_f, g_f = ada_modulation(c, ada_w, ada_b)
    h = modulate(rms_norm(x, mix_norm), sh_m, sc_m)
    u = h @ w_in
    cuts = [CONV_WIDTH, 2 * CONV_WIDTH, 3 * CONV_WIDTH, 3 * CONV_WIDTH + LRU_WIDTH]
    a_b, a_c, a_x, r_gate, r_x = jnp.split(u, cuts, axis=-1)
    y_a = a_b * causal_depthwise_conv(a_c * a_x, conv_a_w)
    xr = causal_depthwise_conv(r_x, conv_b_w) + conv_b_b
    y_b = jax.nn.gelu(r_gate) * rg_lru(xr, rg_a_w, rg_a_b, rg_x_w, rg_x_b, rg_lambda).astype(x.dtype)
    y = jnp.concatenate([y_a, y_b], axis=-1) @ w_out
    x = x + g_m[:, None, :] * y
    hf = modulate(rms_norm(x, ffn_norm), sh_f, sc_f)
    return x + g_f[:, None, :] * swiglu(hf, ffn_w_gate, ffn_w_up, ffn_w_down)

def odd_layer(x, c, ada_w, ada_b, mix_norm, w_qkv, q_norm, k_norm, w_out,
              ffn_norm, ffn_w_gate, ffn_w_up, ffn_w_down):
    sh_m, sc_m, g_m, sh_f, sc_f, g_f = ada_modulation(c, ada_w, ada_b)
    h = modulate(rms_norm(x, mix_norm), sh_m, sc_m)
    bsz, seq, _ = x.shape
    qkv = (h @ w_qkv).reshape(bsz, seq, 3, SB_HEADS, HEAD_DIM)
    q = rms_norm(qkv[:, :, 0], q_norm).transpose(0, 2, 1, 3)
    k = rms_norm(qkv[:, :, 1], k_norm).transpose(0, 2, 1, 3)
    v = qkv[:, :, 2].transpose(0, 2, 1, 3)
    o = stick_breaking_attention(q, k, v).astype(x.dtype)
    o = o.transpose(0, 2, 1, 3).reshape(bsz, seq, SB_HEADS * HEAD_DIM)
    x = x + g_m[:, None, :] * (o @ w_out)
    hf = modulate(rms_norm(x, ffn_norm), sh_f, sc_f)
    return x + g_f[:, None, :] * swiglu(hf, ffn_w_gate, ffn_w_up, ffn_w_down)

def second_inputs(seed: int = 0) -> dict:
    key = jax.random.key(seed)
    ks = jax.random.split(key, 40)
    f32 = jnp.float32

    def nrm(k, shape, scale):
        return jax.random.normal(k, shape, f32) * scale

    d = D_MODEL
    u = jax.random.uniform(ks[12], (LRU_WIDTH,), f32, 0.9, 0.999)
    a0 = u ** (1.0 / RG_C)
    lam = jnp.log(a0) - jnp.log1p(-a0)
    return {
        'x': nrm(ks[0], (BATCH, SEQ, d), 1.0),
        'c': nrm(ks[1], (BATCH, d), 1.0),
        'l0_ada_w': nrm(ks[2], (d, N_MOD * d), 0.5 * d ** -0.5),
        'l0_ada_b': nrm(ks[3], (N_MOD * d,), 0.02),
        'l0_mix_norm': 1.0 + nrm(ks[4], (d,), 0.02),
        'l0_w_in': nrm(ks[5], (d, 3 * CONV_WIDTH + 2 * LRU_WIDTH), d ** -0.5),
        'l0_conv_a_w': nrm(ks[6], (SHORT_CONV_K, CONV_WIDTH), SHORT_CONV_K ** -0.5),
        'l0_conv_b_w': nrm(ks[7], (LRU_CONV_K, LRU_WIDTH), LRU_CONV_K ** -0.5),
        'l0_conv_b_b': nrm(ks[8], (LRU_WIDTH,), 0.01),
        'l0_rg_a_w': nrm(ks[9], (LRU_HEADS, HEAD_DIM, HEAD_DIM), HEAD_DIM ** -0.5),
        'l0_rg_a_b': nrm(ks[10], (LRU_HEADS, HEAD_DIM), 0.01),
        'l0_rg_x_w': nrm(ks[11], (LRU_HEADS, HEAD_DIM, HEAD_DIM), HEAD_DIM ** -0.5),
        'l0_rg_x_b': nrm(ks[13], (LRU_HEADS, HEAD_DIM), 0.01),
        'l0_rg_lambda': lam,
        'l0_w_out': nrm(ks[14], (CONV_WIDTH + LRU_WIDTH, d), (CONV_WIDTH + LRU_WIDTH) ** -0.5),
        'l0_ffn_norm': 1.0 + nrm(ks[15], (d,), 0.02),
        'l0_ffn_w_gate': nrm(ks[16], (d, D_FF_2), d ** -0.5),
        'l0_ffn_w_up': nrm(ks[17], (d, D_FF_2), d ** -0.5),
        'l0_ffn_w_down': nrm(ks[18], (D_FF_2, d), D_FF_2 ** -0.5),
        'l1_ada_w': nrm(ks[19], (d, N_MOD * d), 0.5 * d ** -0.5),
        'l1_ada_b': nrm(ks[20], (N_MOD * d,), 0.02),
        'l1_mix_norm': 1.0 + nrm(ks[21], (d,), 0.02),
        'l1_w_qkv': nrm(ks[22], (d, 3 * SB_HEADS * HEAD_DIM), d ** -0.5),
        'l1_q_norm': 1.0 + nrm(ks[23], (HEAD_DIM,), 0.02),
        'l1_k_norm': 1.0 + nrm(ks[24], (HEAD_DIM,), 0.02),
        'l1_w_out': nrm(ks[25], (SB_HEADS * HEAD_DIM, d), (SB_HEADS * HEAD_DIM) ** -0.5),
        'l1_ffn_norm': 1.0 + nrm(ks[26], (d,), 0.02),
        'l1_ffn_w_gate': nrm(ks[27], (d, D_FF_2), d ** -0.5),
        'l1_ffn_w_up': nrm(ks[28], (d, D_FF_2), d ** -0.5),
        'l1_ffn_w_down': nrm(ks[29], (D_FF_2, d), D_FF_2 ** -0.5),
    }

def second_block(x, c,
              l0_ada_w, l0_ada_b, l0_mix_norm, l0_w_in, l0_conv_a_w, l0_conv_b_w, l0_conv_b_b,
              l0_rg_a_w, l0_rg_a_b, l0_rg_x_w, l0_rg_x_b, l0_rg_lambda, l0_w_out,
              l0_ffn_norm, l0_ffn_w_gate, l0_ffn_w_up, l0_ffn_w_down,
              l1_ada_w, l1_ada_b, l1_mix_norm, l1_w_qkv, l1_q_norm, l1_k_norm, l1_w_out,
              l1_ffn_norm, l1_ffn_w_gate, l1_ffn_w_up, l1_ffn_w_down):
    even_params = [(l0_ada_w, l0_ada_b, l0_mix_norm, l0_w_in, l0_conv_a_w, l0_conv_b_w, l0_conv_b_b,
                    l0_rg_a_w, l0_rg_a_b, l0_rg_x_w, l0_rg_x_b, l0_rg_lambda, l0_w_out,
                    l0_ffn_norm, l0_ffn_w_gate, l0_ffn_w_up, l0_ffn_w_down)]
    odd_params = [(l1_ada_w, l1_ada_b, l1_mix_norm, l1_w_qkv, l1_q_norm, l1_k_norm, l1_w_out,
                   l1_ffn_norm, l1_ffn_w_gate, l1_ffn_w_up, l1_ffn_w_down)]
    for layer in range(DEPTH):
        if layer % 2 == 0:
            x = even_layer(x, c, *even_params[layer // 2])
        else:
            x = odd_layer(x, c, *odd_params[layer // 2])
    return x


def setup_inputs(seed=0):
    out = dict(first_inputs(seed))
    for name, value in second_inputs(seed + 1).items():
        if name != "x":
            out[name + "_2"] = value
    return out


def reference(
    x, mem, positions, attn_norm_g, mlp_norm_g, mem_norm_g, final_norm_g, mla_w_in,
    mla_q_norm_g, mla_kv_norm_g, mla_w_uq, mla_w_ukv, swa_w_in, swa_sinks, w_mem_kv, w_o,
    mlp_w_up, mlp_w_down, c_2, l0_ada_w_2, l0_ada_b_2, l0_mix_norm_2, l0_w_in_2, l0_conv_a_w_2,
    l0_conv_b_w_2, l0_conv_b_b_2, l0_rg_a_w_2, l0_rg_a_b_2, l0_rg_x_w_2, l0_rg_x_b_2,
    l0_rg_lambda_2, l0_w_out_2, l0_ffn_norm_2, l0_ffn_w_gate_2, l0_ffn_w_up_2, l0_ffn_w_down_2,
    l1_ada_w_2, l1_ada_b_2, l1_mix_norm_2, l1_w_qkv_2, l1_q_norm_2, l1_k_norm_2, l1_w_out_2,
    l1_ffn_norm_2, l1_ffn_w_gate_2, l1_ffn_w_up_2, l1_ffn_w_down_2,
):
    x = first_block(
        x, mem, positions, attn_norm_g, mlp_norm_g, mem_norm_g, final_norm_g, mla_w_in,
        mla_q_norm_g, mla_kv_norm_g, mla_w_uq, mla_w_ukv, swa_w_in, swa_sinks, w_mem_kv, w_o,
        mlp_w_up, mlp_w_down,
    )
    return second_block(
        x, c_2, l0_ada_w_2, l0_ada_b_2, l0_mix_norm_2, l0_w_in_2, l0_conv_a_w_2, l0_conv_b_w_2,
        l0_conv_b_b_2, l0_rg_a_w_2, l0_rg_a_b_2, l0_rg_x_w_2, l0_rg_x_b_2, l0_rg_lambda_2,
        l0_w_out_2, l0_ffn_norm_2, l0_ffn_w_gate_2, l0_ffn_w_up_2, l0_ffn_w_down_2, l1_ada_w_2,
        l1_ada_b_2, l1_mix_norm_2, l1_w_qkv_2, l1_q_norm_2, l1_k_norm_2, l1_w_out_2,
        l1_ffn_norm_2, l1_ffn_w_gate_2, l1_ffn_w_up_2, l1_ffn_w_down_2,
    )


_drawn_inputs = setup_inputs


def setup_inputs(seed=0):
    import zlib

    import numpy as np

    out = dict(_drawn_inputs(seed))
    spreads = {}
    factors = {'attn_norm_g': 6.198,
     'mem_norm_g': 8.0,
     'mla_q_norm_g': 8.0,
     'mla_kv_norm_g': 8.0,
     'swa_sinks': 14.894,
     'l0_mix_norm_2': 4.887,
     'l0_conv_b_b_2': 45.053,
     'l0_rg_a_b_2': 64.0,
     'l0_rg_x_b_2': 64.0,
     'l0_ffn_norm_2': 26.592,
     'l1_mix_norm_2': 149.292,
     'l1_q_norm_2': 200.0,
     'l1_k_norm_2': 200.0,
     'l1_ffn_norm_2': 37.253}
    for name, (base, spread) in spreads.items():
        noise = np.random.default_rng([zlib.crc32(name.encode()), seed]).standard_normal(out[name].shape)
        drawn = base * np.exp(spread * noise) if base else spread * noise
        out[name] = __import__('jax').numpy.asarray(drawn.astype(out[name].dtype))
    for name, factor in factors.items():
        out[name] = (out[name] * factor).astype(out[name].dtype)
    return out
```

```python
from contextlib import ExitStack
import math

import concourse.bass as bass
from concourse import mybir

F32 = mybir.dt.float32
F32R = mybir.dt.float32r
I32 = mybir.dt.int32
ALU = mybir.AluOpType
ACT = mybir.ActivationFunctionType
AX = mybir.AxisListType

P = 128
T = 256
NT = T // P
D = 1024
KD = D // P
BANK = 512
HD = 64
EPS = 1e-6
BIG = 1e30

MLA_HEADS, QR, KVR, ROPE = 12, 384, 256, 32
QK = HD + ROPE
HALF = ROPE // 2
SWA_HEADS, SWA_GROUP = 12, 3
MEM_HEADS = 4
CROSS = MEM_HEADS * HD
FF = 4 * D
FF2 = 2816
GB = 256
SLOT = KD * BANK

STREAM = [
    ("mem", 2, 2, 2), ("w_in", 2, 2, 2), ("w_uq", 1, 3, 6), ("w_ukv", 1, 3, 6), ("w_o0", 2, 2, 2),
    ("up0", 8, 8, 2), ("down0", 8, 2, 2), ("swa", 4, 4, 2), ("w_o1", 2, 2, 2),
    ("up1", 8, 8, 2), ("down1", 8, 2, 2), ("lru_in", 5, 5, 2), ("lru_out", 2, 2, 2),
    ("gate_up0", 11, 11, 2), ("ffn_down0", 8, 4, 2), ("qkv", 6, 6, 2), ("sb_out", 2, 2, 2),
    ("gate_up1", 11, 11, 2), ("ffn_down1", 8, 4, 2),
]
FIRST_SLOT, FIRST_TURN, FIRST_PART = {}, {}, {}
_s = _t = _p = 0
for _name, _slots, _turns, _parts in STREAM:
    FIRST_SLOT[_name], FIRST_TURN[_name], FIRST_PART[_name] = _s, _t, _p
    _s, _t, _p = _s + _slots, _t + _turns, _p + _slots * _parts
NSLOTS = _s
SIX_PARTS = {FIRST_SLOT["w_uq"], FIRST_SLOT["w_ukv"]}


SHAPES = {"w_uq": (3, MLA_HEADS * QK), "w_ukv": (2, MLA_HEADS * 2 * HD), "swa": (KD, 384),
          "ffn_down0": (11, 256), "ffn_down1": (11, 256)}
SHAPE = [SHAPES.get(name, (KD, BANK)) for name, slots, _, _ in STREAM for _ in range(slots)]
SHAPE[FIRST_SLOT["w_in"] + 1] = (KD, QR + KVR + ROPE + CROSS - BANK)


def parts_through(n):
    return sum(6 if s in SIX_PARTS else 2 for s in range(n + 1))


COL_A = {"attn": 0, "mlp": 16, "mem": 32, "final": 40, "qn": 48, "kvn": 51, "mix0": 53, "ffn0": 61,
         "mix1": 69, "ffn1": 77, "lam": 85, "convb_b": 89, "rga_b": 93, "rgx_b": 97, "conv_a": 101, "c": 113}
ROWS_A = 121
COL_B = {"conv_b": 0, "ada_b0": 16, "ada_b1": 64, "gq": 112, "gk": 113}
ROWS_B = 114

NORMS = [("mem", KD), ("attn0", KD), ("qn", 3), ("kvn", 2), ("mlp0", KD), ("attn1", KD), ("mlp1", KD),
         ("final", KD), ("mix0", KD), ("ffn0", KD), ("mix1", KD), ("ffn1", KD)]
NORM_AT = {name: k for k, (name, _) in enumerate(NORMS)}


def squares(c):
    return 4 if c == KD else 1


def pairs(c):
    return [list(range(a, min(a + 2, c))) for a in range(0, c, 2)]


NORM_SQ = [sum(squares(c) for _, c in NORMS[:k]) for k in range(len(NORMS) + 1)]
SPLIT_NORMS = [c if name != "final" else 0 for name, c in NORMS]
NORM_PAIRS = [sum(len(pairs(c)) for c in SPLIT_NORMS[:k]) for k in range(len(NORMS) + 1)]

HIDDEN_BEFORE = {"0": 0, "1": 16, "ffn0": 32, "ffn1": 43}

HEADS = [("mla", 0, h) for h in range(MLA_HEADS)] + [("cross", 0, h) for h in range(MEM_HEADS)] \
    + [("swa", 1, h) for h in range(SWA_HEADS)] + [("cross", 1, h) for h in range(MEM_HEADS)]
SB_HEADS = 16


def build(nc, a, out):
    ctx = ExitStack()
    with ctx:
        def sb(name, shape, dt=F32):
            return ctx.enter_context(nc.sbuf_tensor(name, shape, dt))

        def sem(name):
            return ctx.enter_context(nc.semaphore(name))

        raw = sb("raw", [P, 2, SLOT])
        w_hi = sb("w_hi", [P, 2, SLOT], F32R)
        w_lo = sb("w_lo", [P, 2, SLOT], F32R)
        ada_raw = sb("ada_raw", [P, 2, 2, BANK])
        xT = sb("xT", [P, KD, T])
        h_hi = sb("h_hi", [P, KD, T], F32R)
        h_lo = sb("h_lo", [P, KD, T], F32R)
        h_full = nc.alloc_sbuf_tensor_at("h_full", [P, KD, T], F32, offset=nc.sbuf_base - 4 * KD * T)
        mem_k1 = sb("mem_k1", [P, 2, T])
        mem_v1 = sb("mem_v1", [P, 2, T])
        ident = sb("ident", [P, P])
        ones = sb("ones", [P, P])
        col_a = sb("col_a", [P, ROWS_A])
        col_b = sb("col_b", [P, ROWS_B])
        mod = sb("mod", [P, 2, 48])
        ada_cols = sb("ada_cols", [P, 96])
        modg = sb("modg", [P, 2, 2, KD])
        scratch = sb("scratch", [P, 4, T])
        negmax = sb("negmax", [P, 8, NT, 4])
        sums = sb("sums", [P, 8, NT, 4])
        rsum = sb("rsum", [P, NT, 4])
        sinkexp = sb("sinkexp", [P, NT, 4])
        sink = sb("sink", [P, SWA_HEADS])
        negsink = sb("negsink", [P, SWA_HEADS])
        posq_i = sb("posq_i", [P, NT], I32)
        posq = sb("posq", [P, NT])
        posk_i = sb("posk_i", [P, T], I32)
        silu_c = sb("silu_c", [P, KD])
        lam4 = sb("lam4", [P, 6, 4])
        gqk = sb("gqk", [P, 1])
        sb_ms = sb("sb_ms", [P, 5, NT, 8])
        arena = sb("arena", [P, 16384])
        arena_at = nc.sbuf_base - 16384 * 4

        def at(name, first, shape, dt=F32):
            return nc.alloc_sbuf_tensor_at(name, shape, dt, offset=arena_at + 4 * first)

        rows_mem = at("rows_mem", 3648, [P, NT, D])
        rows_x = at("rows_x", 5952, [P, NT, D])
        memT = at("memT", 8256, [P, KD, T])
        sq = at("sq", 10304, [P, KD, T])
        rows_a = at("rows_a", 12352, [P, P])
        rows_b = at("rows_b", 12480, [P, P])
        mem_k0 = at("mem_k0", 0, [P, 2, T])
        mem_v0 = at("mem_v0", 512, [P, 2, T])
        qx0 = at("qx0", 1024, [P, 2, T])
        krow = at("krow", 1536, [P, NT, ROPE])
        krot = at("krot", 1600, [P, NT, ROPE])
        cosT = at("cosT", 1664, [P, NT, HALF])
        sinT = at("sinT", 1696, [P, NT, HALF])
        causal = at("causal", 1728, [P, 3 * P])
        probs0 = at("probs0", 2112, [P, 2, 384])
        probsT0 = at("probsT0", 2880, [P, 2, 384])
        q_rows = at("q_rows", 3648, [P, NT, MLA_HEADS, QK])
        k_rows = at("k_rows", 5952, [P, NT, MLA_HEADS, QK])
        v_rows = at("v_rows", 8256, [P, NT, MLA_HEADS, HD])
        mla_qT = at("mla_qT", 9792, [P, MLA_HEADS, T])
        mla_kT = at("mla_kT", 12864, [P, MLA_HEADS, T])
        sq_c = at("sq_c", 9792, [P, 3, T])
        cq_hi = at("cq_hi", 10560, [P, 3, T], F32R)
        cq_lo = at("cq_lo", 11328, [P, 3, T], F32R)
        ckv_hi = at("ckv_hi", 12096, [P, 2, T], F32R)
        ckv_lo = at("ckv_lo", 12608, [P, 2, T], F32R)
        cqT = at("cqT", 13120, [P, 3, T])
        ckvT = at("ckvT", 13888, [P, 2, T])
        rope_tmp = at("rope_tmp", 9792, [P, 4, NT, MLA_HEADS, HALF])
        inv_freq = at("inv_freq", 15936, [P, HALF])
        angle = at("angle", 15952, [P, 5, NT * HALF])
        o_rows0 = at("o_rows0", 3648, [P, NT, D])
        cross_p0 = at("cross_p0", 5952, [P, 2, BANK])
        cross_pT0 = at("cross_pT0", 6976, [P, 2, BANK])
        a_hi = at("a_hi", 0, [P, FF // P, T], F32R)
        a_lo = at("a_lo", 8192, [P, FF // P, T], F32R)
        a_full = at("a_full", 8192, [P, FF // P, T])
        swa_qT = at("swa_qT", 0, [P, 6, T])
        swa_kT = at("swa_kT", 1536, [P, 2, T])
        swa_v = at("swa_v", 2048, [P, NT, 4 * HD])
        qx1 = at("qx1", 2560, [P, 2, T])
        probs1 = at("probs1", 3072, [P, 2, 384])
        probsT1 = at("probsT1", 3840, [P, 2, 384])
        dist = at("dist", 4608, [P, 3 * P])
        alibi = at("alibi", 4992, [P, 2, 384])
        swa_kT_swapped = at("swa_kT_swapped", 12352, [P, 2, T])
        o_rows1 = at("o_rows1", 5760, [P, NT, D])
        cross_p1 = at("cross_p1", 8192, [P, 2, BANK])
        cross_pT1 = at("cross_pT1", 9216, [P, 2, BANK])
        gate_b = at("gate_b", 0, [P, 4, T])
        conv_in = at("conv_in", 1024, [P, 4, T + 4])
        gate_c = at("gate_c", 2064, [P, 4, T])
        gelu_r = at("gelu_r", 3088, [P, 4, T])
        rx = at("rx", 4112, [P, 4, T + 4])
        xr = at("xr", 5152, [P, 4, T])
        rg_r = at("rg_r", 6176, [P, 4, T])
        rg_i = at("rg_i", 7200, [P, 4, T])
        lru_a = at("lru_a", 8224, [P, 4, T])
        lru_b = at("lru_b", 9248, [P, 4, T])
        lru_h = at("lru_h", 12288, [P, 4, T])
        y_mix = at("y_mix", 13312, [P, 4, T])
        rg_w = at("rg_w", 14336, [P, 2, 4, P])
        sb_rows = at("sb_rows", 0, [P, 3, NT, D])
        sb_o = at("sb_o", 0, [P, NT, D])
        sb_qT = at("sb_qT", 6144, [P, KD, T])
        sb_kT = at("sb_kT", 8192, [P, KD, T])
        sb_l = at("sb_l", 10240, [P, 2, 384])
        sb_sp = at("sb_sp", 11008, [P, 2, 384])
        sb_u = at("sb_u", 11776, [P, 2, 384])
        sb_sq = at("sb_sq", 12544, [P, NT, BANK])
        suffix = at("suffix", 13568, [P, P])
        strict = at("strict", 13696, [P, P])
        o_final = at("o_final", 0, [P, NT, D])

        ps = ctx.enter_context(nc.psum_tensor("ps", [P, 8, BANK], F32))
        NORM_BANK, ADA_BANK = 6, 7

        vec_loaded, mem_loaded, x_loaded, pos_loaded = sem("vec_loaded"), sem("mem_loaded"), sem("x_loaded"), sem("pos_loaded")
        rg_loaded = sem("rg_loaded")
        raw_loaded = [sem("raw_loaded0"), sem("raw_loaded1")]
        split_hi, split_lo = sem("split_hi"), sem("split_lo")
        parts_done = sem("parts_done")
        acc_out = [sem("acc_out0"), sem("acc_out1")]
        ada_loaded = [sem("ada_loaded0"), sem("ada_loaded1")]
        ada_step, ada_reduced = sem("ada_step"), sem("ada_reduced")
        consts, dve_step, act_step, pool_step = sem("consts"), sem("dve_step"), sem("act_step"), sem("pool_step")
        turned, unturned = sem("turned"), sem("unturned")
        vec_cols, resid_ready = sem("vec_cols"), sem("resid_ready")
        norm_sq, norm_sum, norm_total = sem("norm_sq"), sem("norm_sum"), sem("norm_total")
        norm_var, norm_y, norm_h, norm_hi, norm_lo = (sem("norm_var"), sem("norm_y"), sem("norm_h"),
                                                      sem("norm_hi"), sem("norm_lo"))
        lam_log, decay_rates, gqk_ready, dist_ready = sem("lam_log"), sem("decay_rates"), sem("gqk_ready"), sem("dist_ready")
        angles, sines, tables, rope_done = sem("angles"), sem("sines"), sem("tables"), sem("rope_done")
        scores, biased, exped, probs_turned, probs_copied, heads_done, o_copied = (
            sem("scores"), sem("biased"), sem("exped"), sem("probs_turned"), sem("probs_copied"),
            sem("heads_done"), sem("o_copied"))
        alibi_ready, sink_arg, sink_exp = sem("alibi_ready"), sem("sink_arg"), sem("sink_exp")
        mix_turned, mix_full, mix_hi, mix_lo = sem("mix_turned"), sem("mix_full"), sem("mix_hi"), sem("mix_lo")
        hid_sq, hid_hi, hid_lo = sem("hid_sq"), sem("hid_hi"), sem("hid_lo")
        xr_ready, gates, gates_out, decay, tanh_done, gain_sq, gain = (
            sem("xr_ready"), sem("gates"), sem("gates_out"), sem("decay"), sem("tanh_done"), sem("gain_sq"), sem("gain"))
        qk_sq, qk_var, qk_y, qk_scaled, qk_turned, qk_out = (
            sem("qk_sq"), sem("qk_var"), sem("qk_y"), sem("qk_scaled"), sem("qk_turned"), sem("qk_out"))
        z_ready, z_soft, sp_ready, sp_masked, u_ready, sums_ready, logw_ready, w_exped, w_masked = (
            sem("z_ready"), sem("z_soft"), sem("sp_ready"), sem("sp_masked"), sem("u_ready"), sem("sums_ready"),
            sem("logw_ready"), sem("w_exped"), sem("w_masked"))
        q_out, k_out, qk_banks = sem("q_out"), sem("k_out"), sem("qk_banks")
        out_copied, stored = [sem("out_copied0"), sem("out_copied1")], sem("stored")

        block = ctx.enter_context(nc.Block())

        def rows(v, i=None):
            v = v if i is None else v[i]
            return v.rearrange("(c p) -> c p", p=P)

        def k_major(w):
            return w.rearrange("(c p) n -> p c n", p=P)

        def ring(buf, slot, kc, cols):
            return buf[:, slot, 0:kc * cols].rearrange("p (c n) -> p c n", c=kc)

        class Slot:

            def __init__(self, phase, j, i=None, step=0):
                n = FIRST_SLOT[phase] + j
                grow = (lambda per, first: first) if i is None else (lambda per, first: i * (step * per) + first)
                self.slot = n % 2
                self.first = n < 2
                self.kc, self.cols = SHAPE[n]
                self.words = self.kc * self.cols
                self.loaded = grow(16, 32 * (n // 2 + 1))
                self.split = grow(2, 2 * n)
                self.free = grow(2, 2 * n - 2)
                self.used = grow(2, parts_through(n - 2))
                self.before = grow(2, parts_through(n - 1))

        def turn(phase, j, i=None, step=0):
            return FIRST_TURN[phase] + j if i is None else i * step + (FIRST_TURN[phase] + j)

        @block.sync
        def _(sp):
            def load(s, src):
                if not s.first:
                    sp.wait_ge(split_lo, s.free)
                kc = s.kc
                to, cut = ring(raw, s.slot, kc, s.cols), kc // 2
                sp.dma_start(to[:, 0:cut, :], src[:, 0:cut, :]).then_inc(raw_loaded[s.slot], 16)
                sp.dma_start(to[:, cut:kc, :], src[:, cut:kc, :]).then_inc(raw_loaded[s.slot], 16)

            sp.dma_start(rows_mem[:, :, :], a["mem"].rearrange("b (t p) d -> p (b t) d", p=P)).then_inc(mem_loaded, 16)
            for l in range(2):
                load(Slot("mem", l), k_major(a["w_mem_kv"][l]))
            sp.dma_start(rows_x[:, :, :], a["x"].rearrange("b (t p) d -> p (b t) d", p=P)).then_inc(x_loaded, 16)
            load(Slot("w_in", 0), k_major(a["mla_w_in"][0])[:, :, 0:512])
            load(Slot("w_in", 1), k_major(a["mla_w_in"][0])[:, :, 512:928])
            load(Slot("w_uq", 0), k_major(a["mla_w_uq"][0]))
            load(Slot("w_ukv", 0), k_major(a["mla_w_ukv"][0]))

            def load_columns(phase, w, slots):
                for j in range(slots):
                    load(Slot(phase, j), k_major(w)[:, :, j * BANK:(j + 1) * BANK])

            def load_mlp(l):
                w_up, w_down = k_major(a["mlp_w_up"][l]), k_major(a["mlp_w_down"][l])
                with sp.Fori(0, 4) as i:
                    for j in range(2):
                        load(Slot(f"up{l}", j, i, 2), w_up[:, :, bass.ds(i * (2 * BANK) + j * BANK, BANK)])
                with sp.Fori(0, 2) as i:
                    for j in range(4):
                        load(Slot(f"down{l}", j, i, 4), w_down[:, j * KD:(j + 1) * KD, bass.ds(i * BANK, BANK)])

            def load_ffn(l):
                gate, up, down = (k_major(a[f"l{l}_ffn_w_{x}_2"]) for x in ("gate", "up", "down"))

                def load_pair(s, first):
                    both = ring(raw, s.slot, KD, 2 * GB)
                    sp.wait_ge(split_lo, s.free)
                    sp.dma_start(both[:, :, 0:GB], gate[:, :, bass.ds(first, GB)]).then_inc(raw_loaded[s.slot], 16)
                    sp.dma_start(both[:, :, GB:2 * GB], up[:, :, bass.ds(first, GB)]).then_inc(raw_loaded[s.slot], 16)

                with sp.Fori(0, 5) as i:
                    for j in range(2):
                        load_pair(Slot(f"gate_up{l}", j, i, 2), i * (2 * GB) + j * GB)
                load_pair(Slot(f"gate_up{l}", 10), 10 * GB)
                with sp.Fori(0, 4) as i:
                    for j in range(2):
                        load(Slot(f"ffn_down{l}", j, i, 2), down[:, j * 11:(j + 1) * 11, bass.ds(i * 256, 256)])

            load_columns("w_o0", a["w_o"][0], 2)
            load_mlp(0)
            for j in range(4):
                load(Slot("swa", j), k_major(a["swa_w_in"][0])[:, :, j * 384:(j + 1) * 384])
            load_columns("w_o1", a["w_o"][1], 2)
            load_mlp(1)
            load_columns("lru_in", a["l0_w_in_2"], 5)
            load_columns("lru_out", a["l0_w_out_2"], 2)
            load_ffn(0)
            load_columns("qkv", a["l1_w_qkv_2"], 6)
            load_columns("sb_out", a["l1_w_out_2"], 2)
            load_ffn(1)
            y = out.rearrange("b (t p) d -> p (b t) d", p=P)
            for t in range(NT):
                sp.wait_ge(out_copied[t], 2)
                sp.dma_start(y[:, t, :], o_final[:, t, :]).then_inc(stored, 16)
            sp.wait_ge(stored, 16 * NT)

        @block.gpsimd
        def _(pool):
            def step(ins, n):
                ins.then_inc(pool_step, 1)
                pool.wait_ge(pool_step, n)

            def triangle(to, fill, base, q, k, n):
                step(nc.gpsimd.affine_select(out=to, in_=to, compare_op=ALU.is_gt, fill=fill, base=base,
                                             pattern=[[k, P]], channel_multiplier=q), n)

            step(nc.gpsimd.memset(ident[:, :], 0.0), 1)
            nc.gpsimd.affine_select(out=ident[:, :], in_=ident[:, :], compare_op=ALU.not_equal, fill=1.0, base=0,
                                    pattern=[[-1, P]], channel_multiplier=1).then_inc(consts, 1)
            nc.gpsimd.memset(ones[:, :], 1.0).then_inc(consts, 1)
            step(nc.gpsimd.memset(causal[:, :], 0.0), 2)
            triangle(causal[:, 0:P], BIG, 1, 1, -1, 3)
            triangle(causal[:, 2 * P:3 * P], BIG, 1, 1, -1, 4)
            for f in range(HALF):
                last = nc.gpsimd.memset(inv_freq[:, f:f + 1], float(10000.0 ** (-(f * 2.0) / ROPE)))
            last.then_inc(consts, 1)

            ada = [k_major(a[f"l{l}_ada_w_2"]) for l in range(2)]

            def ada_load(l, slot, group, quarter, m):
                if not (isinstance(m, int) and m < 2):
                    pool.wait_ge(ada_step, m * 2 - 2)
                pool.dma_start(ada_raw[:, slot, :, :], ada[l][:, 2 * quarter:2 * quarter + 2, group])\
                    .then_inc(ada_loaded[slot], 16)

            def ada_loads(first, last):
                cut = 12 * (first // 12)
                with pool.Fori(first, last) as g:
                    for u in range(4):
                        group = g if u < 2 else g + 1
                        ada_load(first // 12, u % 2, bass.ds((group - cut) * BANK, BANK), (u + 2) % 4, g * 4 + (u + 2))

            def ada_pair(group, half):
                for u in range(2):
                    at_group = slice(group % 12 * BANK, (group % 12 + 1) * BANK)
                    ada_load(group // 12, u, at_group, 2 * half + u, 4 * group + 2 * half + u)

            ada_pair(0, 0)
            ada_loads(0, 8)

            pool.wait_ge(dist_ready, 2)
            triangle(dist[:, 0:P], BIG, 1, 1, -1, 5)
            triangle(dist[:, P:2 * P], BIG, 0, -1, 1, 6)
            triangle(dist[:, 2 * P:3 * P], BIG, 1, 1, -1, 7)
            for h in range(SWA_HEADS):
                if h >= 2:
                    pool.wait_ge(biased, MLA_HEADS + MEM_HEADS + h - 1)
                slope = 2.0 ** (-8.0 * (h + 1.0) / SWA_HEADS)
                nc.gpsimd.tensor_scalar(alibi[:, h % 2, :], dist[:, :], slope, None, ALU.mult).then_inc(alibi_ready, 1)

            ada_loads(8, 11)
            ada_pair(11, 1)
            ada_pair(12, 0)
            ada_loads(12, 16)

            pool.wait_ge(parts_done, parts_through(FIRST_SLOT["lru_in"] - 1))
            step(nc.gpsimd.memset(rg_w[:, :, :, :], 0.0), 8)
            for g, w in enumerate((a["l0_rg_a_w_2"], a["l0_rg_x_w_2"])):
                for half in range(2):
                    pool.dma_start(rg_w[half * HD:(half + 1) * HD, g, :, half * HD:(half + 1) * HD],
                                   w.rearrange("(b two) i j -> two i b j", two=2)[half]).then_inc(rg_loaded, 16)

            ada_loads(16, 23)
            ada_pair(23, 1)

            pool.wait_ge(parts_done, parts_through(FIRST_SLOT["qkv"] - 1))
            nc.gpsimd.memset(suffix[:, :], 1.0).then_inc(pool_step, 1)
            nc.gpsimd.memset(strict[:, :], 1.0).then_inc(pool_step, 1)
            pool.wait_ge(pool_step, 10)
            triangle(suffix[:, :], 0.0, 0, 1, -1, 11)
            triangle(strict[:, :], 0.0, 0, -1, 1, 12)
            def on_diagonal(buf, h):
                return buf[:, h % 2, :].rearrange("p (k q) -> p k q", k=3)[:, 0:3:2, :]

            mask = strict[:, :].unsqueeze(1).to_broadcast([P, 2, P])
            for h in range(SB_HEADS + 1):
                if h < SB_HEADS:
                    pool.wait_ge(sp_ready, h + 1)
                    nc.gpsimd.tensor_tensor(on_diagonal(sb_sp, h), on_diagonal(sb_sp, h), mask, ALU.mult)\
                        .then_inc(sp_masked, 1)
                if h >= 1:
                    pool.wait_ge(w_exped, h)
                    nc.gpsimd.tensor_tensor(on_diagonal(sb_u, h - 1), on_diagonal(sb_u, h - 1), mask, ALU.mult)\
                        .then_inc(w_masked, 1)

        def wait_count(s, b):
            return s.before + (b + 1)

        def sb_rows_out(act, g):
            act.wait_ge(heads_done, len(HEADS) + 4 * (g + 1))
            nc.scalar.activation(sb_o[:, :, 4 * g * HD:(4 * g + 4) * HD], ps[:, 6 + g % 2, :].rearrange("p (t d) -> p t d", t=NT),
                                 ACT.Copy).then_inc(o_copied, 1)

        def wait_pair(eng, name, q):
            if name == "mem":
                eng.wait_ge(unturned, 3 + q)
            elif name in ("attn0", "mix0"):
                eng.wait_ge(resid_ready, (4 if name == "mix0" else 0) + q + 1)
            elif name == "mix1":
                for b in range(2):
                    eng.wait_ge(acc_out[b], turn("ffn_down0", q) + 1)
            elif name in ("qn", "kvn"):
                wait_source(eng, name)
            else:
                phase = {"mlp0": "w_o0", "attn1": "down0", "mlp1": "w_o1", "final": "down1", "ffn0": "lru_out",
                         "ffn1": "sb_out"}[name]
                eng.wait_ge(acc_out[q % 2], turn(phase, q // 2) + 1)

        def wait_source(eng, name):
            if name == "mem":
                eng.wait_ge(unturned, 6)
            elif name == "attn0":
                eng.wait_ge(resid_ready, 4)
            elif name == "mix0":
                eng.wait_ge(resid_ready, 8)
            else:
                last = {"qn": turn("w_in", 0), "kvn": turn("w_in", 1), "mlp0": turn("w_o0", 1), "attn1": turn("down0", 1),
                        "mlp1": turn("w_o1", 1), "final": turn("down1", 1), "ffn0": turn("lru_out", 1),
                        "mix1": turn("ffn_down0", 3), "ffn1": turn("sb_out", 1), "out": turn("ffn_down1", 3)}[name]
                eng.wait_ge(acc_out[0], last + 1)
                eng.wait_ge(acc_out[1], last + 1)

        def norm_io(name):
            if name == "mem":
                return memT, sq, h_hi, h_lo
            if name == "qn":
                return cqT, sq_c, cq_hi, cq_lo
            if name == "kvn":
                return ckvT, sq_c, ckv_hi, ckv_lo
            return xT, (h_full if name in ("attn1", "final", "mix1") else sq), h_hi, h_lo

        @block.scalar
        def _(act):
            steps = [0]

            def link(ins):
                steps[0] += 1
                ins.then_inc(act_step, 1)
                act.wait_ge(act_step, steps[0])

            def split(s, halves=(0, 1)):
                act.wait_ge(raw_loaded[s.slot], s.loaded)
                if not s.first:
                    act.wait_ge(parts_done, s.used)
                for half in halves:
                    cut = slice(half * s.words // 2, (half + 1) * s.words // 2)
                    nc.scalar.activation(w_hi[:, s.slot, cut], raw[:, s.slot, cut], ACT.Copy).then_inc(split_hi, 1)

            def norm(name, used=None):
                k = NORM_AT[name]
                c = NORMS[k][1]
                src, squared, hi, _ = norm_io(name)
                if NORM_PAIRS[k]:
                    act.wait_ge(norm_lo, NORM_PAIRS[k])
                per = c // squares(c)
                for q in range(squares(c)):
                    wait_pair(act, name, q)
                    cut = slice(q * per, (q + 1) * per)
                    nc.scalar.activation(squared[:, cut, :], src[:, cut, :], ACT.Square).then_inc(norm_sq, 1)
                act.wait_ge(norm_var, k + 1)
                link(nc.scalar.activation(scratch[:, 2, :], scratch[:, 1, :], ACT.Ln))
                nc.scalar.activation(scratch[:, 2, :], scratch[:, 2, :], ACT.Exp, scale=-0.5).then_inc(norm_y, 1)
                if name == "final":
                    return
                if used is not None:
                    act.wait_ge(parts_done, used)
                for q, chunks in enumerate(pairs(c)):
                    cut = slice(chunks[0], chunks[-1] + 1)
                    act.wait_ge(norm_h, NORM_PAIRS[k] + q + 1)
                    nc.scalar.activation(hi[:, cut, :], squared[:, cut, :], ACT.Copy).then_inc(norm_hi, 1)

            def acc(b, cols=BANK):
                return ps[:, b, 0:cols]

            def wait_part(s, b):
                act.wait_ge(parts_done, wait_count(s, b))

            def load_rows(dst, src, first):
                n = src.shape[0]
                act.dma_start(dst[first:first + n, 0:src.shape[1]], src).then_inc(vec_loaded, 16)

            load_rows(rows_a, rows(a["mem_norm_g"]), COL_A["mem"])
            for key, name in (("attn", "attn_norm_g"), ("mlp", "mlp_norm_g")):
                load_rows(rows_a, a[name].rearrange("l (c p) -> (l c) p", p=P), COL_A[key])
            for key, name in (("final", "final_norm_g"), ("mix0", "l0_mix_norm_2"), ("ffn0", "l0_ffn_norm_2"),
                              ("mix1", "l1_mix_norm_2"), ("ffn1", "l1_ffn_norm_2"), ("lam", "l0_rg_lambda_2"),
                              ("convb_b", "l0_conv_b_b_2")):
                load_rows(rows_a, rows(a[name]), COL_A[key])
            for key, name in (("qn", "mla_q_norm_g"), ("kvn", "mla_kv_norm_g"), ("c", "c_2")):
                load_rows(rows_a, rows(a[name], 0), COL_A[key])
            for key, name in (("rga_b", "l0_rg_a_b_2"), ("rgx_b", "l0_rg_x_b_2")):
                load_rows(rows_a, a[name].rearrange("(c two) j -> c (two j)", two=2), COL_A[key])
            load_rows(rows_a, a["l0_conv_a_w_2"].rearrange("k (c p) -> (k c) p", p=P), COL_A["conv_a"])
            load_rows(rows_b, a["l0_conv_b_w_2"].rearrange("k (c p) -> (k c) p", p=P), COL_B["conv_b"])
            for l in range(2):
                load_rows(rows_b, rows(a[f"l{l}_ada_b_2"]), COL_B[f"ada_b{l}"])
            for key, name in (("gq", "l1_q_norm_2"), ("gk", "l1_k_norm_2")):
                for half in range(2):
                    act.dma_start(rows_b[COL_B[key]:COL_B[key] + 1, half * HD:(half + 1) * HD],
                                  a[name].rearrange("(o d) -> o d", o=1)).then_inc(vec_loaded, 16)
            act.dma_start(posk_i[:, :], a["positions"].rearrange("b t -> (b t)").partition_broadcast(P)).then_inc(pos_loaded, 16)
            for t in range(NT):
                act.dma_start(posq_i[:, t:t + 1], a["positions"][0, t * P:(t + 1) * P].rearrange("(p o) -> p o", o=1)).then_inc(pos_loaded, 16)
            act.dma_start(sink[:, :], a["swa_sinks"].rearrange("l h -> (l h)").partition_broadcast(P)).then_inc(pos_loaded, 16)

            nc.scalar.preload_act_table_set("natural_log_exp_and_others")
            split(Slot("mem", 0))
            norm("mem")
            for b in range(4):
                act.wait_ge(turned, 7 + b)
                nc.scalar.activation(xT[:, 2 * b:2 * b + 2, :], ps[:, 2 + b, :].rearrange("p (c t) -> p c t", c=2),
                                     ACT.Copy).then_inc(resid_ready, 1)
            split(Slot("mem", 1))
            for l, keys in enumerate((mem_k0, mem_k1)):
                wait_part(Slot("mem", l), 0)
                nc.scalar.activation(keys[:, :, :], acc(0).rearrange("p (c t) -> p c t", c=2), ACT.Copy).then_inc(acc_out[0], 1)
                if l == 0:
                    split(Slot("mem", 2))
            act.wait_ge(vec_cols, 2)
            link(nc.scalar.activation(lam4[:, 1, :], lam4[:, 0, :], ACT.Exp, scale=-1.0))
            nc.scalar.activation(lam4[:, 1, :], lam4[:, 1, :], ACT.Ln, bias=1.0).then_inc(lam_log, 1)
            norm("attn0", used=parts_through(1))
            split(Slot("mem", 3))
            act.wait_ge(angles, 1)
            for q, to in ((1, sinT), (2, cosT)):
                nc.scalar.activation(to[:, :, :], angle[:, q, :].rearrange("p (t f) -> p t f", t=NT), ACT.Sin).then_inc(sines, 1)
            nc.scalar.activation(silu_c[:, :], col_a[:, COL_A["c"]:COL_A["c"] + KD], ACT.Silu).then_inc(sines, 1)
            nc.scalar.preload_act_table_set("natural_log_exp_and_others")

            wait_part(Slot("w_in", 0), 0)
            nc.scalar.activation(cqT[:, 0:2, :], acc(0).rearrange("p (c t) -> p c t", c=2), ACT.Copy).then_inc(acc_out[0], 1)
            norm("qn")
            split(Slot("w_in", 2))
            wait_part(Slot("w_in", 1), 0)
            nc.scalar.activation(ckvT[:, 1, :], acc(0, T), ACT.Copy)
            nc.scalar.activation(qx0[:, 0, :], ps[:, 0, T:2 * T], ACT.Copy, scale=-HD ** -0.5).then_inc(acc_out[0], 1)
            norm("kvn")
            split(Slot("w_in", 3))
            for g in range(3):
                act.wait_ge(parts_done, Slot("w_uq", 0).before + 2 * g + 1)
                nc.scalar.activation(q_rows[:, 0, 4 * g:4 * g + 4, :], acc(0, 4 * QK).rearrange("p (h d) -> p h d", h=4),
                                     ACT.Copy, scale=-QK ** -0.5).then_inc(acc_out[0], 1)
            for g in range(3):
                act.wait_ge(parts_done, Slot("w_ukv", 0).before + 2 * g + 1)
                kv = acc(0).rearrange("p (h d) -> p h d", h=4)
                nc.scalar.activation(k_rows[:, 0, 4 * g:4 * g + 4, 0:HD], kv[:, :, 0:HD], ACT.Copy)
                nc.scalar.activation(v_rows[:, 0, 4 * g:4 * g + 4, :], kv[:, :, HD:2 * HD], ACT.Copy).then_inc(acc_out[0], 1)
            for j in range(6):
                act.wait_ge(qk_banks, 2 * j + 1)
                nc.scalar.activation(mla_qT[0:QK, 2 * j:2 * j + 2, :], ps[0:QK, 2 + j % 2, :].rearrange("p (h t) -> p h t", h=2),
                                     ACT.Copy).then_inc(q_out, 1)
            split(Slot("w_o0", 0))

            def exp_head(hc):
                kind, l, h = HEADS[hc]
                g, j = hc // 4, hc % 4
                b = hc % 2
                act.wait_ge(biased, hc + 1)
                if kind == "cross":
                    p = (cross_p0 if l == 0 else cross_p1)[:, b, :]
                    src = ps[:, 2 + b, :]
                    cuts = (slice(0, T), slice(T, 2 * T))
                    if hc >= 2:
                        act.wait_ge(probs_turned, hc - 1)
                else:
                    p = (probs0 if kind == "mla" else probs1)[:, b, :]
                    src = p
                    cuts = (slice(0, P), slice(P, 3 * P))
                for t, cut in enumerate(cuts):
                    ins = nc.scalar.activation(p[:, cut], src[:, cut], ACT.Exp, scale=-1.0, bias=negmax[:, g, t, j:j + 1],
                                               accum_out=sums[:, g, t, j:j + 1])
                ins.then_inc(exped, 1)

            def copy_probs(hc):
                kind, l, _ = HEADS[hc]
                if kind == "cross":
                    n, to = 4, (cross_pT0 if l == 0 else cross_pT1)
                else:
                    n, to = 3, (probsT0 if kind == "mla" else probsT1)
                act.wait_ge(probs_turned, hc + 1)
                if hc >= 2:
                    act.wait_ge(heads_done, hc - 1)
                nc.scalar.activation(to[:, hc % 2, 0:n * P], ps[:, 4 + hc % 2, 0:n * P], ACT.Copy).then_inc(probs_copied, 1)

            def sink_sums(g):
                act.wait_ge(sink_arg, g - 3)
                nc.scalar.activation(sinkexp[:, :, :], sinkexp[:, :, :], ACT.Exp).then_inc(sink_exp, 1)

            def heads(first, last):
                for hc in range(first, last + 1):
                    if hc < last:
                        exp_head(hc)
                    if hc > first:
                        copy_probs(hc - 1)
                    if hc % 4 == 3 and HEADS[hc][0] == "swa":
                        sink_sums(hc // 4)

            def mix_high(n):
                for q in range(4):
                    act.wait_ge(mix_turned, 4 * n + q + 1)
                    nc.scalar.activation(h_hi[:, 2 * q:2 * q + 2, :], ps[:, 2 + q, :].rearrange("p (c t) -> p c t", c=2),
                                         ACT.Copy).then_inc(mix_hi, 1)

            heads(0, 16)
            mix_high(0)
            split(Slot("w_o0", 1))
            split(Slot("w_o0", 2))

            def mlp(l):
                norm(f"mlp{l}")
                split(Slot(f"up{l}", 1))
                for j in range(8):
                    s = Slot(f"up{l}", j)
                    for b in range(2):
                        at_pair = slice(4 * j + 2 * b, 4 * j + 2 * b + 2)
                        full = a_full[:, at_pair, :]
                        wait_part(s, b)
                        nc.scalar.activation(full, acc(b).rearrange("p (c t) -> p c t", c=2), ACT.Relu).then_inc(acc_out[b], 1)
                        act.wait_ge(acc_out[b], turn(f"up{l}", j) + 1)
                        nc.scalar.activation(full, full, ACT.Square).then_inc(hid_sq, 1)
                        act.wait_ge(hid_sq, 16 * l + 2 * j + b + 1)
                        nc.scalar.activation(a_hi[:, at_pair, :], full, ACT.Copy).then_inc(hid_hi, 1)
                    split(Slot(f"up{l}", j + 2))
                for j in range(7):
                    split(Slot(f"down{l}", j + 2))

            mlp(0)

            norm("attn1")
            split(Slot("down0", 9))
            for j in range(4):
                wait_part(Slot("swa", j), 0)
                two = acc(0).rearrange("p (c t) -> p c t", c=2)
                if j < 2:
                    nc.scalar.activation(swa_qT[:, 3 * j:3 * j + 2, :], two, ACT.Copy, scale=-HD ** -0.5).then_inc(acc_out[0], 1)
                elif j == 2:
                    nc.scalar.activation(swa_kT_swapped[0:HD, :, :], two[HD:P], ACT.Copy)
                    nc.scalar.activation(swa_kT_swapped[HD:P, :, :], two[0:HD], ACT.Copy)
                    nc.scalar.activation(swa_kT[:, :, :], two, ACT.Copy).then_inc(acc_out[0], 1)
                else:
                    nc.scalar.activation(qx1[:, :, :], two, ACT.Copy, scale=-HD ** -0.5).then_inc(acc_out[0], 1)
                if j < 3:
                    split(Slot("swa", j + 2))
            heads(16, 32)
            mix_high(1)
            split(Slot("swa", 5))
            split(Slot("swa", 6))
            mlp(1)

            norm("final")
            norm("mix0")
            split(Slot("down1", 9))
            for j in range(5):
                if j == 3:
                    nc.scalar.preload_act_table(ACT.Gelu_apprx_tanh)
                for b in range(2):
                    if j in (0, 1, 3) or (j == 4):
                        wait_part(Slot("lru_in", j), b)
                        two = acc(b).rearrange("p (c t) -> p c t", c=2)
                        cut = slice(2 * b, 2 * b + 2)
                        to = {0: gate_b, 1: gate_c, 3: gelu_r}.get(j)
                        to = to[:, cut, :] if j < 4 else rx[:, cut, 3:3 + T]
                        nc.scalar.activation(to, two, ACT.Gelu_apprx_tanh if j == 3 else ACT.Copy).then_inc(acc_out[b], 1)
                if j < 4:
                    split(Slot("lru_in", j + 2))
            for g, (to, bias) in enumerate(((rg_r, "rga_b"), (rg_i, "rgx_b"))):
                for c in range(4):
                    act.wait_ge(gates, 2 * g + c // 2 + 1)
                    nc.scalar.activation(to[:, c, :], ps[:, 2 + 2 * g + c // 2, (c % 2) * T:(c % 2 + 1) * T], ACT.Sigmoid,
                                         bias=col_a[:, COL_A[bias] + c:COL_A[bias] + c + 1]).then_inc(gates_out, 1)
            act.wait_ge(gates_out, 4)
            act.wait_ge(decay_rates, 2)
            for c in range(4):
                nc.scalar.activation(lru_a[:, c, :], rg_r[:, c, :], ACT.Exp, scale=lam4[:, 3, c:c + 1]).then_inc(decay, 1)
                nc.scalar.activation(lru_b[:, c, :], rg_r[:, c, :], ACT.Tanh, scale=lam4[:, 4, c:c + 1]).then_inc(tanh_done, 1)
            act.wait_ge(gain_sq, 1)
            nc.scalar.activation(lru_b[:, :, :], lru_b[:, :, :], ACT.Sqrt).then_inc(gain, 1)
            nc.scalar.preload_act_table_set("natural_log_exp_and_others")
            for q in range(4):
                act.wait_ge(mix_full, q + 1)
                src = y_mix[:, 2 * q:2 * q + 2, :] if q < 2 else lru_h[:, 2 * q - 4:2 * q - 2, :]
                nc.scalar.activation(h_hi[:, 2 * q:2 * q + 2, :], src, ACT.Copy).then_inc(mix_hi, 1)
            split(Slot("lru_out", 1))
            split(Slot("lru_out", 2))

            def ffn(l):
                norm(f"ffn{l}")
                split(Slot(f"gate_up{l}", 1))
                nc.scalar.preload_act_table(ACT.Silu)

                for j in range(11):
                    at_pair = slice(2 * j, 2 * j + 2)
                    wait_part(Slot(f"gate_up{l}", j), 0)
                    nc.scalar.activation(a_full[:, at_pair, :], acc(0).rearrange("p (c t) -> p c t", c=2), ACT.Silu).then_inc(acc_out[0], 1)
                    act.wait_ge(acc_out[1], turn(f"gate_up{l}", j) + 1)
                    nc.scalar.activation(a_hi[:, at_pair, :], a_full[:, at_pair, :], ACT.Copy).then_inc(hid_hi, 1)
                    split(Slot(f"gate_up{l}", j + 2))
                with act.Fori(0, 3) as i:
                    for j in range(2):
                        split(Slot(f"ffn_down{l}", j + 2, i, 2))
                if l == 0:
                    split(Slot("qkv", 0))
                nc.scalar.preload_act_table_set("natural_log_exp_and_others")

            ffn(0)
            norm("mix1")
            split(Slot("qkv", 1))

            def qk_rows(j):
                part, half = j // 2, j % 2
                for b in range(2):
                    wait_part(Slot("qkv", j), b)
                    nc.scalar.activation(sb_rows[:, part, b, half * BANK:(half + 1) * BANK], acc(b), ACT.Copy).then_inc(acc_out[b], 1)
                    if part < 2:
                        if j >= 1:
                            act.wait_ge(qk_var, j)
                        act.wait_ge(acc_out[b], turn("qkv", j) + 1)
                        nc.scalar.activation(sb_sq[:, b, :], sb_rows[:, part, b, half * BANK:(half + 1) * BANK], ACT.Square).then_inc(qk_sq, 1)
                if part < 2:
                    act.wait_ge(qk_var, j + 1)
                    link(nc.scalar.activation(sb_ms[:, 1, :, :], sb_ms[:, 0, :, :], ACT.Ln))
                    nc.scalar.activation(sb_ms[:, 1, :, :], sb_ms[:, 1, :, :], ACT.Exp, scale=-0.5).then_inc(qk_y, 1)

            def qk_copy(j):
                to = sb_qT if j < 2 else sb_kT
                for q in range(2):
                    act.wait_ge(qk_turned, 2 * j + q + 1)
                    c = 4 * (j % 2) + 2 * q
                    nc.scalar.activation(to[:, c:c + 2, :], ps[:, 2 + 2 * (j % 2) + q, :].rearrange("p (c t) -> p c t", c=2),
                                         ACT.Copy, scale=gqk[:, 0:1] if j < 2 else 1.0).then_inc(qk_out, 1)

            act.wait_ge(gqk_ready, 1)
            for j in range(6):
                qk_rows(j)
                if j < 5:
                    split(Slot("qkv", j + 2))
                if 1 <= j < 5:
                    qk_copy(j - 1)

            def soft(h):
                act.wait_ge(z_ready, h + 1)
                if h >= 2:
                    act.wait_ge(u_ready, h - 1)
                z = sb_l[:, h % 2, :]
                link(nc.scalar.activation(z, ps[:, 2 + h % 2, 0:384], ACT.Abs))
                link(nc.scalar.activation(z, z, ACT.Exp, scale=-1.0))
                nc.scalar.activation(z, z, ACT.Ln, bias=1.0).then_inc(z_soft, 1)

            for h in range(SB_HEADS + 1):
                if h < SB_HEADS:
                    soft(h)
                if h >= 1:
                    act.wait_ge(logw_ready, h)
                    nc.scalar.activation(sb_u[:, (h - 1) % 2, :], sb_u[:, (h - 1) % 2, :], ACT.Exp).then_inc(w_exped, 1)
                if h >= 5 and (h - 1) % 4 == 0:
                    sb_rows_out(act, (h - 5) // 4)
            sb_rows_out(act, 3)
            mix_high(2)
            split(Slot("sb_out", 1))
            split(Slot("sb_out", 2))
            ffn(1)
            for q in range(2):
                act.wait_ge(turned, 11 + q)
                nc.scalar.activation(o_final[:, 0, q * BANK:(q + 1) * BANK], ps[:, 2 + q, :], ACT.Copy).then_inc(out_copied[0], 1)

        @block.vector
        def _(dve):
            steps = [0]

            def link(ins):
                steps[0] += 1
                ins.then_inc(dve_step, 1)
                dve.wait_ge(dve_step, steps[0])

            def split(s):
                for half in range(2):
                    cut = slice(half * s.words // 2, (half + 1) * s.words // 2)
                    dve.wait_ge(split_hi, s.split + (half + 1))
                    nc.vector.tensor_tensor(w_lo[:, s.slot, cut], raw[:, s.slot, cut], w_hi[:, s.slot, cut].bitcast(F32),
                                            ALU.subtract).then_inc(split_lo, 1)

            gains = {"mem": (col_a, "mem", 0), "attn0": (col_a, "attn", 0), "attn1": (col_a, "attn", 8),
                     "mlp0": (col_a, "mlp", 0), "mlp1": (col_a, "mlp", 8), "final": (col_a, "final", 0),
                     "qn": (col_a, "qn", 0), "kvn": (col_a, "kvn", 0)}

            def sum_squares(name, q):
                dve.wait_ge(norm_sq, NORM_SQ[NORM_AT[name]] + q + 1)
                squared = norm_io(name)[1]
                link(nc.vector.tensor_tensor(squared[:, 0:2, :], squared[:, 0:2, :], squared[:, 2 * q:2 * q + 2, :], ALU.add))

            def norm(name, used=None, summed=False):
                k = NORM_AT[name]
                c = NORMS[k][1]
                src, squared, hi, lo = norm_io(name)
                total, var, y, r = (scratch[:, q, :] for q in range(4))
                if c == KD:
                    for q in (3,) if summed else (1, 2, 3):
                        sum_squares(name, q)
                else:
                    dve.wait_ge(norm_sq, NORM_SQ[k + 1])
                if c == 3:
                    link(nc.vector.tensor_tensor(squared[:, 0, :], squared[:, 0, :], squared[:, 2, :], ALU.add))
                nc.vector.tensor_tensor(total, squared[:, 0, :], squared[:, 1, :], ALU.add).then_inc(norm_sum, 1)
                dve.wait_ge(norm_total, k + 1)
                nc.vector.tensor_scalar(var, ps[:, NORM_BANK, 0:T], 1.0 / (c * P), EPS, ALU.mult, ALU.add).then_inc(norm_var, 1)
                dve.wait_ge(norm_y, k + 1)
                link(nc.vector.tensor_tensor(r, y, y, ALU.mult))
                link(nc.vector.scalar_tensor_tensor(r, r, -0.5, var, ALU.mult, ALU.mult))
                link(nc.vector.scalar_tensor_tensor(r, r, 1.5, y, ALU.add, ALU.mult))
                wait_source(dve, name)
                shift = None
                if name in gains:
                    cols, key, first = gains[name]
                    gain_of = lambda ch: cols[:, COL_A[key] + first + ch:COL_A[key] + first + ch + 1]
                else:
                    l, which = int(name[-1]), 0 if name.startswith("mix") else 1
                    gain_of = lambda ch: modg[:, l, which, ch:ch + 1]
                    shift = lambda ch: mod[:, l, 24 * which + ch:24 * which + ch + 1]

                def low(q):
                    cut = slice(pairs(c)[q][0], pairs(c)[q][-1] + 1)
                    dve.wait_ge(norm_hi, NORM_PAIRS[k] + q + 1)
                    nc.vector.tensor_tensor(lo[:, cut, :], squared[:, cut, :], hi[:, cut, :].bitcast(F32),
                                            ALU.subtract).then_inc(norm_lo, 1)

                for q, chunks in enumerate(pairs(c)):
                    to = src if name == "final" else squared
                    for ch in chunks:
                        ins = nc.vector.scalar_tensor_tensor(to[:, ch, :], src[:, ch, :], gain_of(ch), r, ALU.mult, ALU.mult)
                    if shift is not None:
                        link(ins)
                        for ch in chunks:
                            ins = nc.vector.tensor_scalar(to[:, ch, :], to[:, ch, :], shift(ch), None, ALU.add)
                    ins.then_inc(resid_ready if name == "final" else norm_h, 1)
                    if used is not None and q == 1:
                        dve.wait_ge(parts_done, used)
                    if q >= 1 and name != "final":
                        low(q - 1)
                if name != "final":
                    if used is not None and len(pairs(c)) == 1:
                        dve.wait_ge(parts_done, used)
                    low(len(pairs(c)) - 1)

            def wait_part(s, b):
                dve.wait_ge(parts_done, wait_count(s, b))

            def two(bank):
                return ps[:, bank, :].rearrange("p (c t) -> p c t", c=2)

            def sum_before(following, j, b):
                if (j, b) == (1, 0) and following:
                    sum_squares(following, 1)
                    sum_squares(following, 2)

            def add_to_residual(phase, j, following=None):
                for b in range(2):
                    s = Slot(phase, j if phase.startswith("w_o") else 4 * j + 3)
                    wait_part(s, b)
                    x = xT[:, 4 * j + 2 * b:4 * j + 2 * b + 2, :]
                    nc.vector.tensor_tensor(x, x, two(b), ALU.add).then_inc(acc_out[b], 1)
                    sum_before(following, j, b)

            def add_gated(phase, j, l, following=None):
                for b in range(2):
                    wait_part(Slot(phase, j), b)
                    for ch in range(2):
                        x = xT[:, 4 * j + 2 * b + ch, :]
                        g = 16 + 4 * j + 2 * b + ch
                        ins = nc.vector.scalar_tensor_tensor(x, ps[:, b, ch * T:(ch + 1) * T], mod[:, l, g:g + 1], x,
                                                             ALU.mult, ALU.add)
                    ins.then_inc(acc_out[b], 1)
                    sum_before(following, j, b)

            dve.wait_ge(turned, 1)
            nc.vector.tensor_copy(col_a[:, :], ps[:, 2, 0:ROWS_A]).then_inc(unturned, 1)
            dve.wait_ge(turned, 2)
            nc.vector.tensor_copy(col_b[:, :], ps[:, 3, 0:ROWS_B]).then_inc(unturned, 1)
            for q, bank in enumerate((4, 5, 2, 3)):
                dve.wait_ge(turned, 3 + q)
                nc.vector.tensor_copy(memT[:, 2 * q:2 * q + 2, :], two(bank)).then_inc(unturned, 1)
            dve.wait_ge(unturned, 6)
            lam = col_a[:, COL_A["lam"]:COL_A["lam"] + 4]
            nc.vector.scalar_tensor_tensor(lam4[:, 0, :], lam, -1.0, lam, ALU.mult, ALU.max).then_inc(vec_cols, 1)
            nc.vector.tensor_scalar(lam4[:, 2, :], lam, -1.0, 0.0, ALU.mult, ALU.max).then_inc(vec_cols, 1)
            gq, gk = (col_b[:, COL_B[x]:COL_B[x] + 1] for x in ("gq", "gk"))
            nc.vector.scalar_tensor_tensor(gqk[:, :], gq, HD ** -0.5, gk, ALU.mult, ALU.mult).then_inc(gqk_ready, 1)
            split(Slot("mem", 0))
            norm("mem")
            split(Slot("mem", 1))

            dve.wait_ge(pos_loaded, 64)
            dve.wait_ge(consts, 3)
            link(nc.vector.tensor_copy(posq[:, :], posq_i[:, :]))
            nc.vector.tensor_scalar(negsink[:, :], sink[:, :], -1.0, None, ALU.mult)
            for t in range(NT):
                ins = nc.vector.tensor_scalar(angle[:, 0, t * HALF:(t + 1) * HALF], inv_freq[:, :], posq[:, t:t + 1], None, ALU.mult)
            link(ins)
            ang, arg, cos_arg, turns, _ = (angle[:, q, :] for q in range(5))
            link(nc.vector.tensor_scalar(turns, ang, 1.0 / (2.0 * math.pi), 1.5 * 2.0 ** 23, ALU.mult, ALU.add))
            link(nc.vector.tensor_scalar(turns, turns, -1.5 * 2.0 ** 23, None, ALU.add))
            first, second = 6.28125, 0.0019350051879882812
            link(nc.vector.scalar_tensor_tensor(arg, turns, -first, ang, ALU.mult, ALU.add))
            link(nc.vector.scalar_tensor_tensor(arg, turns, -second, arg, ALU.mult, ALU.add))
            link(nc.vector.scalar_tensor_tensor(arg, turns, -(2.0 * math.pi - first - second), arg, ALU.mult, ALU.add))
            link(nc.vector.tensor_scalar(arg, arg, 3.1415925, -3.1415925, ALU.min, ALU.max))
            link(nc.vector.scalar_tensor_tensor(cos_arg, arg, -1.0, arg, ALU.mult, ALU.max))
            nc.vector.tensor_scalar(cos_arg, cos_arg, -1.0, math.pi / 2.0, ALU.mult, ALU.add).then_inc(angles, 1)

            for l, values in enumerate((mem_v0, mem_v1)):
                wait_part(Slot("mem", l), 1)
                nc.vector.tensor_copy(values[:, :, :], two(1)).then_inc(acc_out[1], 1)
                if l == 0:
                    split(Slot("mem", 2))
            dve.wait_ge(lam_log, 1)
            link(nc.vector.tensor_tensor(lam4[:, 5, :], lam4[:, 2, :], lam4[:, 1, :], ALU.add))
            for to, factor in ((3, -8.0), (4, 8.0)):
                nc.vector.tensor_scalar(lam4[:, to, :], lam4[:, 5, :], factor, None, ALU.mult).then_inc(decay_rates, 1)
            norm("attn0", used=parts_through(1))
            split(Slot("mem", 3))

            wait_part(Slot("w_in", 0), 1)
            nc.vector.tensor_copy(cqT[:, 2, :], ps[:, 1, 0:T])
            nc.vector.tensor_copy(ckvT[:, 0, :], ps[:, 1, T:2 * T]).then_inc(acc_out[1], 1)
            norm("qn")
            split(Slot("w_in", 2))
            wait_part(Slot("w_in", 1), 1)
            nc.vector.tensor_scalar(qx0[:, 1, :], ps[:, 1, 0:T], -HD ** -0.5, None, ALU.mult)
            nc.vector.tensor_copy(krow[:, :, :], ps[:, 1, T:T + NT * ROPE].rearrange("p (t r) -> p t r", t=NT)).then_inc(acc_out[1], 1)
            norm("kvn")
            split(Slot("w_in", 3))
            for g in range(3):
                dve.wait_ge(parts_done, Slot("w_uq", 0).before + 2 * g + 2)
                nc.vector.tensor_scalar(q_rows[:, 1, 4 * g:4 * g + 4, :], ps[:, 1, 0:4 * QK].rearrange("p (h d) -> p h d", h=4),
                                        -QK ** -0.5, None, ALU.mult).then_inc(acc_out[1], 1)

            def rope(src, to, heads):
                c, sn = (x[:, :, :].unsqueeze(2).to_broadcast([P, NT, heads, HALF]) for x in (cosT, sinT))
                x1, x2 = src[:, :, :, 0:HALF], src[:, :, :, HALF:ROPE]
                t = [rope_tmp[:, q, :, 0:heads, :] for q in range(4)]
                for q, (x, trig) in enumerate(((x1, c), (x2, sn), (x1, sn), (x2, c))):
                    ins = nc.vector.tensor_tensor(t[q], x, trig, ALU.mult)
                link(ins)
                nc.vector.tensor_tensor(to[:, :, :, 0:HALF], t[0], t[1], ALU.subtract)
                link(nc.vector.tensor_tensor(to[:, :, :, HALF:ROPE], t[2], t[3], ALU.add))

            for g in range(3):
                dve.wait_ge(parts_done, Slot("w_ukv", 0).before + 2 * g + 2)
                kv = ps[:, 1, :].rearrange("p (h d) -> p h d", h=4)
                nc.vector.tensor_copy(k_rows[:, 1, 4 * g:4 * g + 4, 0:HD], kv[:, :, 0:HD])
                nc.vector.tensor_copy(v_rows[:, 1, 4 * g:4 * g + 4, :], kv[:, :, HD:2 * HD]).then_inc(acc_out[1], 1)
                if g == 0:
                    dve.wait_ge(sines, 3)
                    dve.wait_ge(acc_out[1], turn("w_uq", 2) + 1)
                    rope(krow[:, :, :].unsqueeze(2), krot[:, :, :].unsqueeze(2), 1)
                    dve.wait_ge(acc_out[0], turn("w_uq", 2) + 1)
                    rope(q_rows[:, :, :, HD:QK], q_rows[:, :, :, HD:QK], MLA_HEADS)
            nc.vector.tensor_copy(k_rows[:, :, :, HD:QK],
                                  krot[:, :, :].unsqueeze(2).to_broadcast([P, NT, MLA_HEADS, ROPE])).then_inc(rope_done, 1)
            for j in range(6):
                dve.wait_ge(qk_banks, 2 * j + 2)
                nc.vector.tensor_copy(mla_kT[0:QK, 2 * j:2 * j + 2, :],
                                      ps[0:QK, 4 + j % 2, :].rearrange("p (h t) -> p h t", h=2)).then_inc(k_out, 1)
            split(Slot("w_o0", 0))

            def bias_head(hc):
                kind, l, h = HEADS[hc]
                g, j, b = hc // 4, hc % 4, hc % 2
                dve.wait_ge(scores, hc + 1)
                if hc >= 2:
                    dve.wait_ge(probs_turned, hc - 1)
                if kind == "cross":
                    nc.vector.tensor_reduce(negmax[:, g, :, j], two(2 + b), AX.X, ALU.min).then_inc(biased, 1)
                    return
                p = (probs0 if kind == "mla" else probs1)[:, b, :]
                if kind == "swa":
                    dve.wait_ge(alibi_ready, h + 1)
                bias = causal[:, :] if kind == "mla" else alibi[:, h % 2, :]
                start = 3.0e38 if kind == "mla" else negsink[:, h:h + 1]
                for t, cut in enumerate((slice(0, P), slice(P, 3 * P))):
                    ins = nc.vector.tensor_tensor_reduce(p[:, cut], ps[:, 2 + b, cut], bias[:, cut], 1.0, start, ALU.add,
                                                         ALU.min, negmax[:, g, t, j:j + 1])
                ins.then_inc(biased, 1)

            def group_out(g, rows_to, first):
                dve.wait_ge(exped, 4 * g + 4)
                if HEADS[4 * g][0] == "swa":
                    dve.wait_ge(sink_exp, g - 3)
                    link(nc.vector.tensor_tensor(sums[:, g, :, :], sums[:, g, :, :], sinkexp[:, :, :], ALU.add))
                link(nc.vector.reciprocal(rsum[:, :, :], sums[:, g, :, :]))
                dve.wait_ge(heads_done, 4 * g + 4)
                nc.vector.tensor_tensor(rows_to[:, :, first:first + 4 * HD].rearrange("p t (h d) -> p t h d", h=4),
                                        ps[:, 6 + g % 2, :].rearrange("p (t h d) -> p t h d", t=NT, h=4),
                                        rsum[:, :, :].unsqueeze(3).to_broadcast([P, NT, 4, HD]), ALU.mult).then_inc(o_copied, 1)
                dve.wait_ge(o_copied, g + 1)

            def heads(first, last, rows_to):
                for hc in range(first, last + 2):
                    if hc < last:
                        bias_head(hc)
                        if hc % 4 == 3 and HEADS[hc][0] == "swa":
                            g = hc // 4
                            h = 4 * (g - 4)
                            dve.wait_ge(biased, hc + 1)
                            nc.vector.tensor_tensor(sinkexp[:, :, :], negmax[:, g, :, :],
                                                    sink[:, h:h + 4].unsqueeze(1).to_broadcast([P, NT, 4]), ALU.add)\
                                .then_inc(sink_arg, 1)
                    if hc >= first + 5 and (hc - 1) % 4 == 0:
                        group_out((hc - 5) // 4, rows_to, (hc - 5 - first) * HD)

            def mix_low(n, sources):
                for q in range(4):
                    dve.wait_ge(mix_hi, 4 * n + q + 1)
                    nc.vector.tensor_tensor(h_lo[:, 2 * q:2 * q + 2, :], sources[q], h_hi[:, 2 * q:2 * q + 2, :].bitcast(F32),
                                            ALU.subtract).then_inc(mix_lo, 1)

            heads(0, 16, o_rows0)
            mix_low(0, [two(2 + q) for q in range(4)])
            split(Slot("w_o0", 1))
            add_to_residual("w_o0", 0)
            split(Slot("w_o0", 2))
            add_to_residual("w_o0", 1, following="mlp0")

            ada_sum = scratch[:, 0:2, :].rearrange("p c t -> p (c t)")

            def ada_unit(m, slot, quarter, loads):
                dve.wait_ge(ada_loaded[slot], loads)
                for q in range(2):
                    w, c = ada_raw[:, slot, q, :], silu_c[:, 2 * quarter + q:2 * quarter + q + 1]
                    if quarter == 0 and q == 0:
                        ins = nc.vector.tensor_scalar(ada_sum, w, c, None, ALU.mult)
                    else:
                        dve.wait_ge(ada_step, m * 2 + q)
                        ins = nc.vector.scalar_tensor_tensor(ada_sum, w, c, ada_sum, ALU.mult, ALU.add)
                    ins.then_inc(ada_step, 1)

            def ada_units(slot_no, j, i=None):
                grow = (lambda per, first: first) if i is None else (lambda per, first: i * per + first)
                for u in range(2):
                    ada_unit(grow(4, 2 * slot_no + u), u, 2 * (j % 2) + u, grow(32, 16 * (slot_no + 1)))

            def ada_group_done(group):
                dve.wait_ge(ada_reduced, group)

            def ada_keep(third):
                link(nc.vector.tensor_copy(ada_cols[:, 32 * third:32 * (third + 1)], ps[:, ADA_BANK, 0:32]))

            def modulation(l):
                c = COL_B[f"ada_b{l}"]
                link(nc.vector.tensor_tensor(mod[:, l, :], ada_cols[:, 48 * l:48 * (l + 1)], col_b[:, c:c + 48], ALU.add))
                for q, key in enumerate((f"mix{l}", f"ffn{l}")):
                    ins = nc.vector.scalar_tensor_tensor(modg[:, l, q, :], mod[:, l, 8 + 24 * q:16 + 24 * q], 1.0,
                                                         col_a[:, COL_A[key]:COL_A[key] + KD], ALU.add, ALU.mult)
                link(ins)

            def mlp(l):
                norm(f"mlp{l}", summed=True)
                split(Slot(f"up{l}", 1))
                with dve.Fori(0, 4) as i:
                    for j in range(2):
                        for b in range(2):
                            at_pair = bass.ds(i * 8 + (4 * j + 2 * b), 2)
                            dve.wait_ge(hid_hi, i * 4 + (HIDDEN_BEFORE[str(l)] + 2 * j + b + 1))
                            nc.vector.tensor_tensor(a_lo[:, at_pair, :], a_full[:, at_pair, :],
                                                    a_hi[:, at_pair, :].bitcast(F32), ALU.subtract).then_inc(hid_lo, 1)
                            if b == 0:
                                ada_units(16 * l + j, j, i)
                        split(Slot(f"up{l}", j + 2, i, 2))
                    ada_group_done(i + (8 * l + 1))
                for j in range(8):
                    ada_units(16 * l + 8 + j, j)
                    if j % 4 == 3:
                        add_to_residual(f"down{l}", j // 4, following=("attn1", "final")[l])
                    if j < 7:
                        split(Slot(f"down{l}", j + 2))
                    if j % 2:
                        ada_group_done(8 * l + 4 + j // 2 + 1)

            mlp(0)

            norm("attn1", summed=True)
            ada_keep(0)
            nc.vector.tensor_scalar(dist[:, 0:P], posk_i[:, 0:P], -1.0, posq[:, 0:1], ALU.mult, ALU.add).then_inc(dist_ready, 1)
            nc.vector.tensor_scalar(dist[:, P:3 * P], posk_i[:, :], -1.0, posq[:, 1:2], ALU.mult, ALU.add).then_inc(dist_ready, 1)
            split(Slot("down0", 9))
            for j in range(4):
                wait_part(Slot("swa", j), 1)
                if j < 2:
                    nc.vector.tensor_scalar(swa_qT[:, 3 * j + 2, :], ps[:, 1, 0:T], -HD ** -0.5, None, ALU.mult).then_inc(acc_out[1], 1)
                else:
                    nc.vector.tensor_copy(swa_v[:, :, (j - 2) * P:(j - 1) * P],
                                          ps[:, 1, 0:NT * P].rearrange("p (t d) -> p t d", t=NT)).then_inc(acc_out[1], 1)
                if j < 3:
                    split(Slot("swa", j + 2))
            heads(16, 32, o_rows1)
            mix_low(1, [two(2 + q) for q in range(4)])
            split(Slot("swa", 5))
            add_to_residual("w_o1", 0)
            split(Slot("swa", 6))
            add_to_residual("w_o1", 1, following="mlp1")
            mlp(1)

            norm("final", summed=True)
            ada_keep(1)
            modulation(0)
            norm("mix0")
            split(Slot("down1", 9))
            link(nc.vector.memset(conv_in[:, :, 0:2], 0.0))
            link(nc.vector.memset(rx[:, :, 0:3], 0.0))
            split(Slot("lru_in", 2))
            split(Slot("lru_in", 3))
            for b in range(2):
                wait_part(Slot("lru_in", 2), b)
                cut = slice(2 * b, 2 * b + 2)
                dve.wait_ge(acc_out[b], turn("lru_in", 1) + 1)
                nc.vector.tensor_tensor(conv_in[:, cut, 2:2 + T], gate_c[:, cut, :], two(b), ALU.mult).then_inc(acc_out[b], 1)
                dve.wait_ge(acc_out[b], turn("lru_in", 2) + 1)
            split(Slot("lru_in", 4))

            def conv(to, src, taps, cols, key, bias=None):
                for k in range(taps):
                    for c in range(4):
                        w = cols[:, key + 4 * k + c:key + 4 * k + c + 1]
                        if k == 0 and bias is None:
                            ins = nc.vector.tensor_scalar(to[:, c, :], src[:, c, 0:T], w, None, ALU.mult)
                        elif k == 0:
                            ins = nc.vector.tensor_scalar(to[:, c, :], src[:, c, 0:T], w, bias(c), ALU.mult, ALU.add)
                        else:
                            ins = nc.vector.scalar_tensor_tensor(to[:, c, :], src[:, c, k:k + T], w, to[:, c, :], ALU.mult, ALU.add)
                    link(ins)

            conv(y_mix, conv_in, 3, col_a, COL_A["conv_a"])
            for q in range(2):
                cut = slice(2 * q, 2 * q + 2)
                nc.vector.tensor_tensor(y_mix[:, cut, :], y_mix[:, cut, :], gate_b[:, cut, :], ALU.mult).then_inc(mix_full, 1)
            split(Slot("lru_in", 5))
            for b in range(2):
                dve.wait_ge(acc_out[b], turn("lru_in", 4) + 1)
            cb = COL_A["convb_b"]
            conv(xr, rx, 4, col_b, COL_B["conv_b"], lambda c: col_a[:, cb + c:cb + c + 1])
            nc.vector.memset(sb_ms[:, 4, :, :], 0.0).then_inc(xr_ready, 1)
            dve.wait_ge(gates_out, 8)
            link(nc.vector.tensor_tensor(rg_i[:, :, :], rg_i[:, :, :], xr[:, :, :], ALU.mult))
            dve.wait_ge(decay, 4)
            dve.wait_ge(tanh_done, 4)
            link(nc.vector.tensor_tensor(rg_r[:, :, :], lru_a[:, :, :], lru_a[:, :, :], ALU.mult))
            nc.vector.scalar_tensor_tensor(lru_b[:, :, :], rg_r[:, :, :], 1.0, lru_b[:, :, :], ALU.add, ALU.mult).then_inc(gain_sq, 1)
            dve.wait_ge(gain, 1)
            link(nc.vector.tensor_tensor(lru_b[:, :, :], lru_b[:, :, :], rg_i[:, :, :], ALU.mult))
            for c in range(4):
                ins = nc.vector.tensor_tensor_scan(lru_h[:, c, :], lru_a[:, c, :], lru_b[:, c, :], 0.0, ALU.mult, ALU.add)
            link(ins)
            for q in range(2):
                cut = slice(2 * q, 2 * q + 2)
                nc.vector.tensor_tensor(lru_h[:, cut, :], lru_h[:, cut, :], gelu_r[:, cut, :], ALU.mult).then_inc(mix_full, 1)
            dve.wait_ge(mix_full, 4)
            mix_low(2, [y_mix[:, 0:2, :], y_mix[:, 2:4, :], lru_h[:, 0:2, :], lru_h[:, 2:4, :]])
            split(Slot("lru_out", 1))
            add_gated("lru_out", 0, 0)
            split(Slot("lru_out", 2))
            add_gated("lru_out", 1, 0, following="ffn0")

            def ffn(l):
                norm(f"ffn{l}", summed=True)
                split(Slot(f"gate_up{l}", 1))

                def hidden(j, i=None):
                    s, ahead = Slot(f"gate_up{l}", j, i, 2), Slot(f"gate_up{l}", j + 2, i, 2)
                    at_pair = bass.ds(i * 4 + 2 * j, 2) if i is not None else slice(2 * j, 2 * j + 2)
                    grow = (lambda first: first) if i is None else (lambda first: i * 2 + first)
                    full = a_full[:, at_pair, :]
                    if l == 0 and j < 10:
                        ada_units(32 + j, j, i)
                    dve.wait_ge(parts_done, s.before + 2)
                    dve.wait_ge(acc_out[0], grow(turn(f"gate_up{l}", j) + 1))
                    nc.vector.tensor_tensor(full, full, two(1), ALU.mult).then_inc(acc_out[1], 1)
                    dve.wait_ge(hid_hi, grow(HIDDEN_BEFORE[f"ffn{l}"] + j + 1))
                    nc.vector.tensor_tensor(a_lo[:, at_pair, :], full, a_hi[:, at_pair, :].bitcast(F32),
                                            ALU.subtract).then_inc(hid_lo, 1)
                    split(ahead)

                def add(i):
                    for b in range(2):
                        dve.wait_ge(parts_done, i * 4 + (Slot(f"ffn_down{l}", 1).before + b + 1))
                        if isinstance(i, int):
                            x, g = xT[:, 2 * i + b, :], mod[:, l, 40 + 2 * i + b:41 + 2 * i + b]
                        else:
                            x, g = xT[:, bass.ds(i * 2 + b, 1), :], mod[:, l, bass.ds(i * 2 + (40 + b), 1)]
                        y = ps[:, b, 0:T] if isinstance(i, int) else ps[:, b, 0:T].unsqueeze(1)
                        nc.vector.scalar_tensor_tensor(x, y, g, x, ALU.mult, ALU.add).then_inc(acc_out[b], 1)

                with dve.Fori(0, 4) as i:
                    for j in range(2):
                        hidden(j, i)
                    if l == 0:
                        ada_group_done(i + 17)
                for j in (8, 9, 10):
                    hidden(j)
                    if l == 0 and j == 9:
                        ada_group_done(21)
                with dve.Fori(0, 3) as i:
                    if l == 0:
                        ada_units(42, 0, i)
                    split(Slot(f"ffn_down{l}", 2, i, 2))
                    if l == 0:
                        ada_units(43, 1, i)
                    add(i)
                    split(Slot(f"ffn_down{l}", 3, i, 2))
                    if l == 0:
                        ada_group_done(i + 22)
                if l == 0:
                    ada_keep(2)
                    modulation(1)
                if l == 0:
                    split(Slot("qkv", 0))
                    sum_squares("mix1", 1)
                    sum_squares("mix1", 2)
                add(3)

            ffn(0)
            norm("mix1", summed=True)
            split(Slot("qkv", 1))

            for j in range(6):
                if j < 4:
                    part, half = j // 2, j % 2
                    for b in range(2):
                        dve.wait_ge(qk_sq, 2 * j + b + 1)
                        ins = nc.vector.tensor_reduce(sb_ms[:, 0, b, :], sb_sq[:, b, :].rearrange("p (h d) -> p h d", h=8),
                                                      AX.X, ALU.add)
                    link(ins)
                    ms, y, t, r = (sb_ms[:, q, :, :] for q in (0, 1, 2, 3))
                    nc.vector.tensor_scalar(ms, ms, 1.0 / HD, EPS, ALU.mult, ALU.add).then_inc(qk_var, 1)
                    dve.wait_ge(qk_y, j + 1)
                    link(nc.vector.tensor_tensor(t, y, y, ALU.mult))
                    link(nc.vector.scalar_tensor_tensor(t, t, -0.5, ms, ALU.mult, ALU.mult))
                    link(nc.vector.scalar_tensor_tensor(r, t, 1.5, y, ALU.add, ALU.mult))
                    for b in range(2):
                        x = sb_rows[:, part, b, half * BANK:(half + 1) * BANK].rearrange("p (h d) -> p h d", h=8)
                        ins = nc.vector.tensor_tensor(x, x, sb_ms[:, 3, b, :].unsqueeze(2).to_broadcast([P, 8, HD]), ALU.mult)
                    ins.then_inc(qk_scaled, 1)
                    dve.wait_ge(qk_scaled, j + 1)
                if j < 5:
                    split(Slot("qkv", j + 2))
            for h in range(SB_HEADS + 1):
                if h < SB_HEADS:
                    b = h % 2
                    z, soft = ps[:, 2 + b, 0:384], sb_l[:, b, :]
                    dve.wait_ge(z_soft, h + 1)
                    if h >= 2:
                        dve.wait_ge(sums_ready, h - 1)
                        dve.wait_ge(heads_done, len(HEADS) + h - 1)
                    nc.vector.scalar_tensor_tensor(sb_sp[:, b, :], z, 0.0, soft, ALU.max, ALU.add).then_inc(sp_ready, 1)
                    nc.vector.scalar_tensor_tensor(sb_u[:, b, :], z, 0.0, soft, ALU.min, ALU.subtract).then_inc(u_ready, 1)
                if h >= 1:
                    b = (h - 1) % 2
                    dve.wait_ge(sums_ready, h)
                    dve.wait_ge(u_ready, h)
                    nc.vector.tensor_tensor(sb_u[:, b, :], sb_u[:, b, :], ps[:, 4 + b, 0:384], ALU.subtract).then_inc(logw_ready, 1)
            mix_low(3, [two(2 + q) for q in range(4)])
            split(Slot("sb_out", 1))
            add_gated("sb_out", 0, 1)
            split(Slot("sb_out", 2))
            add_gated("sb_out", 1, 1, following="ffn1")
            ffn(1)
            for q in range(2):
                dve.wait_ge(turned, 13 + q)
                nc.vector.tensor_copy(o_final[:, 1, q * BANK:(q + 1) * BANK], ps[:, 4 + q, :]).then_inc(out_copied[1], 1)

        @block.tensor
        def _(pe):
            def product(to, sh, sl, mh, ml, first, last):
                nc.tensor.matmul(to, sh, mh, start=first, stop=False, skip_group_check=True)
                nc.tensor.matmul(to, sh, ml, start=False, stop=False, skip_group_check=True)
                return nc.tensor.matmul(to, sl, mh, start=False, stop=last, skip_group_check=True)

            def begin(s):
                pe.wait_ge(split_lo, s.split + 2)
                return ring(w_hi, s.slot, s.kc, s.cols), ring(w_lo, s.slot, s.kc, s.cols)

            def features(s, b, blocks, hi, lo, first=True, last=True, chunk=0):
                wh, wl = ring(w_hi, s.slot, s.kc, s.cols), ring(w_lo, s.slot, s.kc, s.cols)
                for q, block_of in enumerate(blocks):
                    for c in range(s.kc):
                        ins = product(ps[:, b, q * T:(q + 1) * T], block_of(wh, c), block_of(wl, c),
                                      hi[:, chunk + c, :], lo[:, chunk + c, :],
                                      first and q == 0 and c == 0, last and q == len(blocks) - 1 and c == s.kc - 1)
                return ins

            def token_rows(s, to, t, col, n, hi, lo, first=True, last=True):
                wh, wl = ring(w_hi, s.slot, s.kc, s.cols), ring(w_lo, s.slot, s.kc, s.cols)
                cut = slice(t * P, (t + 1) * P)
                for c in range(s.kc):
                    ins = product(to, hi[:, c, cut], lo[:, c, cut], wh[:, c, col:col + n], wl[:, c, col:col + n],
                                  first and c == 0, last and c == s.kc - 1)
                return ins

            def at_col(col):
                return lambda w, c: w[:, c, col:col + P]

            def wait_acc(b, t):
                pe.wait_ge(acc_out[b], t)

            def norm_sum_all(name):
                k = NORM_AT[name]
                pe.wait_ge(norm_sum, k + 1)
                nc.tensor.matmul(ps[:, NORM_BANK, 0:T], ones[:, :], scratch[:, 0, :], start=True, stop=True).then_inc(norm_total, 1)

            def wait_norm(name):
                pe.wait_ge(norm_lo, NORM_PAIRS[NORM_AT[name] + 1])

            def two_bank_slot(phase, j, i=None, step=0):
                s = Slot(phase, j, i, step)
                pe.wait_ge(split_lo, s.split + 2)
                for b in range(2):
                    wait_acc(b, turn(phase, j, i, step))
                    features(s, b, [at_col((2 * b + q) * P) for q in range(2)], h_hi, h_lo).then_inc(parts_done, 1)

            def four_blocks(phase, slots, first=0):
                for j in range(first, slots):
                    two_bank_slot(phase, j)

            def as_chunks_arrive(phase, name, work=None):
                s = Slot(phase, 0)
                wh, wl = ring(w_hi, s.slot, s.kc, s.cols), ring(w_lo, s.slot, s.kc, s.cols)
                k = NORM_AT[name]
                if work is None:
                    work = [("features", (2 * b * P, (2 * b + 1) * P)) for b in range(2)]
                regions = []
                for b, (kind, *what) in enumerate(work):
                    if kind == "features":
                        regions.append([(ps[:, b, q * T:(q + 1) * T],
                                         lambda c, col=col: (wh[:, c, col:col + P], wl[:, c, col:col + P], h_hi[:, c, :], h_lo[:, c, :]))
                                        for q, col in enumerate(what[0])])
                    else:
                        col, n, tiles = what
                        regions.append([(ps[:, b, to:to + n],
                                         lambda c, t=t: (h_hi[:, c, t * P:(t + 1) * P], h_lo[:, c, t * P:(t + 1) * P],
                                                         wh[:, c, col:col + n], wl[:, c, col:col + n]))
                                        for t, to in tiles])
                pe.wait_ge(split_lo, s.split + 2)
                for b in range(2):
                    if turn(phase, 0):
                        wait_acc(b, turn(phase, 0))
                for p, chunks in enumerate(pairs(KD)):
                    pe.wait_ge(norm_lo, NORM_PAIRS[k] + p + 1)
                    for b in range(2):
                        for r, (to, operands) in enumerate(regions[b]):
                            for c in chunks:
                                ins = product(to, *operands(c), c == 0 and r == 0, c == KD - 1 and r == len(regions[b]) - 1)
                        if chunks[-1] == KD - 1:
                            ins.then_inc(parts_done, 1)

            def turn_pair(bank, src, ncols=P):
                for ch in range(2):
                    for t in range(NT):
                        ins = nc.tensor.transpose(ps[0:ncols, bank, ch * T + t * P:ch * T + (t + 1) * P], src(ch, t), ident[:, :])
                return ins

            pe.wait_ge(consts, 2)
            pe.wait_ge(vec_loaded, 16 * 23)
            nc.tensor.transpose(ps[:, 2, 0:ROWS_A], rows_a[0:ROWS_A, :], ident[0:ROWS_A, 0:ROWS_A]).then_inc(turned, 1)
            nc.tensor.transpose(ps[:, 3, 0:ROWS_B], rows_b[0:ROWS_B, :], ident[0:ROWS_B, 0:ROWS_B]).then_inc(turned, 1)
            pe.wait_ge(mem_loaded, 16)
            for q, bank in enumerate((4, 5, 2, 3)):
                if q >= 2:
                    pe.wait_ge(unturned, q - 1)
                turn_pair(bank, lambda ch, t: rows_mem[:, t, (2 * q + ch) * P:(2 * q + ch + 1) * P]).then_inc(turned, 1)
            pe.wait_ge(x_loaded, 16)
            for q in range(4):
                pe.wait_ge(unturned, (5, 6, 3, 4)[q])
                turn_pair(2 + q, lambda ch, t: rows_x[:, t, (2 * q + ch) * P:(2 * q + ch + 1) * P]).then_inc(turned, 1)

            norm_sum_all("mem")
            as_chunks_arrive("mem", "mem", [("features", (0, P)), ("rows", CROSS, CROSS, [(0, 0), (1, T)])])
            s = Slot("mem", 1)
            pe.wait_ge(split_lo, s.split + 2)
            wait_acc(0, 1)
            features(s, 0, [at_col(0), at_col(P)], h_hi, h_lo).then_inc(parts_done, 1)
            wait_acc(1, 1)
            token_rows(s, ps[:, 1, 0:T], 0, CROSS, CROSS, h_hi, h_lo, last=False)
            token_rows(s, ps[:, 1, T:2 * T], 1, CROSS, CROSS, h_hi, h_lo, first=False).then_inc(parts_done, 1)

            norm_sum_all("attn0")
            as_chunks_arrive("w_in", "attn0")
            s, t = Slot("w_in", 1), turn("w_in", 1)
            pe.wait_ge(split_lo, s.split + 2)
            wait_acc(0, t)
            features(s, 0, [at_col(0), at_col(P + ROPE)], h_hi, h_lo).then_inc(parts_done, 1)
            norm_sum_all("qn")
            wait_acc(1, t)
            features(s, 1, [at_col(2 * P + ROPE)], h_hi, h_lo, last=False)
            for tile in range(NT):
                ins = token_rows(s, ps[:, 1, T + tile * ROPE:T + (tile + 1) * ROPE], tile, P, ROPE, h_hi, h_lo,
                                 first=False, last=tile == 1)
            ins.then_inc(parts_done, 1)
            norm_sum_all("kvn")
            for phase, name, hi, lo, n in (("w_uq", "qn", cq_hi, cq_lo, 4 * QK), ("w_ukv", "kvn", ckv_hi, ckv_lo, 8 * HD)):
                s = Slot(phase, 0)
                wait_norm(name)
                pe.wait_ge(split_lo, s.split + 2)
                for g in range(3):
                    for tile in range(NT):
                        wait_acc(tile, turn(phase, g))
                        token_rows(s, ps[:, tile, 0:n], tile, g * n, n, hi, lo).then_inc(parts_done, 1)
            pe.wait_ge(rope_done, 1)
            pe.wait_ge(resid_ready, 4)
            for c in range(2):
                pe.wait_ge(acc_out[c], turn("w_ukv", 2) + 1)
            for j in range(6):
                if j >= 2:
                    pe.wait_ge(q_out, j - 1)
                turn_pair(2 + j % 2, lambda ch, t: q_rows[:, t, 2 * j + ch, :], QK).then_inc(qk_banks, 1)
                if j >= 2:
                    pe.wait_ge(k_out, j - 1)
                turn_pair(4 + j % 2, lambda ch, t: k_rows[:, t, 2 * j + ch, :], QK).then_inc(qk_banks, 1)

            def score_head(hc):
                kind, l, h = HEADS[hc]
                b = hc % 2
                if hc >= 2:
                    pe.wait_ge(exped if HEADS[hc - 2][0] == "cross" else biased, hc - 1)
                s = ps[:, 2 + b, :]
                if kind == "cross":
                    rows_of = slice(h % 2 * HD, (h % 2 + 1) * HD)
                    q, k = (qx0 if l == 0 else qx1)[rows_of, h // 2, :], (mem_k0 if l == 0 else mem_k1)[rows_of, h // 2, :]
                    nc.tensor.matmul(s[:, 0:T], q[:, 0:P], k, start=True, stop=False, skip_group_check=True)
                    nc.tensor.matmul(s[:, T:2 * T], q[:, P:T], k, start=False, stop=True, skip_group_check=True).then_inc(scores, 1)
                    return
                if kind == "mla":
                    q, k = mla_qT[0:QK, h, :], mla_kT[0:QK, h, :]
                else:
                    kv = h // SWA_GROUP
                    rows_of = slice(h % 2 * HD, (h % 2 + 1) * HD)
                    keys = swa_kT if h % 2 == kv % 2 else swa_kT_swapped
                    q, k = swa_qT[rows_of, h // 2, :], keys[rows_of, kv // 2, :]
                nc.tensor.matmul(s[:, 0:P], q[:, 0:P], k[:, 0:P], start=True, stop=False, skip_group_check=True)
                nc.tensor.matmul(s[:, P:3 * P], q[:, P:T], k, start=False, stop=True, skip_group_check=True).then_inc(scores, 1)

            def prob_blocks(hc):
                return [(0, 0), (0, 1), (1, 0), (1, 1)] if HEADS[hc][0] == "cross" else [(0, 0), (1, 0), (1, 1)]

            def turn_probs(hc):
                kind, l, h = HEADS[hc]
                b = hc % 2
                pe.wait_ge(exped, hc + 1)
                if hc >= 2:
                    pe.wait_ge(probs_copied, hc - 1)
                p = {"mla": probs0, "swa": probs1, "cross": cross_p0 if l == 0 else cross_p1}[kind][:, b, :]
                for n in range(len(prob_blocks(hc))):
                    ins = nc.tensor.transpose(ps[:, 4 + b, n * P:(n + 1) * P], p[:, n * P:(n + 1) * P], ident[:, :])
                ins.then_inc(probs_turned, 1)

            def values_head(hc):
                kind, l, h = HEADS[hc]
                g, j = hc // 4, hc % 4
                pe.wait_ge(probs_copied, hc + 1)
                if j == 0 and g >= 2:
                    pe.wait_ge(o_copied, g - 1)
                p = {"mla": probsT0, "swa": probsT1, "cross": cross_pT0 if l == 0 else cross_pT1}[kind][:, hc % 2, :]
                blocks = prob_blocks(hc)
                for n, (qt, kt) in enumerate(blocks):
                    if kind == "mla":
                        v = v_rows[:, kt, h, :]
                    elif kind == "swa":
                        v = swa_v[:, kt, h // SWA_GROUP * HD:(h // SWA_GROUP + 1) * HD]
                    else:
                        v = (mem_v0 if l == 0 else mem_v1)[:, kt, h * HD:(h + 1) * HD]
                    ins = nc.tensor.matmul(ps[:, 6 + g % 2, qt * T + j * HD:qt * T + (j + 1) * HD], p[:, n * P:(n + 1) * P], v,
                                           start=j == 0 and n == 0, stop=j == 3 and n == len(blocks) - 1, skip_group_check=True)
                ins.then_inc(heads_done, 1)

            def heads(first, last):
                score_head(first)
                for hc in range(first, last + 1):
                    if hc + 1 < last:
                        score_head(hc + 1)
                    if hc < last:
                        turn_probs(hc)
                    if hc > first:
                        values_head(hc - 1)

            def mix_turn(n, rows_from, copied):
                pe.wait_ge(o_copied, copied)
                for q in range(4):
                    turn_pair(2 + q, lambda ch, t: rows_from[:, t, (2 * q + ch) * P:(2 * q + ch + 1) * P]).then_inc(mix_turned, 1)

            pe.wait_ge(q_out, 6)
            pe.wait_ge(k_out, 6)
            heads(0, 16)
            mix_turn(0, o_rows0, 4)
            pe.wait_ge(mix_lo, 4)
            four_blocks("w_o0", 2)

            def ada_reduce(group, col):
                pe.wait_ge(ada_step, group * 8 + 8)
                for q in range(4):
                    to = ps[:, ADA_BANK, col + q:col + q + 1] if isinstance(col, int) else ps[:, ADA_BANK, bass.ds(col + q, 1)]
                    ins = nc.tensor.matmul(to, scratch[:, q // 2, (q % 2) * P:(q % 2 + 1) * P], ones[:, 0:1],
                                           start=True, stop=True)
                ins.then_inc(ada_reduced, 1)

            def mlp(l):
                norm_sum_all(f"mlp{l}")
                as_chunks_arrive(f"up{l}", f"mlp{l}")
                two_bank_slot(f"up{l}", 1)
                ada_reduce(8 * l, 0)
                with pe.Fori(1, 4) as i:
                    for j in range(2):
                        two_bank_slot(f"up{l}", j, i, 2)
                    ada_reduce(i + 8 * l, i * 4)
                with pe.Fori(0, 2) as i:
                    for j in range(4):
                        s = Slot(f"down{l}", j, i, 4)
                        pe.wait_ge(hid_lo, HIDDEN_BEFORE[str(l)] + 4 * (j + 1))
                        pe.wait_ge(split_lo, s.split + 2)
                        for b in range(2):
                            if j == 0:
                                wait_acc(b, turn(f"down{l}", 0, i, 1))
                            features(s, b, [at_col((2 * b + q) * P) for q in range(2)], a_hi, a_lo, first=j == 0, last=j == 3,
                                     chunk=KD * j).then_inc(parts_done, 1)
                        if j % 2:
                            ada_reduce(i * 2 + (8 * l + 4 + j // 2), i * 8 + (16 + 4 * (j // 2)))

            mlp(0)

            norm_sum_all("attn1")
            as_chunks_arrive("swa", "attn1", [("features", (0, P)), ("features", (2 * P,))])
            for j in range(1, 4):
                s, t = Slot("swa", j), turn("swa", j)
                pe.wait_ge(split_lo, s.split + 2)

                wait_acc(0, t)
                blocks = [at_col(0), at_col(P)] if j < 3 else [at_col(P), at_col(2 * P)]
                features(s, 0, blocks, h_hi, h_lo).then_inc(parts_done, 1)
                wait_acc(1, t)
                if j < 2:
                    features(s, 1, [at_col(2 * P)], h_hi, h_lo).then_inc(parts_done, 1)
                else:
                    col = 2 * P if j == 2 else 0
                    token_rows(s, ps[:, 1, 0:P], 0, col, P, h_hi, h_lo, last=False)
                    token_rows(s, ps[:, 1, P:2 * P], 1, col, P, h_hi, h_lo, first=False).then_inc(parts_done, 1)
            for c in range(2):
                pe.wait_ge(acc_out[c], turn("swa", 3) + 1)
            heads(16, 32)
            mix_turn(1, o_rows1, 8)
            pe.wait_ge(mix_lo, 8)
            four_blocks("w_o1", 2)
            mlp(1)

            norm_sum_all("final")
            norm_sum_all("mix0")
            as_chunks_arrive("lru_in", "mix0")
            four_blocks("lru_in", 5, first=1)
            pe.wait_ge(rg_loaded, 64)
            pe.wait_ge(xr_ready, 1)
            for g in range(2):
                for c in range(4):
                    ins = nc.tensor.matmul(ps[:, 2 + 2 * g + c // 2, c % 2 * T:(c % 2 + 1) * T], rg_w[:, g, c, :], xr[:, c, :],
                                           start=c % 2 == 0, stop=c % 2 == 1, skip_group_check=True)
                    if c % 2:
                        ins.then_inc(gates, 1)
            pe.wait_ge(mix_lo, 12)
            four_blocks("lru_out", 2)

            def ffn(l):
                norm_sum_all(f"ffn{l}")
                as_chunks_arrive(f"gate_up{l}", f"ffn{l}")
                two_bank_slot(f"gate_up{l}", 1)
                if l == 0:
                    ada_reduce(16, 0)
                with pe.Fori(1, 5) as i:
                    for j in range(2):
                        two_bank_slot(f"gate_up{l}", j, i, 2)
                    if l == 0:
                        ada_reduce(i + 16, i * 4)
                two_bank_slot(f"gate_up{l}", 10)

                def down(i):
                    for j in range(2):
                        s = Slot(f"ffn_down{l}", 2 * i + j) if isinstance(i, int) else Slot(f"ffn_down{l}", j, i, 2)
                        pe.wait_ge(hid_lo, HIDDEN_BEFORE[f"ffn{l}"] + (6 if j == 0 else 11))
                        pe.wait_ge(split_lo, s.split + 2)
                        for b in range(2):
                            if j == 0:
                                wait_acc(b, i + turn(f"ffn_down{l}", 0))
                            features(s, b, [at_col(b * P)], a_hi, a_lo, first=j == 0, last=j == 1, chunk=11 * j).then_inc(parts_done, 1)

                with pe.Fori(0, 3) as i:
                    down(i)
                    if l == 0:
                        ada_reduce(i + 21, i * 4 + 20)
                down(3)

            ffn(0)
            norm_sum_all("mix1")

            def turn_qk(j):
                pe.wait_ge(qk_scaled, j + 1)
                for q in range(2):
                    if j >= 2:
                        pe.wait_ge(qk_out, 2 * (j - 2) + q + 1)
                    turn_pair(2 + 2 * (j % 2) + q, lambda ch, t: sb_rows[:, j // 2, t, (4 * (j % 2) + 2 * q + ch) * P:
                                                                         (4 * (j % 2) + 2 * q + ch + 1) * P]).then_inc(qk_turned, 1)

            as_chunks_arrive("qkv", "mix1", [("rows", 0, BANK, [(b, 0)]) for b in range(2)])
            for j in range(1, 6):
                s, t = Slot("qkv", j), turn("qkv", j)
                pe.wait_ge(split_lo, s.split + 2)
                for b in range(2):
                    wait_acc(b, t)
                    token_rows(s, ps[:, b, :], b, 0, BANK, h_hi, h_lo).then_inc(parts_done, 1)
                if 1 <= j < 5:
                    turn_qk(j - 1)
            for c in range(2):
                pe.wait_ge(acc_out[c], turn("qkv", 5) + 1)
            pe.wait_ge(qk_out, 8)
            pe.wait_ge(pool_step, 12)

            def z_head(h):
                rows_of, c = slice(h % 2 * HD, (h % 2 + 1) * HD), h // 2
                if h >= 2:
                    pe.wait_ge(u_ready, h - 1)
                z = ps[:, 2 + h % 2, :]
                nc.tensor.matmul(z[:, 0:T], sb_kT[rows_of, c, 0:P], sb_qT[rows_of, c, :], start=True, stop=False,
                                 skip_group_check=True)
                nc.tensor.matmul(z[:, T:T + P], sb_kT[rows_of, c, P:T], sb_qT[rows_of, c, P:T], start=False, stop=True,
                                 skip_group_check=True).then_inc(z_ready, 1)

            def sum_head(h):
                pe.wait_ge(sp_masked, h + 1)
                if h >= 2:
                    pe.wait_ge(logw_ready, h - 1)
                to, sp_of = ps[:, 4 + h % 2, :], sb_sp[:, h % 2, :]
                nc.tensor.matmul(to[:, 0:384], suffix[:, :], sp_of, start=True, stop=False, skip_group_check=True)
                nc.tensor.matmul(to[:, P:T], ones[:, :], sp_of[:, T:T + P], start=False, stop=True,
                                 skip_group_check=True).then_inc(sums_ready, 1)

            def sb_values(h):
                g, j = h // 4, h % 4
                pe.wait_ge(w_masked, h + 1)
                if j == 0 and g >= 2:
                    pe.wait_ge(o_copied, len(HEADS) // 4 + g - 1)
                for n, (qt, kt) in enumerate(((0, 0), (1, 0), (1, 1))):
                    ins = nc.tensor.matmul(ps[:, 6 + g % 2, qt * T + j * HD:qt * T + (j + 1) * HD],
                                           sb_u[:, h % 2, n * P:(n + 1) * P], sb_rows[:, 2, kt, h * HD:(h + 1) * HD],
                                           start=j == 0 and n == 0, stop=j == 3 and n == 2, skip_group_check=True)
                ins.then_inc(heads_done, 1)

            z_head(0)
            for h in range(SB_HEADS + 1):
                if h + 1 < SB_HEADS:
                    z_head(h + 1)
                if h < SB_HEADS:
                    sum_head(h)
                if h >= 1:
                    sb_values(h - 1)
            mix_turn(2, sb_o, 12)
            pe.wait_ge(mix_lo, 16)
            four_blocks("sb_out", 2)
            ffn(1)
            wait_source(pe, "out")
            for t in range(NT):
                for q in range(2):
                    for ch in range(4):
                        ins = nc.tensor.transpose(ps[:, 2 + 2 * t + q, ch * P:(ch + 1) * P],
                                                  xT[:, 4 * q + ch, t * P:(t + 1) * P], ident[:, :])
                    ins.then_inc(turned, 1)


_OUT = ((1, T, D), "float32")


def kernel(**inputs):
    import numpy as np
    import concourse.bacc as bacc
    from concourse.bass_utils import run_bass_kernel_spmd as run

    nc = bacc.Bacc("TRN2", target_bir_lowering=False, num_devices=1)
    arrays, args = {}, {}
    for name, value in inputs.items():
        v = np.ascontiguousarray(value)
        arrays[f"in_{name}"] = v
        args[name] = nc.dram_tensor(f"in_{name}", v.shape, mybir.dt.from_np(v.dtype), kind="ExternalInput").ap()
    out = nc.dram_tensor("out_0", _OUT[0], F32, kind="ExternalOutput").ap()
    build(nc, args, out)
    r = run(nc, [arrays], core_ids=[0])
    return r.results[0]["out_0"]
```

```python
from contextlib import ExitStack
import math

import concourse.bass as bass
from concourse import mybir

F32 = mybir.dt.float32
F32R = mybir.dt.float32r
I32 = mybir.dt.int32
ALU = mybir.AluOpType
ACT = mybir.ActivationFunctionType
AX = mybir.AxisListType

P = 128
T = 256
NT = T // P
D = 1024
KD = D // P
BANK = 512
HD = 64
EPS = 1e-6
BIG = 1e30

MLA_HEADS, QR, KVR, ROPE = 12, 384, 256, 32
QK = HD + ROPE
HALF = ROPE // 2
SWA_HEADS, SWA_GROUP = 12, 3
MEM_HEADS = 4
CROSS = MEM_HEADS * HD
FF = 4 * D
FF2 = 2816
GB = 256
SLOT = KD * BANK

STREAM = [
    ("mem", 2, 2, 2), ("w_in", 2, 2, 2), ("w_uq", 1, 3, 6), ("w_ukv", 1, 3, 6), ("w_o0", 2, 2, 2),
    ("up0", 8, 8, 2), ("down0", 8, 2, 2), ("swa", 4, 4, 2), ("w_o1", 2, 2, 2),
    ("up1", 8, 8, 2), ("down1", 8, 2, 2), ("lru_in", 5, 5, 2), ("lru_out", 2, 2, 2),
    ("gate_up0", 11, 11, 2), ("ffn_down0", 8, 4, 2), ("qkv", 6, 6, 2), ("sb_out", 2, 2, 2),
    ("gate_up1", 11, 11, 2), ("ffn_down1", 8, 4, 2),
]
FIRST_SLOT, FIRST_TURN, FIRST_PART = {}, {}, {}
_s = _t = _p = 0
for _name, _slots, _turns, _parts in STREAM:
    FIRST_SLOT[_name], FIRST_TURN[_name], FIRST_PART[_name] = _s, _t, _p
    _s, _t, _p = _s + _slots, _t + _turns, _p + _slots * _parts
NSLOTS = _s
SIX_PARTS = {FIRST_SLOT["w_uq"], FIRST_SLOT["w_ukv"]}


SHAPES = {"w_uq": (3, MLA_HEADS * QK), "w_ukv": (2, MLA_HEADS * 2 * HD), "swa": (KD, 384),
          "ffn_down0": (11, 256), "ffn_down1": (11, 256)}
SHAPE = [SHAPES.get(name, (KD, BANK)) for name, slots, _, _ in STREAM for _ in range(slots)]
SHAPE[FIRST_SLOT["w_in"] + 1] = (KD, QR + KVR + ROPE + CROSS - BANK)


def parts_through(n):
    return sum(6 if s in SIX_PARTS else 2 for s in range(n + 1))


COL_A = {"attn": 0, "mlp": 16, "mem": 32, "final": 40, "qn": 48, "kvn": 51, "mix0": 53, "ffn0": 61,
         "mix1": 69, "ffn1": 77, "lam": 85, "convb_b": 89, "rga_b": 93, "rgx_b": 97, "conv_a": 101, "c": 113}
ROWS_A = 121
COL_B = {"conv_b": 0, "ada_b0": 16, "ada_b1": 64, "gq": 112, "gk": 113}
ROWS_B = 114

NORMS = [("mem", KD), ("attn0", KD), ("qn", 3), ("kvn", 2), ("mlp0", KD), ("attn1", KD), ("mlp1", KD),
         ("final", KD), ("mix0", KD), ("ffn0", KD), ("mix1", KD), ("ffn1", KD)]
NORM_AT = {name: k for k, (name, _) in enumerate(NORMS)}


def squares(c):
    return 4 if c == KD else 1


def pairs(c):
    return [list(range(a, min(a + 2, c))) for a in range(0, c, 2)]


NORM_SQ = [sum(squares(c) for _, c in NORMS[:k]) for k in range(len(NORMS) + 1)]
SPLIT_NORMS = [c if name != "final" else 0 for name, c in NORMS]
NORM_PAIRS = [sum(len(pairs(c)) for c in SPLIT_NORMS[:k]) for k in range(len(NORMS) + 1)]

HIDDEN_BEFORE = {"0": 0, "1": 16, "ffn0": 32, "ffn1": 43}

HEADS = [("mla", 0, h) for h in range(MLA_HEADS)] + [("cross", 0, h) for h in range(MEM_HEADS)] \
    + [("swa", 1, h) for h in range(SWA_HEADS)] + [("cross", 1, h) for h in range(MEM_HEADS)]
SPLIT_AFTER = (5, 9)
SB_HEADS = 16

LRU_ORDER = (4, 1, 2, 3, 0)
LRU_PAIRS = (2, 3, 0, 1)


def build(nc, a, out):
    ctx = ExitStack()
    with ctx:
        def sb(name, shape, dt=F32):
            return ctx.enter_context(nc.sbuf_tensor(name, shape, dt))

        def sem(name):
            return ctx.enter_context(nc.semaphore(name))

        raw = sb("raw", [P, 2, SLOT])
        w_hi = sb("w_hi", [P, 2, SLOT], F32R)
        w_lo = sb("w_lo", [P, 2, SLOT], F32R)
        ada_raw = sb("ada_raw", [P, 2, 2, BANK])
        xT = sb("xT", [P, KD, T])
        h_hi = sb("h_hi", [P, KD, T], F32R)
        h_lo = sb("h_lo", [P, KD, T], F32R)
        h_full = nc.alloc_sbuf_tensor_at("h_full", [P, KD, T], F32, offset=nc.sbuf_base - 4 * KD * T)
        mem_k1 = sb("mem_k1", [P, 2, T])
        mem_v1 = sb("mem_v1", [P, 2, T])
        ident = sb("ident", [P, P])
        ones = sb("ones", [P, P])
        col_a = sb("col_a", [P, ROWS_A])
        col_b = sb("col_b", [P, ROWS_B])
        mod = sb("mod", [P, 2, 48])
        ada_cols = sb("ada_cols", [P, 96])
        modg = sb("modg", [P, 2, 2, KD])
        scratch = sb("scratch", [P, 4, T])
        negmax = sb("negmax", [P, 8, NT, 4])
        sums = sb("sums", [P, 8, NT, 4])
        rsum = sb("rsum", [P, NT, 4])
        sinkexp = sb("sinkexp", [P, NT, 4])
        sink = sb("sink", [P, SWA_HEADS])
        negsink = sb("negsink", [P, SWA_HEADS])
        posq_i = sb("posq_i", [P, NT], I32)
        posq = sb("posq", [P, NT])
        posk_i = sb("posk_i", [P, T], I32)
        silu_c = sb("silu_c", [P, KD])
        lam4 = sb("lam4", [P, 6, 4])
        gqk = sb("gqk", [P, 1])
        sb_ms = sb("sb_ms", [P, 4, NT, 8])
        arena = sb("arena", [P, 16384])
        arena_at = nc.sbuf_base - 16384 * 4

        def at(name, first, shape, dt=F32):
            return nc.alloc_sbuf_tensor_at(name, shape, dt, offset=arena_at + 4 * first)

        rows_mem = at("rows_mem", 3648, [P, NT, D])
        rows_x = at("rows_x", 5952, [P, NT, D])
        memT = at("memT", 8256, [P, KD, T])
        sq = at("sq", 10304, [P, KD, T])
        rows_a = at("rows_a", 12352, [P, P])
        rows_b = at("rows_b", 12480, [P, P])
        mem_k0 = at("mem_k0", 0, [P, 2, T])
        mem_v0 = at("mem_v0", 512, [P, 2, T])
        qx0 = at("qx0", 1024, [P, 2, T])
        krow = at("krow", 1536, [P, NT, ROPE])
        krot = at("krot", 1600, [P, NT, ROPE])
        cosT = at("cosT", 1664, [P, NT, HALF])
        sinT = at("sinT", 1696, [P, NT, HALF])
        causal = at("causal", 1728, [P, 3 * P])
        probs0 = at("probs0", 2112, [P, 3, BANK])
        probsT0 = at("probsT0", 3648, [P, 3, BANK])
        q_rows = at("q_rows", 3648, [P, NT, MLA_HEADS, QK])
        k_rows = at("k_rows", 5952, [P, NT, MLA_HEADS, QK])
        v_rows = at("v_rows", 8256, [P, NT, MLA_HEADS, HD])
        mla_qT = at("mla_qT", 9792, [P, MLA_HEADS, T])
        mla_kT = at("mla_kT", 12864, [P, MLA_HEADS, T])
        sq_c = at("sq_c", 9792, [P, 3, T])
        cq_hi = at("cq_hi", 10560, [P, 3, T], F32R)
        cq_lo = at("cq_lo", 11328, [P, 3, T], F32R)
        ckv_hi = at("ckv_hi", 12096, [P, 2, T], F32R)
        ckv_lo = at("ckv_lo", 12608, [P, 2, T], F32R)
        cqT = at("cqT", 13120, [P, 3, T])
        ckvT = at("ckvT", 13888, [P, 2, T])
        rope_tmp = at("rope_tmp", 9792, [P, 4, NT, MLA_HEADS, HALF])
        inv_freq = at("inv_freq", 15936, [P, HALF])
        angle = at("angle", 15952, [P, 5, NT * HALF])
        o_rows0 = at("o_rows0", 5952, [P, NT, D])
        a_hi = at("a_hi", 0, [P, FF // P, T], F32R)
        a_lo = at("a_lo", 8192, [P, FF // P, T], F32R)
        a_full = at("a_full", 8192, [P, FF // P, T])
        swa_qT = at("swa_qT", 0, [P, 6, T])
        swa_kT = at("swa_kT", 1536, [P, 2, T])
        swa_v = at("swa_v", 2048, [P, NT, 4 * HD])
        qx1 = at("qx1", 2560, [P, 2, T])
        probs1 = at("probs1", 3072, [P, 3, BANK])
        probsT1 = at("probsT1", 8192, [P, 3, BANK])
        dist = at("dist", 4608, [P, 3 * P])
        alibi = at("alibi", 4992, [P, 2, 384])
        swa_kT_swapped = at("swa_kT_swapped", 12352, [P, 2, T])
        o_rows1 = at("o_rows1", 5760, [P, NT, D])
        conv_in = at("conv_in", 1024, [P, 4, T + 4])
        gate_c = at("gate_c", 2064, [P, 4, T])
        gelu_r = at("gelu_r", 3088, [P, 4, T])
        rx = at("rx", 4112, [P, 4, T + 4])
        xr = at("xr", 5152, [P, 4, T])
        rg_r = at("rg_r", 6176, [P, 4, T])
        rg_i = at("rg_i", 7200, [P, 4, T])
        lru_a = at("lru_a", 8224, [P, 4, T])
        lru_b = at("lru_b", 9248, [P, 4, T])
        lru_h = at("lru_h", 12288, [P, 4, T])
        y_mix = at("y_mix", 13312, [P, 4, T])
        rg_w = at("rg_w", 14336, [P, 2, 4, P])
        sb_rows = at("sb_rows", 0, [P, 3, NT, D])
        sb_o = at("sb_o", 0, [P, NT, D])
        sb_qT = at("sb_qT", 6144, [P, KD, T])
        sb_kT = at("sb_kT", 8192, [P, KD, T])
        sb_l = at("sb_l", 10240, [P, 3, 384])
        sb_sp = at("sb_sp", 11392, [P, 3, 384])
        sb_u = at("sb_u", 12544, [P, 3, 384])
        sb_sq = at("sb_sq", 12544, [P, NT, BANK])
        suffix = at("suffix", 13696, [P, P])
        strict = at("strict", 13824, [P, P])
        o_final = at("o_final", 0, [P, NT, D])

        ps = ctx.enter_context(nc.psum_tensor("ps", [P, 8, BANK], F32))
        NORM_BANK, ADA_BANK = 6, 7
        SCORE_BANKS, TURNED_BANKS = (2, 3, 0), (4, 5, 1)

        vec_loaded, mem_loaded, x_loaded, pos_loaded = sem("vec_loaded"), sem("mem_loaded"), sem("x_loaded"), sem("pos_loaded")
        rg_loaded = sem("rg_loaded")
        raw_loaded = [sem("raw_loaded0"), sem("raw_loaded1")]
        split_hi, split_lo = sem("split_hi"), sem("split_lo")
        parts_done = sem("parts_done")
        acc_out = [sem("acc_out0"), sem("acc_out1")]
        ada_loaded = [sem("ada_loaded0"), sem("ada_loaded1")]
        ada_step, ada_reduced = sem("ada_step"), sem("ada_reduced")
        consts, dve_step, act_step, pool_step = sem("consts"), sem("dve_step"), sem("act_step"), sem("pool_step")
        turned, unturned = sem("turned"), sem("unturned")
        vec_cols, resid_ready = sem("vec_cols"), sem("resid_ready")
        norm_sq, norm_sum, norm_total = sem("norm_sq"), sem("norm_sum"), sem("norm_total")
        norm_var, norm_y, norm_h, norm_hi, norm_lo = (sem("norm_var"), sem("norm_y"), sem("norm_h"),
                                                      sem("norm_hi"), sem("norm_lo"))
        lam_log, decay_rates, gqk_ready, dist_ready = sem("lam_log"), sem("decay_rates"), sem("gqk_ready"), sem("dist_ready")
        angles, sines, tables, rope_done = sem("angles"), sem("sines"), sem("tables"), sem("rope_done")
        scores, biased, exped, probs_turned, probs_copied, heads_done, o_copied = (
            sem("scores"), sem("biased"), sem("exped"), sem("probs_turned"), sem("probs_copied"),
            sem("heads_done"), sem("o_copied"))
        alibi_ready, sink_arg, sink_exp = sem("alibi_ready"), sem("sink_arg"), sem("sink_exp")
        mix_turned, mix_full, mix_hi, mix_lo = sem("mix_turned"), sem("mix_full"), sem("mix_hi"), sem("mix_lo")
        hid_sq, hid_hi, hid_lo = sem("hid_sq"), sem("hid_hi"), sem("hid_lo")
        xr_ready, gates, gates_out, decay, tanh_done, gain_sq, gain = (
            sem("xr_ready"), sem("gates"), sem("gates_out"), sem("decay"), sem("tanh_done"), sem("gain_sq"), sem("gain"))
        qk_sq, qk_var, qk_y, qk_scaled, qk_turned, qk_out = (
            sem("qk_sq"), sem("qk_var"), sem("qk_y"), sem("qk_scaled"), sem("qk_turned"), sem("qk_out"))
        z_ready, z_soft, sp_ready, sp_masked, u_ready, sums_ready, logw_ready, w_exped, w_masked = (
            sem("z_ready"), sem("z_soft"), sem("sp_ready"), sem("sp_masked"), sem("u_ready"), sem("sums_ready"),
            sem("logw_ready"), sem("w_exped"), sem("w_masked"))
        q_out, k_out, qk_banks = sem("q_out"), sem("k_out"), sem("qk_banks")
        out_copied, stored = [sem("out_copied0"), sem("out_copied1")], sem("stored")

        block = ctx.enter_context(nc.Block())

        def rows(v, i=None):
            v = v if i is None else v[i]
            return v.rearrange("(c p) -> c p", p=P)

        def k_major(w):
            return w.rearrange("(c p) n -> p c n", p=P)

        def ring(buf, slot, kc, cols):
            return buf[:, slot, 0:kc * cols].rearrange("p (c n) -> p c n", c=kc)

        class Slot:

            def __init__(self, phase, j, i=None, step=0):
                n = FIRST_SLOT[phase] + j
                grow = (lambda per, first: first) if i is None else (lambda per, first: i * (step * per) + first)
                self.slot = n % 2
                self.first = n < 2
                self.kc, self.cols = SHAPE[n]
                self.words = self.kc * self.cols
                self.loaded = grow(16, 32 * (n // 2 + 1))
                self.split = grow(2, 2 * n)
                self.free = grow(2, 2 * n - 2)
                self.used = grow(2, parts_through(n - 2))
                self.before = grow(2, parts_through(n - 1))

        def turn(phase, j, i=None, step=0):
            return FIRST_TURN[phase] + j if i is None else i * step + (FIRST_TURN[phase] + j)

        vector_loads = []

        def load_rows(dst, src, first):
            vector_loads.append((dst[first:first + src.shape[0], 0:src.shape[1]], src))

        load_rows(rows_a, rows(a["mem_norm_g"]), COL_A["mem"])
        for key, name in (("attn", "attn_norm_g"), ("mlp", "mlp_norm_g")):
            load_rows(rows_a, a[name].rearrange("l (c p) -> (l c) p", p=P), COL_A[key])
        for key, name in (("final", "final_norm_g"), ("mix0", "l0_mix_norm_2"), ("ffn0", "l0_ffn_norm_2"),
                          ("mix1", "l1_mix_norm_2"), ("ffn1", "l1_ffn_norm_2"), ("lam", "l0_rg_lambda_2"),
                          ("convb_b", "l0_conv_b_b_2")):
            load_rows(rows_a, rows(a[name]), COL_A[key])
        for key, name in (("qn", "mla_q_norm_g"), ("kvn", "mla_kv_norm_g"), ("c", "c_2")):
            load_rows(rows_a, rows(a[name], 0), COL_A[key])
        for key, name in (("rga_b", "l0_rg_a_b_2"), ("rgx_b", "l0_rg_x_b_2")):
            load_rows(rows_a, a[name].rearrange("(c two) j -> c (two j)", two=2), COL_A[key])
        load_rows(rows_a, a["l0_conv_a_w_2"].rearrange("k (c p) -> (k c) p", p=P), COL_A["conv_a"])
        load_rows(rows_b, a["l0_conv_b_w_2"].rearrange("k (c p) -> (k c) p", p=P), COL_B["conv_b"])
        for l in range(2):
            load_rows(rows_b, rows(a[f"l{l}_ada_b_2"]), COL_B[f"ada_b{l}"])
        for key, name in (("gq", "l1_q_norm_2"), ("gk", "l1_k_norm_2")):
            for half in range(2):
                vector_loads.append((rows_b[COL_B[key]:COL_B[key] + 1, half * HD:(half + 1) * HD],
                                     a[name].rearrange("(o d) -> o d", o=1)))

        @block.sync
        def _(sp):
            def load(s, src):
                if not s.first:
                    sp.wait_ge(split_lo, s.free)
                kc = s.kc
                to, cut = ring(raw, s.slot, kc, s.cols), kc // 2
                sp.dma_start(to[:, 0:cut, :], src[:, 0:cut, :]).then_inc(raw_loaded[s.slot], 16)
                sp.dma_start(to[:, cut:kc, :], src[:, cut:kc, :]).then_inc(raw_loaded[s.slot], 16)

            sp.dma_start(rows_mem[:, :, :], a["mem"].rearrange("b (t p) d -> p (b t) d", p=P)).then_inc(mem_loaded, 16)
            for to, src in vector_loads[0::2]:
                sp.dma_start(to, src).then_inc(vec_loaded, 16)
            load(Slot("mem", 0), k_major(a["w_mem_kv"][0]))
            sp.dma_start(rows_x[:, :, :], a["x"].rearrange("b (t p) d -> p (b t) d", p=P)).then_inc(x_loaded, 16)
            load(Slot("mem", 1), k_major(a["w_mem_kv"][1]))
            load(Slot("w_in", 0), k_major(a["mla_w_in"][0])[:, :, 0:512])
            load(Slot("w_in", 1), k_major(a["mla_w_in"][0])[:, :, 512:928])
            load(Slot("w_uq", 0), k_major(a["mla_w_uq"][0]))
            load(Slot("w_ukv", 0), k_major(a["mla_w_ukv"][0]))

            def load_columns(phase, w, slots, order=None):
                for j in range(slots):
                    at_block = order[j] if order else j
                    load(Slot(phase, j), k_major(w)[:, :, at_block * BANK:(at_block + 1) * BANK])

            def load_mlp(l):
                w_up, w_down = k_major(a["mlp_w_up"][l]), k_major(a["mlp_w_down"][l])
                with sp.Fori(0, 4) as i:
                    for j in range(2):
                        load(Slot(f"up{l}", j, i, 2), w_up[:, :, bass.ds(i * (2 * BANK) + j * BANK, BANK)])
                with sp.Fori(0, 2) as i:
                    for j in range(4):
                        load(Slot(f"down{l}", j, i, 4), w_down[:, j * KD:(j + 1) * KD, bass.ds(i * BANK, BANK)])

            def load_ffn(l):
                gate, up, down = (k_major(a[f"l{l}_ffn_w_{x}_2"]) for x in ("gate", "up", "down"))

                def load_pair(s, first):
                    both = ring(raw, s.slot, KD, 2 * GB)
                    sp.wait_ge(split_lo, s.free)
                    sp.dma_start(both[:, :, 0:GB], gate[:, :, bass.ds(first, GB)]).then_inc(raw_loaded[s.slot], 16)
                    sp.dma_start(both[:, :, GB:2 * GB], up[:, :, bass.ds(first, GB)]).then_inc(raw_loaded[s.slot], 16)

                with sp.Fori(0, 5) as i:
                    for j in range(2):
                        load_pair(Slot(f"gate_up{l}", j, i, 2), i * (2 * GB) + j * GB)
                load_pair(Slot(f"gate_up{l}", 10), 10 * GB)
                with sp.Fori(0, 4) as i:
                    for j in range(2):
                        load(Slot(f"ffn_down{l}", j, i, 2), down[:, j * 11:(j + 1) * 11, bass.ds(i * 256, 256)])

            load_columns("w_o0", a["w_o"][0], 2)
            load_mlp(0)
            for j in range(4):
                load(Slot("swa", j), k_major(a["swa_w_in"][0])[:, :, j * 384:(j + 1) * 384])
            load_columns("w_o1", a["w_o"][1], 2)
            load_mlp(1)
            load_columns("lru_in", a["l0_w_in_2"], 5, order=LRU_ORDER)
            load_columns("lru_out", a["l0_w_out_2"], 2)
            load_ffn(0)
            load_columns("qkv", a["l1_w_qkv_2"], 6)
            load_columns("sb_out", a["l1_w_out_2"], 2)
            load_ffn(1)
            y = out.rearrange("b (t p) d -> p (b t) d", p=P)
            for t in range(NT):
                sp.wait_ge(out_copied[t], 2)
                sp.dma_start(y[:, t, :], o_final[:, t, :]).then_inc(stored, 16)
            sp.wait_ge(stored, 16 * NT)

        @block.gpsimd
        def _(pool):
            def step(ins, n):
                ins.then_inc(pool_step, 1)
                pool.wait_ge(pool_step, n)

            def triangle(to, fill, base, q, k, n):
                step(nc.gpsimd.affine_select(out=to, in_=to, compare_op=ALU.is_gt, fill=fill, base=base,
                                             pattern=[[k, P]], channel_multiplier=q), n)

            step(nc.gpsimd.memset(ident[:, :], 0.0), 1)
            nc.gpsimd.affine_select(out=ident[:, :], in_=ident[:, :], compare_op=ALU.not_equal, fill=1.0, base=0,
                                    pattern=[[-1, P]], channel_multiplier=1).then_inc(consts, 1)
            nc.gpsimd.memset(ones[:, :], 1.0).then_inc(consts, 1)
            step(nc.gpsimd.memset(causal[:, :], 0.0), 2)
            triangle(causal[:, 0:P], BIG, 1, 1, -1, 3)
            triangle(causal[:, 2 * P:3 * P], BIG, 1, 1, -1, 4)
            for f in range(HALF):
                last = nc.gpsimd.memset(inv_freq[:, f:f + 1], float(10000.0 ** (-(f * 2.0) / ROPE)))
            last.then_inc(consts, 1)

            ada = [k_major(a[f"l{l}_ada_w_2"]) for l in range(2)]

            def ada_load(l, slot, group, quarter, m):
                if not (isinstance(m, int) and m < 2):
                    pool.wait_ge(ada_step, m * 2 - 2)
                pool.dma_start(ada_raw[:, slot, :, :], ada[l][:, 2 * quarter:2 * quarter + 2, group])\
                    .then_inc(ada_loaded[slot], 16)

            def ada_loads(first, last):
                cut = 12 * (first // 12)
                with pool.Fori(first, last) as g:
                    for u in range(4):
                        group = g if u < 2 else g + 1
                        ada_load(first // 12, u % 2, bass.ds((group - cut) * BANK, BANK), (u + 2) % 4, g * 4 + (u + 2))

            def ada_pair(group, half):
                for u in range(2):
                    at_group = slice(group % 12 * BANK, (group % 12 + 1) * BANK)
                    ada_load(group // 12, u, at_group, 2 * half + u, 4 * group + 2 * half + u)

            ada_pair(0, 0)
            ada_loads(0, 8)

            pool.wait_ge(dist_ready, 2)
            triangle(dist[:, 0:P], BIG, 1, 1, -1, 5)
            triangle(dist[:, P:2 * P], BIG, 0, -1, 1, 6)
            triangle(dist[:, 2 * P:3 * P], BIG, 1, 1, -1, 7)
            for h in range(SWA_HEADS):
                if h >= 2:
                    pool.wait_ge(biased, MLA_HEADS + MEM_HEADS + h - 1)
                slope = 2.0 ** (-8.0 * (h + 1.0) / SWA_HEADS)
                nc.gpsimd.tensor_scalar(alibi[:, h % 2, :], dist[:, :], slope, None, ALU.mult).then_inc(alibi_ready, 1)

            ada_loads(8, 11)
            ada_pair(11, 1)
            ada_pair(12, 0)
            ada_loads(12, 16)

            pool.wait_ge(parts_done, parts_through(FIRST_SLOT["lru_in"] - 1))
            step(nc.gpsimd.memset(rg_w[:, :, :, :], 0.0), 8)
            for g, w in enumerate((a["l0_rg_a_w_2"], a["l0_rg_x_w_2"])):
                for half in range(2):
                    pool.dma_start(rg_w[half * HD:(half + 1) * HD, g, :, half * HD:(half + 1) * HD],
                                   w.rearrange("(b two) i j -> two i b j", two=2)[half]).then_inc(rg_loaded, 16)

            ada_loads(16, 23)
            ada_pair(23, 1)

            pool.wait_ge(parts_done, parts_through(FIRST_SLOT["qkv"] - 1))
            nc.gpsimd.memset(suffix[:, :], 1.0).then_inc(pool_step, 1)
            nc.gpsimd.memset(strict[:, :], 1.0).then_inc(pool_step, 1)
            pool.wait_ge(pool_step, 10)
            triangle(suffix[:, :], 0.0, 0, 1, -1, 11)
            triangle(strict[:, :], 0.0, 0, -1, 1, 12)
            def on_diagonal(buf, h):
                return buf[:, h % 3, :].rearrange("p (k q) -> p k q", k=3)[:, 0:3:2, :]

            mask = strict[:, :].unsqueeze(1).to_broadcast([P, 2, P])
            for h in range(SB_HEADS + 1):
                if h < SB_HEADS:
                    pool.wait_ge(sp_ready, h + 1)
                    nc.gpsimd.tensor_tensor(on_diagonal(sb_sp, h), on_diagonal(sb_sp, h), mask, ALU.mult)\
                        .then_inc(sp_masked, 1)
                if h >= 1:
                    pool.wait_ge(w_exped, h)
                    nc.gpsimd.tensor_tensor(on_diagonal(sb_u, h - 1), on_diagonal(sb_u, h - 1), mask, ALU.mult)\
                        .then_inc(w_masked, 1)

        def wait_count(s, b):
            return s.before + (b + 1)

        def sb_rows_out(act, g):
            act.wait_ge(heads_done, len(HEADS) + 4 * (g + 1))
            nc.scalar.activation(sb_o[:, :, 4 * g * HD:(4 * g + 4) * HD], ps[:, 6 + g % 2, :].rearrange("p (t d) -> p t d", t=NT),
                                 ACT.Copy).then_inc(o_copied, 1)

        def wait_pair(eng, name, q):
            if name == "mem":
                eng.wait_ge(unturned, q + 1)
            elif name in ("attn0", "mix0"):
                eng.wait_ge(resid_ready, (4 if name == "mix0" else 0) + q + 1)
            elif name == "mix1":
                for b in range(2):
                    eng.wait_ge(acc_out[b], turn("ffn_down0", q) + 1)
            elif name in ("qn", "kvn"):
                wait_source(eng, name)
            else:
                phase = {"mlp0": "w_o0", "attn1": "down0", "mlp1": "w_o1", "final": "down1", "ffn0": "lru_out",
                         "ffn1": "sb_out"}[name]
                eng.wait_ge(acc_out[q % 2], turn(phase, q // 2) + 1)

        def wait_source(eng, name):
            if name == "mem":
                eng.wait_ge(unturned, 4)
            elif name == "attn0":
                eng.wait_ge(resid_ready, 4)
            elif name == "mix0":
                eng.wait_ge(resid_ready, 8)
            else:
                last = {"qn": turn("w_in", 0), "kvn": turn("w_in", 1), "mlp0": turn("w_o0", 1), "attn1": turn("down0", 1),
                        "mlp1": turn("w_o1", 1), "final": turn("down1", 1), "ffn0": turn("lru_out", 1),
                        "mix1": turn("ffn_down0", 3), "ffn1": turn("sb_out", 1), "out": turn("ffn_down1", 3)}[name]
                eng.wait_ge(acc_out[0], last + 1)
                eng.wait_ge(acc_out[1], last + 1)

        def norm_io(name):
            if name == "mem":
                return memT, sq, h_hi, h_lo
            if name == "qn":
                return cqT, sq_c, cq_hi, cq_lo
            if name == "kvn":
                return ckvT, sq_c, ckv_hi, ckv_lo
            return xT, (h_full if name in ("attn1", "final", "mix1") else sq), h_hi, h_lo

        @block.scalar
        def _(act):
            steps = [0]

            def link(ins):
                steps[0] += 1
                ins.then_inc(act_step, 1)
                act.wait_ge(act_step, steps[0])

            def split(s, halves=(0, 1)):
                act.wait_ge(raw_loaded[s.slot], s.loaded)
                if not s.first:
                    act.wait_ge(parts_done, s.used)
                for half in halves:
                    cut = slice(half * s.words // 2, (half + 1) * s.words // 2)
                    nc.scalar.activation(w_hi[:, s.slot, cut], raw[:, s.slot, cut], ACT.Copy).then_inc(split_hi, 1)

            def norm(name, used=None, before_parts=None, meanwhile=None):
                k = NORM_AT[name]
                c = NORMS[k][1]
                src, squared, hi, _ = norm_io(name)
                if NORM_PAIRS[k]:
                    act.wait_ge(norm_lo, NORM_PAIRS[k])
                per = c // squares(c)
                for q in range(squares(c)):
                    wait_pair(act, name, q)
                    cut = slice(q * per, (q + 1) * per)
                    nc.scalar.activation(squared[:, cut, :], src[:, cut, :], ACT.Square).then_inc(norm_sq, 1)
                if meanwhile:
                    meanwhile()
                act.wait_ge(norm_var, k + 1)
                link(nc.scalar.activation(scratch[:, 2, :], scratch[:, 1, :], ACT.Ln))
                nc.scalar.activation(scratch[:, 2, :], scratch[:, 2, :], ACT.Exp, scale=-0.5).then_inc(norm_y, 1)
                if name == "final":
                    return
                if used is not None:
                    before_parts()
                    act.wait_ge(parts_done, used)
                for q, chunks in enumerate(pairs(c)):
                    cut = slice(chunks[0], chunks[-1] + 1)
                    act.wait_ge(norm_h, NORM_PAIRS[k] + q + 1)
                    nc.scalar.activation(hi[:, cut, :], squared[:, cut, :], ACT.Copy).then_inc(norm_hi, 1)

            def acc(b, cols=BANK):
                return ps[:, b, 0:cols]

            def wait_part(s, b):
                act.wait_ge(parts_done, wait_count(s, b))

            for load in vector_loads[1::2]:
                act.dma_start(load[0], load[1]).then_inc(vec_loaded, 16)
            act.dma_start(posk_i[:, :], a["positions"].rearrange("b t -> (b t)").partition_broadcast(P)).then_inc(pos_loaded, 16)
            for t in range(NT):
                act.dma_start(posq_i[:, t:t + 1], a["positions"][0, t * P:(t + 1) * P].rearrange("(p o) -> p o", o=1)).then_inc(pos_loaded, 16)
            act.dma_start(sink[:, :], a["swa_sinks"].rearrange("l h -> (l h)").partition_broadcast(P)).then_inc(pos_loaded, 16)

            nc.scalar.preload_act_table_set("natural_log_exp_and_others")
            norm("mem", meanwhile=lambda: split(Slot("mem", 0)))
            for b in range(4):
                act.wait_ge(turned, 6 + b)
                nc.scalar.activation(xT[:, 2 * b:2 * b + 2, :], ps[:, 2 + b, :].rearrange("p (c t) -> p c t", c=2),
                                     ACT.Copy).then_inc(resid_ready, 1)
            split(Slot("mem", 1))

            def mem_keys(l, keys):
                wait_part(Slot("mem", l), 0)
                nc.scalar.activation(keys[:, :, :], acc(0).rearrange("p (c t) -> p c t", c=2), ACT.Copy).then_inc(acc_out[0], 1)

            mem_keys(0, mem_k0)
            split(Slot("mem", 2))
            act.wait_ge(vec_cols, 2)
            link(nc.scalar.activation(lam4[:, 1, :], lam4[:, 0, :], ACT.Exp, scale=-1.0))
            nc.scalar.activation(lam4[:, 1, :], lam4[:, 1, :], ACT.Ln, bias=1.0).then_inc(lam_log, 1)
            norm("attn0", used=parts_through(1), before_parts=lambda: mem_keys(1, mem_k1))
            split(Slot("mem", 3))
            act.wait_ge(angles, 1)
            for q, to in ((1, sinT), (2, cosT)):
                nc.scalar.activation(to[:, :, :], angle[:, q, :].rearrange("p (t f) -> p t f", t=NT), ACT.Sin).then_inc(sines, 1)
            nc.scalar.activation(silu_c[:, :], col_a[:, COL_A["c"]:COL_A["c"] + KD], ACT.Silu).then_inc(sines, 1)
            nc.scalar.preload_act_table_set("natural_log_exp_and_others")

            wait_part(Slot("w_in", 0), 0)
            nc.scalar.activation(cqT[:, 0:2, :], acc(0).rearrange("p (c t) -> p c t", c=2), ACT.Copy).then_inc(acc_out[0], 1)
            norm("qn")
            split(Slot("w_in", 2))
            wait_part(Slot("w_in", 1), 0)
            nc.scalar.activation(ckvT[:, 1, :], acc(0, T), ACT.Copy)
            nc.scalar.activation(qx0[:, 0, :], ps[:, 0, T:2 * T], ACT.Copy, scale=-HD ** -0.5).then_inc(acc_out[0], 1)
            norm("kvn")
            split(Slot("w_in", 3))
            for g in range(3):
                act.wait_ge(parts_done, Slot("w_uq", 0).before + 2 * g + 1)
                nc.scalar.activation(q_rows[:, 0, 4 * g:4 * g + 4, :], acc(0, 4 * QK).rearrange("p (h d) -> p h d", h=4),
                                     ACT.Copy, scale=-QK ** -0.5).then_inc(acc_out[0], 1)
            for g in range(3):
                act.wait_ge(parts_done, Slot("w_ukv", 0).before + 2 * g + 1)
                kv = acc(0).rearrange("p (h d) -> p h d", h=4)
                nc.scalar.activation(k_rows[:, 0, 4 * g:4 * g + 4, 0:HD], kv[:, :, 0:HD], ACT.Copy)
                nc.scalar.activation(v_rows[:, 0, 4 * g:4 * g + 4, :], kv[:, :, HD:2 * HD], ACT.Copy).then_inc(acc_out[0], 1)
            for j in range(6):
                act.wait_ge(qk_banks, 2 * j + 1)
                nc.scalar.activation(mla_qT[0:QK, 2 * j:2 * j + 2, :], ps[0:QK, 2 + j % 2, :].rearrange("p (h t) -> p h t", h=2),
                                     ACT.Copy).then_inc(q_out, 1)

            def exp_head(hc):
                kind, l, h = HEADS[hc]
                g, j = hc // 4, hc % 4
                act.wait_ge(biased, hc + 1)
                p = (probs0 if l == 0 else probs1)[:, hc % 3, :]
                if kind == "cross":
                    src = ps[:, SCORE_BANKS[hc % 3], :]
                    cuts = (slice(0, T), slice(T, 2 * T))
                    if hc >= 3:
                        act.wait_ge(probs_turned, hc - 2)
                else:
                    src = p
                    cuts = (slice(0, P), slice(P, 3 * P))
                for t, cut in enumerate(cuts):
                    ins = nc.scalar.activation(p[:, cut], src[:, cut], ACT.Exp, scale=-1.0, bias=negmax[:, g, t, j:j + 1],
                                               accum_out=sums[:, g, t, j:j + 1])
                ins.then_inc(exped, 1)

            def copy_probs(hc):
                kind, l, _ = HEADS[hc]
                n, to = (4 if kind == "cross" else 3), (probsT0 if l == 0 else probsT1)
                act.wait_ge(probs_turned, hc + 1)
                if hc >= 3:
                    act.wait_ge(heads_done, hc - 2)
                nc.scalar.activation(to[:, hc % 3, 0:n * P], ps[:, TURNED_BANKS[hc % 3], 0:n * P], ACT.Copy)\
                    .then_inc(probs_copied, 1)

            def sink_sums(g):
                act.wait_ge(sink_arg, g - 3)
                nc.scalar.activation(sinkexp[:, :, :], sinkexp[:, :, :], ACT.Exp).then_inc(sink_exp, 1)

            def heads(first, last):
                for hc in range(first, last + 1):
                    if hc < last:
                        exp_head(hc)
                    if hc > first:
                        copy_probs(hc - 1)
                    if hc in SPLIT_AFTER:
                        split(Slot("w_o0", 0), (SPLIT_AFTER.index(hc),))
                    if hc % 4 == 3 and HEADS[hc][0] == "swa":
                        sink_sums(hc // 4)

            def mix_high(n):
                for q in range(4):
                    act.wait_ge(mix_turned, 4 * n + q + 1)
                    nc.scalar.activation(h_hi[:, 2 * q:2 * q + 2, :], ps[:, 2 + q, :].rearrange("p (c t) -> p c t", c=2),
                                         ACT.Copy).then_inc(mix_hi, 1)

            heads(0, 16)
            mix_high(0)
            split(Slot("w_o0", 1))
            split(Slot("w_o0", 2))

            def mlp(l):
                norm(f"mlp{l}")
                split(Slot(f"up{l}", 1))
                for j in range(8):
                    s = Slot(f"up{l}", j)
                    for b in range(2):
                        at_pair = slice(4 * j + 2 * b, 4 * j + 2 * b + 2)
                        full = a_full[:, at_pair, :]
                        wait_part(s, b)
                        nc.scalar.activation(full, acc(b).rearrange("p (c t) -> p c t", c=2), ACT.Relu).then_inc(acc_out[b], 1)
                        act.wait_ge(acc_out[b], turn(f"up{l}", j) + 1)
                        nc.scalar.activation(full, full, ACT.Square).then_inc(hid_sq, 1)
                        act.wait_ge(hid_sq, 16 * l + 2 * j + b + 1)
                        nc.scalar.activation(a_hi[:, at_pair, :], full, ACT.Copy).then_inc(hid_hi, 1)
                    split(Slot(f"up{l}", j + 2))
                for j in range(7):
                    split(Slot(f"down{l}", j + 2))

            mlp(0)

            norm("attn1")
            split(Slot("down0", 9))
            for j in range(4):
                wait_part(Slot("swa", j), 0)
                two = acc(0).rearrange("p (c t) -> p c t", c=2)
                if j < 2:
                    nc.scalar.activation(swa_qT[:, 3 * j:3 * j + 2, :], two, ACT.Copy, scale=-HD ** -0.5).then_inc(acc_out[0], 1)
                elif j == 2:
                    nc.scalar.activation(swa_kT_swapped[0:HD, :, :], two[HD:P], ACT.Copy)
                    nc.scalar.activation(swa_kT_swapped[HD:P, :, :], two[0:HD], ACT.Copy)
                    nc.scalar.activation(swa_kT[:, :, :], two, ACT.Copy).then_inc(acc_out[0], 1)
                else:
                    nc.scalar.activation(qx1[:, :, :], two, ACT.Copy, scale=-HD ** -0.5).then_inc(acc_out[0], 1)
                if j < 3:
                    split(Slot("swa", j + 2))
            heads(16, 32)
            mix_high(1)
            split(Slot("swa", 5))
            split(Slot("swa", 6))
            mlp(1)

            norm("final")
            norm("mix0")
            split(Slot("down1", 9))

            def lru_part(j, to, func=ACT.Copy):
                for b in range(2):
                    wait_part(Slot("lru_in", j), b)
                    nc.scalar.activation(to[:, 2 * b:2 * b + 2, :], acc(b).rearrange("p (c t) -> p c t", c=2), func)\
                        .then_inc(acc_out[b], 1)

            lru_part(0, rx[:, :, 3:3 + T])
            split(Slot("lru_in", 2))
            lru_part(1, gate_c)
            split(Slot("lru_in", 3))
            nc.scalar.preload_act_table(ACT.Sigmoid)
            split(Slot("lru_in", 4))
            for g, (to, bias) in enumerate(((rg_r, "rga_b"), (rg_i, "rgx_b"))):
                for c in range(4):
                    act.wait_ge(gates, 2 * g + c // 2 + 1)
                    nc.scalar.activation(to[:, c, :], ps[:, 2 + 2 * g + c // 2, (c % 2) * T:(c % 2 + 1) * T], ACT.Sigmoid,
                                         bias=col_a[:, COL_A[bias] + c:COL_A[bias] + c + 1]).then_inc(gates_out, 1)
            act.wait_ge(gates_out, 4)
            act.wait_ge(decay_rates, 2)
            for c in range(4):
                nc.scalar.activation(lru_a[:, c, :], rg_r[:, c, :], ACT.Exp, scale=lam4[:, 3, c:c + 1]).then_inc(decay, 1)
                nc.scalar.activation(lru_b[:, c, :], rg_r[:, c, :], ACT.Tanh, scale=lam4[:, 4, c:c + 1]).then_inc(tanh_done, 1)
            nc.scalar.preload_act_table(ACT.Gelu_apprx_tanh)
            lru_part(3, gelu_r, ACT.Gelu_apprx_tanh)
            act.wait_ge(gain_sq, 1)
            nc.scalar.activation(lru_b[:, :, :], lru_b[:, :, :], ACT.Sqrt).then_inc(gain, 1)
            nc.scalar.preload_act_table_set("natural_log_exp_and_others")
            split(Slot("lru_in", 5))
            act.wait_ge(parts_done, parts_through(FIRST_SLOT["lru_in"] + 4))
            for n, q in enumerate(LRU_PAIRS):
                if q < 2:
                    act.wait_ge(acc_out[q], turn("lru_in", 4) + 1)
                else:
                    act.wait_ge(mix_full, n + 1)
                src = y_mix[:, 2 * q:2 * q + 2, :] if q < 2 else lru_h[:, 2 * q - 4:2 * q - 2, :]
                nc.scalar.activation(h_hi[:, 2 * q:2 * q + 2, :], src, ACT.Copy).then_inc(mix_hi, 1)
            split(Slot("lru_out", 1))
            split(Slot("lru_out", 2))

            def ffn(l):
                norm(f"ffn{l}")
                split(Slot(f"gate_up{l}", 1))
                nc.scalar.preload_act_table(ACT.Silu)

                for j in range(11):
                    at_pair = slice(2 * j, 2 * j + 2)
                    wait_part(Slot(f"gate_up{l}", j), 0)
                    nc.scalar.activation(a_full[:, at_pair, :], acc(0).rearrange("p (c t) -> p c t", c=2), ACT.Silu).then_inc(acc_out[0], 1)
                    act.wait_ge(acc_out[1], turn(f"gate_up{l}", j) + 1)
                    nc.scalar.activation(a_hi[:, at_pair, :], a_full[:, at_pair, :], ACT.Copy).then_inc(hid_hi, 1)
                    split(Slot(f"gate_up{l}", j + 2))
                with act.Fori(0, 3) as i:
                    for j in range(2):
                        split(Slot(f"ffn_down{l}", j + 2, i, 2))
                if l == 0:
                    split(Slot("qkv", 0))
                nc.scalar.preload_act_table_set("natural_log_exp_and_others")

            ffn(0)
            norm("mix1")
            split(Slot("qkv", 1))

            def qk_rows(j):
                part, half = j // 2, j % 2
                for b in range(2):
                    if (j, b) == (5, 1):
                        soft(0)
                        soft(1)
                    wait_part(Slot("qkv", j), b)
                    nc.scalar.activation(sb_rows[:, part, b, half * BANK:(half + 1) * BANK], acc(b), ACT.Copy).then_inc(acc_out[b], 1)
                    if part < 2:
                        if j >= 1:
                            act.wait_ge(qk_var, j)
                        act.wait_ge(acc_out[b], turn("qkv", j) + 1)
                        nc.scalar.activation(sb_sq[:, b, :], sb_rows[:, part, b, half * BANK:(half + 1) * BANK], ACT.Square).then_inc(qk_sq, 1)
                if part < 2:
                    act.wait_ge(qk_var, j + 1)
                    link(nc.scalar.activation(sb_ms[:, 1, :, :], sb_ms[:, 0, :, :], ACT.Ln))
                    nc.scalar.activation(sb_ms[:, 1, :, :], sb_ms[:, 1, :, :], ACT.Exp, scale=-0.5).then_inc(qk_y, 1)

            def qk_copy(j):
                to = sb_qT if j < 2 else sb_kT
                for q in range(2):
                    act.wait_ge(qk_turned, 2 * j + q + 1)
                    c = 4 * (j % 2) + 2 * q
                    nc.scalar.activation(to[:, c:c + 2, :], ps[:, 2 + 2 * (j % 2) + q, :].rearrange("p (c t) -> p c t", c=2),
                                         ACT.Copy, scale=gqk[:, 0:1] if j < 2 else 1.0).then_inc(qk_out, 1)

            act.wait_ge(gqk_ready, 1)

            def soft(h):
                act.wait_ge(z_ready, h + 1)
                if h >= 3:
                    act.wait_ge(u_ready, h - 2)
                z = sb_l[:, h % 3, :]
                link(nc.scalar.activation(z, ps[:, SCORE_BANKS[h % 3], 0:384], ACT.Abs))
                link(nc.scalar.activation(z, z, ACT.Exp, scale=-1.0))
                nc.scalar.activation(z, z, ACT.Ln, bias=1.0).then_inc(z_soft, 1)

            for j in range(6):
                qk_rows(j)
                if j < 5:
                    split(Slot("qkv", j + 2))
                if 1 <= j < 5:
                    qk_copy(j - 1)
            for h in range(SB_HEADS + 1):
                if h + 2 < SB_HEADS:
                    soft(h + 2)
                if h >= 1:
                    act.wait_ge(logw_ready, h)
                    nc.scalar.activation(sb_u[:, (h - 1) % 3, :], sb_u[:, (h - 1) % 3, :], ACT.Exp).then_inc(w_exped, 1)
                if h >= 6 and h % 4 == 2:
                    sb_rows_out(act, (h - 6) // 4)
            sb_rows_out(act, 3)
            mix_high(2)
            split(Slot("sb_out", 1))
            split(Slot("sb_out", 2))
            ffn(1)
            for q in range(2):
                act.wait_ge(turned, 10 + q)
                nc.scalar.activation(o_final[:, 0, q * BANK:(q + 1) * BANK], ps[:, 2 + q, :], ACT.Copy).then_inc(out_copied[0], 1)

        @block.vector
        def _(dve):
            steps = [0]

            def link(ins):
                steps[0] += 1
                ins.then_inc(dve_step, 1)
                dve.wait_ge(dve_step, steps[0])

            def split(s, halves=(0, 1)):
                for half in halves:
                    cut = slice(half * s.words // 2, (half + 1) * s.words // 2)
                    dve.wait_ge(split_hi, s.split + (half + 1))
                    nc.vector.tensor_tensor(w_lo[:, s.slot, cut], raw[:, s.slot, cut], w_hi[:, s.slot, cut].bitcast(F32),
                                            ALU.subtract).then_inc(split_lo, 1)

            gains = {"mem": (col_a, "mem", 0), "attn0": (col_a, "attn", 0), "attn1": (col_a, "attn", 8),
                     "mlp0": (col_a, "mlp", 0), "mlp1": (col_a, "mlp", 8), "final": (col_a, "final", 0),
                     "qn": (col_a, "qn", 0), "kvn": (col_a, "kvn", 0)}

            def sum_squares(name, q):
                dve.wait_ge(norm_sq, NORM_SQ[NORM_AT[name]] + q + 1)
                squared = norm_io(name)[1]
                link(nc.vector.tensor_tensor(squared[:, 0:2, :], squared[:, 0:2, :], squared[:, 2 * q:2 * q + 2, :], ALU.add))

            def norm(name, used=None, summed=False, before_low=None, meanwhile=None):
                k = NORM_AT[name]
                c = NORMS[k][1]
                src, squared, hi, lo = norm_io(name)
                total, var, y, r = (scratch[:, q, :] for q in range(4))
                if c == KD:
                    for q in (3,) if summed else (1, 2, 3):
                        sum_squares(name, q)
                else:
                    dve.wait_ge(norm_sq, NORM_SQ[k + 1])
                if c == 3:
                    link(nc.vector.tensor_tensor(squared[:, 0, :], squared[:, 0, :], squared[:, 2, :], ALU.add))
                nc.vector.tensor_tensor(total, squared[:, 0, :], squared[:, 1, :], ALU.add).then_inc(norm_sum, 1)
                dve.wait_ge(norm_total, k + 1)
                nc.vector.tensor_scalar(var, ps[:, NORM_BANK, 0:T], 1.0 / (c * P), EPS, ALU.mult, ALU.add).then_inc(norm_var, 1)
                if meanwhile:
                    meanwhile()
                dve.wait_ge(norm_y, k + 1)
                link(nc.vector.tensor_tensor(r, y, y, ALU.mult))
                link(nc.vector.scalar_tensor_tensor(r, r, -0.5, var, ALU.mult, ALU.mult))
                link(nc.vector.scalar_tensor_tensor(r, r, 1.5, y, ALU.add, ALU.mult))
                wait_source(dve, name)
                shift = None
                if name in gains:
                    cols, key, first = gains[name]
                    gain_of = lambda ch: cols[:, COL_A[key] + first + ch:COL_A[key] + first + ch + 1]
                else:
                    l, which = int(name[-1]), 0 if name.startswith("mix") else 1
                    gain_of = lambda ch: modg[:, l, which, ch:ch + 1]
                    shift = lambda ch: mod[:, l, 24 * which + ch:24 * which + ch + 1]

                def low(q):
                    cut = slice(pairs(c)[q][0], pairs(c)[q][-1] + 1)
                    dve.wait_ge(norm_hi, NORM_PAIRS[k] + q + 1)
                    nc.vector.tensor_tensor(lo[:, cut, :], squared[:, cut, :], hi[:, cut, :].bitcast(F32),
                                            ALU.subtract).then_inc(norm_lo, 1)

                for q, chunks in enumerate(pairs(c)):
                    to = src if name == "final" else squared
                    for ch in chunks:
                        ins = nc.vector.scalar_tensor_tensor(to[:, ch, :], src[:, ch, :], gain_of(ch), r, ALU.mult, ALU.mult)
                    if shift is not None:
                        link(ins)
                        for ch in chunks:
                            ins = nc.vector.tensor_scalar(to[:, ch, :], to[:, ch, :], shift(ch), None, ALU.add)
                    ins.then_inc(resid_ready if name == "final" else norm_h, 1)
                    if used is not None and q == 1:
                        before_low()
                        dve.wait_ge(parts_done, used)
                    if q >= 1 and name != "final":
                        low(q - 1)
                if name != "final":
                    low(len(pairs(c)) - 1)

            def wait_part(s, b):
                dve.wait_ge(parts_done, wait_count(s, b))

            def two(bank):
                return ps[:, bank, :].rearrange("p (c t) -> p c t", c=2)

            def sum_before(following, j, b):
                if (j, b) == (1, 0) and following:
                    sum_squares(following, 1)
                    sum_squares(following, 2)

            def add_to_residual(phase, j, following=None):
                for b in range(2):
                    s = Slot(phase, j if phase.startswith("w_o") else 4 * j + 3)
                    wait_part(s, b)
                    x = xT[:, 4 * j + 2 * b:4 * j + 2 * b + 2, :]
                    nc.vector.tensor_tensor(x, x, two(b), ALU.add).then_inc(acc_out[b], 1)
                    sum_before(following, j, b)

            def add_gated(phase, j, l, following=None):
                for b in range(2):
                    wait_part(Slot(phase, j), b)
                    for ch in range(2):
                        x = xT[:, 4 * j + 2 * b + ch, :]
                        g = 16 + 4 * j + 2 * b + ch
                        ins = nc.vector.scalar_tensor_tensor(x, ps[:, b, ch * T:(ch + 1) * T], mod[:, l, g:g + 1], x,
                                                             ALU.mult, ALU.add)
                    ins.then_inc(acc_out[b], 1)
                    sum_before(following, j, b)

            for q in range(4):
                dve.wait_ge(turned, 1 + q)
                nc.vector.tensor_copy(memT[:, 2 * q:2 * q + 2, :], two(2 + q)).then_inc(unturned, 1)
            dve.wait_ge(turned, 5)
            nc.vector.tensor_copy(col_a[:, :], ps[:, ADA_BANK, 0:ROWS_A]).then_inc(unturned, 1)
            nc.vector.tensor_copy(col_b[:, :], ps[:, ADA_BANK, T:T + ROWS_B]).then_inc(unturned, 1)
            dve.wait_ge(unturned, 6)
            lam = col_a[:, COL_A["lam"]:COL_A["lam"] + 4]
            nc.vector.scalar_tensor_tensor(lam4[:, 0, :], lam, -1.0, lam, ALU.mult, ALU.max).then_inc(vec_cols, 1)
            nc.vector.tensor_scalar(lam4[:, 2, :], lam, -1.0, 0.0, ALU.mult, ALU.max).then_inc(vec_cols, 1)
            gq, gk = (col_b[:, COL_B[x]:COL_B[x] + 1] for x in ("gq", "gk"))
            nc.vector.scalar_tensor_tensor(gqk[:, :], gq, HD ** -0.5, gk, ALU.mult, ALU.mult).then_inc(gqk_ready, 1)
            norm("mem", meanwhile=lambda: split(Slot("mem", 0)))
            split(Slot("mem", 1))

            dve.wait_ge(pos_loaded, 64)
            dve.wait_ge(consts, 3)
            link(nc.vector.tensor_copy(posq[:, :], posq_i[:, :]))
            nc.vector.tensor_scalar(negsink[:, :], sink[:, :], -1.0, None, ALU.mult)
            for t in range(NT):
                ins = nc.vector.tensor_scalar(angle[:, 0, t * HALF:(t + 1) * HALF], inv_freq[:, :], posq[:, t:t + 1], None, ALU.mult)
            link(ins)
            ang, arg, cos_arg, turns, _ = (angle[:, q, :] for q in range(5))
            link(nc.vector.tensor_scalar(turns, ang, 1.0 / (2.0 * math.pi), 1.5 * 2.0 ** 23, ALU.mult, ALU.add))
            link(nc.vector.tensor_scalar(turns, turns, -1.5 * 2.0 ** 23, None, ALU.add))
            first, second = 6.28125, 0.0019350051879882812
            link(nc.vector.scalar_tensor_tensor(arg, turns, -first, ang, ALU.mult, ALU.add))
            link(nc.vector.scalar_tensor_tensor(arg, turns, -second, arg, ALU.mult, ALU.add))
            link(nc.vector.scalar_tensor_tensor(arg, turns, -(2.0 * math.pi - first - second), arg, ALU.mult, ALU.add))
            link(nc.vector.tensor_scalar(arg, arg, 3.1415925, -3.1415925, ALU.min, ALU.max))
            link(nc.vector.scalar_tensor_tensor(cos_arg, arg, -1.0, arg, ALU.mult, ALU.max))
            nc.vector.tensor_scalar(cos_arg, cos_arg, -1.0, math.pi / 2.0, ALU.mult, ALU.add).then_inc(angles, 1)

            def mem_values(l, values):
                wait_part(Slot("mem", l), 1)
                nc.vector.tensor_copy(values[:, :, :], two(1)).then_inc(acc_out[1], 1)

            mem_values(0, mem_v0)
            split(Slot("mem", 2))
            dve.wait_ge(lam_log, 1)
            link(nc.vector.tensor_tensor(lam4[:, 5, :], lam4[:, 2, :], lam4[:, 1, :], ALU.add))
            for to, factor in ((3, -8.0), (4, 8.0)):
                nc.vector.tensor_scalar(lam4[:, to, :], lam4[:, 5, :], factor, None, ALU.mult).then_inc(decay_rates, 1)
            norm("attn0", used=parts_through(1), before_low=lambda: mem_values(1, mem_v1))
            split(Slot("mem", 3))

            wait_part(Slot("w_in", 0), 1)
            nc.vector.tensor_copy(cqT[:, 2, :], ps[:, 1, 0:T])
            nc.vector.tensor_copy(ckvT[:, 0, :], ps[:, 1, T:2 * T]).then_inc(acc_out[1], 1)
            norm("qn")
            split(Slot("w_in", 2))
            wait_part(Slot("w_in", 1), 1)
            nc.vector.tensor_scalar(qx0[:, 1, :], ps[:, 1, 0:T], -HD ** -0.5, None, ALU.mult)
            nc.vector.tensor_copy(krow[:, :, :], ps[:, 1, T:T + NT * ROPE].rearrange("p (t r) -> p t r", t=NT)).then_inc(acc_out[1], 1)
            norm("kvn")
            split(Slot("w_in", 3))
            for g in range(3):
                dve.wait_ge(parts_done, Slot("w_uq", 0).before + 2 * g + 2)
                nc.vector.tensor_scalar(q_rows[:, 1, 4 * g:4 * g + 4, :], ps[:, 1, 0:4 * QK].rearrange("p (h d) -> p h d", h=4),
                                        -QK ** -0.5, None, ALU.mult).then_inc(acc_out[1], 1)

            def rope(src, to, heads):
                c, sn = (x[:, :, :].unsqueeze(2).to_broadcast([P, NT, heads, HALF]) for x in (cosT, sinT))
                x1, x2 = src[:, :, :, 0:HALF], src[:, :, :, HALF:ROPE]
                t = [rope_tmp[:, q, :, 0:heads, :] for q in range(4)]
                for q, (x, trig) in enumerate(((x1, c), (x2, sn), (x1, sn), (x2, c))):
                    ins = nc.vector.tensor_tensor(t[q], x, trig, ALU.mult)
                link(ins)
                nc.vector.tensor_tensor(to[:, :, :, 0:HALF], t[0], t[1], ALU.subtract)
                link(nc.vector.tensor_tensor(to[:, :, :, HALF:ROPE], t[2], t[3], ALU.add))

            for g in range(3):
                dve.wait_ge(parts_done, Slot("w_ukv", 0).before + 2 * g + 2)
                kv = ps[:, 1, :].rearrange("p (h d) -> p h d", h=4)
                nc.vector.tensor_copy(k_rows[:, 1, 4 * g:4 * g + 4, 0:HD], kv[:, :, 0:HD])
                nc.vector.tensor_copy(v_rows[:, 1, 4 * g:4 * g + 4, :], kv[:, :, HD:2 * HD]).then_inc(acc_out[1], 1)
                if g == 0:
                    dve.wait_ge(sines, 3)
                    dve.wait_ge(acc_out[1], turn("w_uq", 2) + 1)
                    rope(krow[:, :, :].unsqueeze(2), krot[:, :, :].unsqueeze(2), 1)
                    dve.wait_ge(acc_out[0], turn("w_uq", 2) + 1)
                    rope(q_rows[:, :, :, HD:QK], q_rows[:, :, :, HD:QK], MLA_HEADS)
            nc.vector.tensor_copy(k_rows[:, :, :, HD:QK],
                                  krot[:, :, :].unsqueeze(2).to_broadcast([P, NT, MLA_HEADS, ROPE])).then_inc(rope_done, 1)
            for j in range(6):
                dve.wait_ge(qk_banks, 2 * j + 2)
                nc.vector.tensor_copy(mla_kT[0:QK, 2 * j:2 * j + 2, :],
                                      ps[0:QK, 4 + j % 2, :].rearrange("p (h t) -> p h t", h=2)).then_inc(k_out, 1)

            def bias_head(hc):
                kind, l, h = HEADS[hc]
                g, j, bank = hc // 4, hc % 4, SCORE_BANKS[hc % 3]
                dve.wait_ge(scores, hc + 1)
                if hc >= 3:
                    dve.wait_ge(probs_turned, hc - 2)
                if kind == "cross":
                    nc.vector.tensor_reduce(negmax[:, g, :, j], two(bank), AX.X, ALU.min).then_inc(biased, 1)
                    return
                p = (probs0 if kind == "mla" else probs1)[:, hc % 3, :]
                if kind == "swa":
                    dve.wait_ge(alibi_ready, h + 1)
                bias = causal[:, :] if kind == "mla" else alibi[:, h % 2, :]
                start = 3.0e38 if kind == "mla" else negsink[:, h:h + 1]
                for t, cut in enumerate((slice(0, P), slice(P, 3 * P))):
                    ins = nc.vector.tensor_tensor_reduce(p[:, cut], ps[:, bank, cut], bias[:, cut], 1.0, start, ALU.add,
                                                         ALU.min, negmax[:, g, t, j:j + 1])
                ins.then_inc(biased, 1)

            def group_out(g, rows_to, first):
                dve.wait_ge(exped, 4 * g + 4)
                if HEADS[4 * g][0] == "swa":
                    dve.wait_ge(sink_exp, g - 3)
                    link(nc.vector.tensor_tensor(sums[:, g, :, :], sums[:, g, :, :], sinkexp[:, :, :], ALU.add))
                link(nc.vector.reciprocal(rsum[:, :, :], sums[:, g, :, :]))
                dve.wait_ge(heads_done, 4 * g + 4)
                nc.vector.tensor_tensor(rows_to[:, :, first:first + 4 * HD].rearrange("p t (h d) -> p t h d", h=4),
                                        ps[:, 6 + g % 2, :].rearrange("p (t h d) -> p t h d", t=NT, h=4),
                                        rsum[:, :, :].unsqueeze(3).to_broadcast([P, NT, 4, HD]), ALU.mult).then_inc(o_copied, 1)
                dve.wait_ge(o_copied, g + 1)

            def heads(first, last, rows_to):
                for hc in range(first, last + 2):
                    if hc < last:
                        bias_head(hc)
                        if hc - 1 in SPLIT_AFTER:
                            split(Slot("w_o0", 0), (SPLIT_AFTER.index(hc - 1),))
                        if hc % 4 == 3 and HEADS[hc][0] == "swa":
                            g = hc // 4
                            h = 4 * (g - 4)
                            dve.wait_ge(biased, hc + 1)
                            nc.vector.tensor_tensor(sinkexp[:, :, :], negmax[:, g, :, :],
                                                    sink[:, h:h + 4].unsqueeze(1).to_broadcast([P, NT, 4]), ALU.add)\
                                .then_inc(sink_arg, 1)
                    if hc >= first + 5 and (hc - 1) % 4 == 0:
                        group_out((hc - 5) // 4, rows_to, (hc - 5 - first) * HD)

            def mix_low(n, sources, order=range(4)):
                for m, q in enumerate(order):
                    dve.wait_ge(mix_hi, 4 * n + m + 1)
                    nc.vector.tensor_tensor(h_lo[:, 2 * q:2 * q + 2, :], sources[q], h_hi[:, 2 * q:2 * q + 2, :].bitcast(F32),
                                            ALU.subtract).then_inc(mix_lo, 1)

            heads(0, 16, o_rows0)
            mix_low(0, [two(2 + q) for q in range(4)])
            split(Slot("w_o0", 1))
            add_to_residual("w_o0", 0)
            split(Slot("w_o0", 2))
            add_to_residual("w_o0", 1, following="mlp0")

            ada_sum = scratch[:, 0:2, :].rearrange("p c t -> p (c t)")

            def ada_unit(m, slot, quarter, loads):
                dve.wait_ge(ada_loaded[slot], loads)
                for q in range(2):
                    w, c = ada_raw[:, slot, q, :], silu_c[:, 2 * quarter + q:2 * quarter + q + 1]
                    if quarter == 0 and q == 0:
                        ins = nc.vector.tensor_scalar(ada_sum, w, c, None, ALU.mult)
                    else:
                        dve.wait_ge(ada_step, m * 2 + q)
                        ins = nc.vector.scalar_tensor_tensor(ada_sum, w, c, ada_sum, ALU.mult, ALU.add)
                    ins.then_inc(ada_step, 1)

            def ada_units(slot_no, j, i=None):
                grow = (lambda per, first: first) if i is None else (lambda per, first: i * per + first)
                if j % 2 == 0 and (i is not None or slot_no):
                    dve.wait_ge(ada_reduced, grow(1, slot_no // 2))
                for u in range(2):
                    ada_unit(grow(4, 2 * slot_no + u), u, 2 * (j % 2) + u, grow(32, 16 * (slot_no + 1)))

            def ada_group_done(group):
                dve.wait_ge(ada_reduced, group)

            def ada_keep(third):
                link(nc.vector.tensor_copy(ada_cols[:, 32 * third:32 * (third + 1)], ps[:, ADA_BANK, 0:32]))

            def modulation(l):
                c = COL_B[f"ada_b{l}"]
                link(nc.vector.tensor_tensor(mod[:, l, :], ada_cols[:, 48 * l:48 * (l + 1)], col_b[:, c:c + 48], ALU.add))
                for q, key in enumerate((f"mix{l}", f"ffn{l}")):
                    ins = nc.vector.scalar_tensor_tensor(modg[:, l, q, :], mod[:, l, 8 + 24 * q:16 + 24 * q], 1.0,
                                                         col_a[:, COL_A[key]:COL_A[key] + KD], ALU.add, ALU.mult)
                link(ins)

            def mlp(l):
                norm(f"mlp{l}", summed=True)
                split(Slot(f"up{l}", 1))

                def hidden(i):
                    grow = (lambda per, first: first) if i is None else (lambda per, first: i * per + first)
                    for j in range(2):
                        for b in range(2):
                            at_pair = slice(4 * j + 2 * b, 4 * j + 2 * b + 2) if i is None else bass.ds(i * 8 + (4 * j + 2 * b), 2)
                            dve.wait_ge(hid_hi, grow(4, HIDDEN_BEFORE[str(l)] + 2 * j + b + 1))
                            nc.vector.tensor_tensor(a_lo[:, at_pair, :], a_full[:, at_pair, :],
                                                    a_hi[:, at_pair, :].bitcast(F32), ALU.subtract).then_inc(hid_lo, 1)
                            if b == 0:
                                ada_units(16 * l + j, j, i)
                        split(Slot(f"up{l}", j + 2, i, 2))

                hidden(None)
                with dve.Fori(1, 4) as i:
                    hidden(i)
                for j in range(8):
                    ada_units(16 * l + 8 + j, j)
                    if j % 4 == 3:
                        add_to_residual(f"down{l}", j // 4, following=("attn1", "final")[l])
                    if j < 7:
                        split(Slot(f"down{l}", j + 2))
                ada_group_done(8 * (l + 1))

            mlp(0)

            norm("attn1", summed=True)
            ada_keep(0)
            nc.vector.tensor_scalar(dist[:, 0:P], posk_i[:, 0:P], -1.0, posq[:, 0:1], ALU.mult, ALU.add).then_inc(dist_ready, 1)
            nc.vector.tensor_scalar(dist[:, P:3 * P], posk_i[:, :], -1.0, posq[:, 1:2], ALU.mult, ALU.add).then_inc(dist_ready, 1)
            split(Slot("down0", 9))
            for j in range(4):
                wait_part(Slot("swa", j), 1)
                if j < 2:
                    nc.vector.tensor_scalar(swa_qT[:, 3 * j + 2, :], ps[:, 1, 0:T], -HD ** -0.5, None, ALU.mult).then_inc(acc_out[1], 1)
                else:
                    nc.vector.tensor_copy(swa_v[:, :, (j - 2) * P:(j - 1) * P],
                                          ps[:, 1, 0:NT * P].rearrange("p (t d) -> p t d", t=NT)).then_inc(acc_out[1], 1)
                if j < 3:
                    split(Slot("swa", j + 2))
            heads(16, 32, o_rows1)
            mix_low(1, [two(2 + q) for q in range(4)])
            split(Slot("swa", 5))
            add_to_residual("w_o1", 0)
            split(Slot("swa", 6))
            add_to_residual("w_o1", 1, following="mlp1")
            mlp(1)

            norm("final", summed=True)
            ada_keep(1)
            modulation(0)
            norm("mix0")
            split(Slot("down1", 9))
            link(nc.vector.memset(conv_in[:, :, 0:2], 0.0))
            link(nc.vector.memset(rx[:, :, 0:3], 0.0))
            def conv(to, src, taps, cols, key, bias=None, signal=None):
                for k in range(taps):
                    for c in range(4):
                        w = cols[:, key + 4 * k + c:key + 4 * k + c + 1]
                        if k == 0 and bias is None:
                            ins = nc.vector.tensor_scalar(to[:, c, :], src[:, c, 0:T], w, None, ALU.mult)
                        elif k == 0:
                            ins = nc.vector.tensor_scalar(to[:, c, :], src[:, c, 0:T], w, bias(c), ALU.mult, ALU.add)
                        else:
                            ins = nc.vector.scalar_tensor_tensor(to[:, c, :], src[:, c, k:k + T], w, to[:, c, :], ALU.mult, ALU.add)
                    if k < taps - 1 or signal is None:
                        link(ins)
                if signal is not None:
                    ins.then_inc(signal, 1)

            for b in range(2):
                dve.wait_ge(acc_out[b], turn("lru_in", 0) + 1)
            cb = COL_A["convb_b"]
            split(Slot("lru_in", 2))
            conv(xr, rx, 4, col_b, COL_B["conv_b"], lambda c: col_a[:, cb + c:cb + c + 1], signal=xr_ready)
            split(Slot("lru_in", 3))
            for b in range(2):
                wait_part(Slot("lru_in", 2), b)
                cut = slice(2 * b, 2 * b + 2)
                dve.wait_ge(acc_out[b], turn("lru_in", 1) + 1)
                nc.vector.tensor_tensor(conv_in[:, cut, 2:2 + T], gate_c[:, cut, :], two(b), ALU.mult).then_inc(acc_out[b], 1)
                dve.wait_ge(acc_out[b], turn("lru_in", 2) + 1)
            split(Slot("lru_in", 4))
            conv(y_mix, conv_in, 3, col_a, COL_A["conv_a"])
            dve.wait_ge(xr_ready, 1)
            dve.wait_ge(gates_out, 8)
            link(nc.vector.tensor_tensor(rg_i[:, :, :], rg_i[:, :, :], xr[:, :, :], ALU.mult))
            dve.wait_ge(decay, 4)
            dve.wait_ge(tanh_done, 4)
            link(nc.vector.tensor_tensor(rg_r[:, :, :], lru_a[:, :, :], lru_a[:, :, :], ALU.mult))
            nc.vector.scalar_tensor_tensor(lru_b[:, :, :], rg_r[:, :, :], 1.0, lru_b[:, :, :], ALU.add, ALU.mult).then_inc(gain_sq, 1)
            dve.wait_ge(gain, 1)
            link(nc.vector.tensor_tensor(lru_b[:, :, :], lru_b[:, :, :], rg_i[:, :, :], ALU.mult))
            for c in range(4):
                ins = nc.vector.tensor_tensor_scan(lru_h[:, c, :], lru_a[:, c, :], lru_b[:, c, :], 0.0, ALU.mult, ALU.add)
            link(ins)
            dve.wait_ge(acc_out[0], turn("lru_in", 3) + 1)
            dve.wait_ge(acc_out[1], turn("lru_in", 3) + 1)
            for q in range(2):
                cut = slice(2 * q, 2 * q + 2)
                nc.vector.tensor_tensor(lru_h[:, cut, :], lru_h[:, cut, :], gelu_r[:, cut, :], ALU.mult).then_inc(mix_full, 1)
            split(Slot("lru_in", 5))
            for q in range(2):
                wait_part(Slot("lru_in", 4), q)
                cut = slice(2 * q, 2 * q + 2)
                nc.vector.tensor_tensor(y_mix[:, cut, :], y_mix[:, cut, :], two(q), ALU.mult).then_inc(acc_out[q], 1)
            mix_low(2, [y_mix[:, 0:2, :], y_mix[:, 2:4, :], lru_h[:, 0:2, :], lru_h[:, 2:4, :]], LRU_PAIRS)
            split(Slot("lru_out", 1))
            add_gated("lru_out", 0, 0)
            split(Slot("lru_out", 2))
            add_gated("lru_out", 1, 0, following="ffn0")

            def ffn(l):
                norm(f"ffn{l}", summed=True)
                split(Slot(f"gate_up{l}", 1))

                def hidden(j, i=None):
                    s, ahead = Slot(f"gate_up{l}", j, i, 2), Slot(f"gate_up{l}", j + 2, i, 2)
                    at_pair = bass.ds(i * 4 + 2 * j, 2) if i is not None else slice(2 * j, 2 * j + 2)
                    grow = (lambda first: first) if i is None else (lambda first: i * 2 + first)
                    full = a_full[:, at_pair, :]
                    if l == 0 and j < 10:
                        ada_units(32 + j, j, i)
                    dve.wait_ge(parts_done, s.before + 2)
                    dve.wait_ge(acc_out[0], grow(turn(f"gate_up{l}", j) + 1))
                    nc.vector.tensor_tensor(full, full, two(1), ALU.mult).then_inc(acc_out[1], 1)
                    dve.wait_ge(hid_hi, grow(HIDDEN_BEFORE[f"ffn{l}"] + j + 1))
                    nc.vector.tensor_tensor(a_lo[:, at_pair, :], full, a_hi[:, at_pair, :].bitcast(F32),
                                            ALU.subtract).then_inc(hid_lo, 1)
                    split(ahead)

                def add(i):
                    for b in range(2):
                        dve.wait_ge(parts_done, i * 4 + (Slot(f"ffn_down{l}", 1).before + b + 1))
                        if isinstance(i, int):
                            x, g = xT[:, 2 * i + b, :], mod[:, l, 40 + 2 * i + b:41 + 2 * i + b]
                        else:
                            x, g = xT[:, bass.ds(i * 2 + b, 1), :], mod[:, l, bass.ds(i * 2 + (40 + b), 1)]
                        y = ps[:, b, 0:T] if isinstance(i, int) else ps[:, b, 0:T].unsqueeze(1)
                        nc.vector.scalar_tensor_tensor(x, y, g, x, ALU.mult, ALU.add).then_inc(acc_out[b], 1)

                with dve.Fori(0, 4) as i:
                    for j in range(2):
                        hidden(j, i)
                for j in (8, 9, 10):
                    hidden(j)
                with dve.Fori(0, 3) as i:
                    if l == 0:
                        ada_units(42, 0, i)
                    split(Slot(f"ffn_down{l}", 2, i, 2))
                    if l == 0:
                        ada_units(43, 1, i)
                    add(i)
                    split(Slot(f"ffn_down{l}", 3, i, 2))
                if l == 0:
                    ada_group_done(24)
                    ada_keep(2)
                    modulation(1)
                if l == 0:
                    split(Slot("qkv", 0))
                    sum_squares("mix1", 1)
                    sum_squares("mix1", 2)
                add(3)

            ffn(0)
            norm("mix1", summed=True)
            split(Slot("qkv", 1))

            for j in range(6):
                if j < 4:
                    part, half = j // 2, j % 2
                    for b in range(2):
                        dve.wait_ge(qk_sq, 2 * j + b + 1)
                        ins = nc.vector.tensor_reduce(sb_ms[:, 0, b, :], sb_sq[:, b, :].rearrange("p (h d) -> p h d", h=8),
                                                      AX.X, ALU.add)
                    link(ins)
                    ms, y, t, r = (sb_ms[:, q, :, :] for q in (0, 1, 2, 3))
                    nc.vector.tensor_scalar(ms, ms, 1.0 / HD, EPS, ALU.mult, ALU.add).then_inc(qk_var, 1)
                    dve.wait_ge(qk_y, j + 1)
                    link(nc.vector.tensor_tensor(t, y, y, ALU.mult))
                    link(nc.vector.scalar_tensor_tensor(t, t, -0.5, ms, ALU.mult, ALU.mult))
                    link(nc.vector.scalar_tensor_tensor(r, t, 1.5, y, ALU.add, ALU.mult))
                    for b in range(2):
                        x = sb_rows[:, part, b, half * BANK:(half + 1) * BANK].rearrange("p (h d) -> p h d", h=8)
                        ins = nc.vector.tensor_tensor(x, x, sb_ms[:, 3, b, :].unsqueeze(2).to_broadcast([P, 8, HD]), ALU.mult)
                    ins.then_inc(qk_scaled, 1)
                    dve.wait_ge(qk_scaled, j + 1)
                if j < 5:
                    split(Slot("qkv", j + 2))
            for h in range(SB_HEADS + 1):
                if h < SB_HEADS:
                    b = h % 3
                    z, soft = ps[:, SCORE_BANKS[b], 0:384], sb_l[:, b, :]
                    dve.wait_ge(z_soft, h + 1)
                    if h >= 3:
                        dve.wait_ge(sums_ready, h - 2)
                        dve.wait_ge(heads_done, len(HEADS) + h - 2)
                    nc.vector.scalar_tensor_tensor(sb_sp[:, b, :], z, 0.0, soft, ALU.max, ALU.add).then_inc(sp_ready, 1)
                    nc.vector.scalar_tensor_tensor(sb_u[:, b, :], z, 0.0, soft, ALU.min, ALU.subtract).then_inc(u_ready, 1)
                if h >= 1:
                    b = (h - 1) % 3
                    dve.wait_ge(sums_ready, h)
                    dve.wait_ge(u_ready, h)
                    nc.vector.tensor_tensor(sb_u[:, b, :], sb_u[:, b, :], ps[:, TURNED_BANKS[b], 0:384], ALU.subtract)\
                        .then_inc(logw_ready, 1)
            mix_low(3, [two(2 + q) for q in range(4)])
            split(Slot("sb_out", 1))
            add_gated("sb_out", 0, 1)
            split(Slot("sb_out", 2))
            add_gated("sb_out", 1, 1, following="ffn1")
            ffn(1)
            for q in range(2):
                dve.wait_ge(turned, 12 + q)
                nc.vector.tensor_copy(o_final[:, 1, q * BANK:(q + 1) * BANK], ps[:, 4 + q, :]).then_inc(out_copied[1], 1)

        @block.tensor
        def _(pe):
            def product(to, sh, sl, mh, ml, first, last):
                nc.tensor.matmul(to, sh, mh, start=first, stop=False, skip_group_check=True)
                nc.tensor.matmul(to, sh, ml, start=False, stop=False, skip_group_check=True)
                return nc.tensor.matmul(to, sl, mh, start=False, stop=last, skip_group_check=True)

            def begin(s):
                pe.wait_ge(split_lo, s.split + 2)
                return ring(w_hi, s.slot, s.kc, s.cols), ring(w_lo, s.slot, s.kc, s.cols)

            def features(s, b, blocks, hi, lo, first=True, last=True, chunk=0):
                wh, wl = ring(w_hi, s.slot, s.kc, s.cols), ring(w_lo, s.slot, s.kc, s.cols)
                for q, block_of in enumerate(blocks):
                    for c in range(s.kc):
                        ins = product(ps[:, b, q * T:(q + 1) * T], block_of(wh, c), block_of(wl, c),
                                      hi[:, chunk + c, :], lo[:, chunk + c, :],
                                      first and q == 0 and c == 0, last and q == len(blocks) - 1 and c == s.kc - 1)
                return ins

            def token_rows(s, to, t, col, n, hi, lo, first=True, last=True):
                wh, wl = ring(w_hi, s.slot, s.kc, s.cols), ring(w_lo, s.slot, s.kc, s.cols)
                cut = slice(t * P, (t + 1) * P)
                for c in range(s.kc):
                    ins = product(to, hi[:, c, cut], lo[:, c, cut], wh[:, c, col:col + n], wl[:, c, col:col + n],
                                  first and c == 0, last and c == s.kc - 1)
                return ins

            def at_col(col):
                return lambda w, c: w[:, c, col:col + P]

            def wait_acc(b, t):
                pe.wait_ge(acc_out[b], t)

            def norm_sum_all(name):
                k = NORM_AT[name]
                pe.wait_ge(norm_sum, k + 1)
                nc.tensor.matmul(ps[:, NORM_BANK, 0:T], ones[:, :], scratch[:, 0, :], start=True, stop=True).then_inc(norm_total, 1)

            def wait_norm(name):
                pe.wait_ge(norm_lo, NORM_PAIRS[NORM_AT[name] + 1])

            def two_bank_slot(phase, j, i=None, step=0, reduce=None):
                s = Slot(phase, j, i, step)
                pe.wait_ge(split_lo, s.split + 2)
                for b in range(2):
                    if b and reduce:
                        ada_reduce(*reduce)
                    wait_acc(b, turn(phase, j, i, step))
                    features(s, b, [at_col((2 * b + q) * P) for q in range(2)], h_hi, h_lo).then_inc(parts_done, 1)

            def four_blocks(phase, slots, first=0):
                for j in range(first, slots):
                    two_bank_slot(phase, j)

            def as_chunks_arrive(phase, name, work=None, order=range(4)):
                s = Slot(phase, 0)
                wh, wl = ring(w_hi, s.slot, s.kc, s.cols), ring(w_lo, s.slot, s.kc, s.cols)
                low_part, before = (mix_lo, 4 * name) if isinstance(name, int) else (norm_lo, NORM_PAIRS[NORM_AT[name]])
                if work is None:
                    work = [("features", (2 * b * P, (2 * b + 1) * P)) for b in range(2)]
                regions = []
                for b, (kind, *what) in enumerate(work):
                    if kind == "features":
                        regions.append([(ps[:, b, q * T:(q + 1) * T],
                                         lambda c, col=col: (wh[:, c, col:col + P], wl[:, c, col:col + P], h_hi[:, c, :], h_lo[:, c, :]))
                                        for q, col in enumerate(what[0])])
                    else:
                        col, n, tiles = what
                        regions.append([(ps[:, b, to:to + n],
                                         lambda c, t=t: (h_hi[:, c, t * P:(t + 1) * P], h_lo[:, c, t * P:(t + 1) * P],
                                                         wh[:, c, col:col + n], wl[:, c, col:col + n]))
                                        for t, to in tiles])
                pe.wait_ge(split_lo, s.split + 2)
                for b in range(2):
                    if turn(phase, 0):
                        wait_acc(b, turn(phase, 0))
                for p, pair in enumerate(order):
                    pe.wait_ge(low_part, before + p + 1)
                    for b in range(2):
                        for r, (to, operands) in enumerate(regions[b]):
                            for c in (2 * pair, 2 * pair + 1):
                                ins = product(to, *operands(c), p == 0 and c == 2 * pair and r == 0,
                                              p == 3 and c == 2 * pair + 1 and r == len(regions[b]) - 1)
                        if p == 3:
                            ins.then_inc(parts_done, 1)

            def turn_pair(bank, src, ncols=P):
                for ch in range(2):
                    for t in range(NT):
                        ins = nc.tensor.transpose(ps[0:ncols, bank, ch * T + t * P:ch * T + (t + 1) * P], src(ch, t), ident[:, :])
                return ins

            pe.wait_ge(consts, 2)
            pe.wait_ge(mem_loaded, 16)
            for q in range(4):
                turn_pair(2 + q, lambda ch, t: rows_mem[:, t, (2 * q + ch) * P:(2 * q + ch + 1) * P]).then_inc(turned, 1)
            pe.wait_ge(vec_loaded, 16 * len(vector_loads))
            nc.tensor.transpose(ps[:, ADA_BANK, 0:ROWS_A], rows_a[0:ROWS_A, :], ident[0:ROWS_A, 0:ROWS_A])
            nc.tensor.transpose(ps[:, ADA_BANK, T:T + ROWS_B], rows_b[0:ROWS_B, :], ident[0:ROWS_B, 0:ROWS_B]).then_inc(turned, 1)
            norm_sum_all("mem")
            pe.wait_ge(x_loaded, 16)
            for q in range(4):
                pe.wait_ge(unturned, q + 1)
                turn_pair(2 + q, lambda ch, t: rows_x[:, t, (2 * q + ch) * P:(2 * q + ch + 1) * P]).then_inc(turned, 1)

            as_chunks_arrive("mem", "mem", [("features", (0, P)), ("rows", CROSS, CROSS, [(0, 0), (1, T)])])
            s = Slot("mem", 1)
            pe.wait_ge(split_lo, s.split + 2)
            wait_acc(0, 1)
            features(s, 0, [at_col(0), at_col(P)], h_hi, h_lo).then_inc(parts_done, 1)
            norm_sum_all("attn0")
            wait_acc(1, 1)
            token_rows(s, ps[:, 1, 0:T], 0, CROSS, CROSS, h_hi, h_lo, last=False)
            token_rows(s, ps[:, 1, T:2 * T], 1, CROSS, CROSS, h_hi, h_lo, first=False).then_inc(parts_done, 1)

            as_chunks_arrive("w_in", "attn0")
            s, t = Slot("w_in", 1), turn("w_in", 1)
            pe.wait_ge(split_lo, s.split + 2)
            wait_acc(0, t)
            features(s, 0, [at_col(0), at_col(P + ROPE)], h_hi, h_lo).then_inc(parts_done, 1)
            norm_sum_all("qn")
            wait_acc(1, t)
            features(s, 1, [at_col(2 * P + ROPE)], h_hi, h_lo, last=False)
            for tile in range(NT):
                ins = token_rows(s, ps[:, 1, T + tile * ROPE:T + (tile + 1) * ROPE], tile, P, ROPE, h_hi, h_lo,
                                 first=False, last=tile == 1)
            ins.then_inc(parts_done, 1)
            norm_sum_all("kvn")
            for phase, name, hi, lo, n in (("w_uq", "qn", cq_hi, cq_lo, 4 * QK), ("w_ukv", "kvn", ckv_hi, ckv_lo, 8 * HD)):
                s = Slot(phase, 0)
                wait_norm(name)
                pe.wait_ge(split_lo, s.split + 2)
                for g in range(3):
                    for tile in range(NT):
                        wait_acc(tile, turn(phase, g))
                        token_rows(s, ps[:, tile, 0:n], tile, g * n, n, hi, lo).then_inc(parts_done, 1)
            pe.wait_ge(rope_done, 1)
            pe.wait_ge(resid_ready, 4)
            for c in range(2):
                pe.wait_ge(acc_out[c], turn("w_ukv", 2) + 1)
            for j in range(6):
                if j >= 2:
                    pe.wait_ge(q_out, j - 1)
                turn_pair(2 + j % 2, lambda ch, t: q_rows[:, t, 2 * j + ch, :], QK).then_inc(qk_banks, 1)
                if j >= 2:
                    pe.wait_ge(k_out, j - 1)
                turn_pair(4 + j % 2, lambda ch, t: k_rows[:, t, 2 * j + ch, :], QK).then_inc(qk_banks, 1)

            def score_head(hc):
                kind, l, h = HEADS[hc]
                if hc >= 3:
                    pe.wait_ge(exped if HEADS[hc - 3][0] == "cross" else biased, hc - 2)
                s = ps[:, SCORE_BANKS[hc % 3], :]
                if kind == "cross":
                    rows_of = slice(h % 2 * HD, (h % 2 + 1) * HD)
                    q, k = (qx0 if l == 0 else qx1)[rows_of, h // 2, :], (mem_k0 if l == 0 else mem_k1)[rows_of, h // 2, :]
                    nc.tensor.matmul(s[:, 0:T], q[:, 0:P], k, start=True, stop=False, skip_group_check=True)
                    nc.tensor.matmul(s[:, T:2 * T], q[:, P:T], k, start=False, stop=True, skip_group_check=True).then_inc(scores, 1)
                    return
                if kind == "mla":
                    q, k = mla_qT[0:QK, h, :], mla_kT[0:QK, h, :]
                else:
                    kv = h // SWA_GROUP
                    rows_of = slice(h % 2 * HD, (h % 2 + 1) * HD)
                    keys = swa_kT if h % 2 == kv % 2 else swa_kT_swapped
                    q, k = swa_qT[rows_of, h // 2, :], keys[rows_of, kv // 2, :]
                nc.tensor.matmul(s[:, 0:P], q[:, 0:P], k[:, 0:P], start=True, stop=False, skip_group_check=True)
                nc.tensor.matmul(s[:, P:3 * P], q[:, P:T], k, start=False, stop=True, skip_group_check=True).then_inc(scores, 1)

            def prob_blocks(hc):
                return [(0, 0), (0, 1), (1, 0), (1, 1)] if HEADS[hc][0] == "cross" else [(0, 0), (1, 0), (1, 1)]

            def turn_probs(hc):
                kind, l, h = HEADS[hc]
                pe.wait_ge(exped, hc + 1)
                if hc >= 3:
                    pe.wait_ge(probs_copied, hc - 2)
                p = (probs0 if l == 0 else probs1)[:, hc % 3, :]
                for n in range(len(prob_blocks(hc))):
                    ins = nc.tensor.transpose(ps[:, TURNED_BANKS[hc % 3], n * P:(n + 1) * P], p[:, n * P:(n + 1) * P], ident[:, :])
                ins.then_inc(probs_turned, 1)

            def values_head(hc):
                kind, l, h = HEADS[hc]
                g, j = hc // 4, hc % 4
                pe.wait_ge(probs_copied, hc + 1)
                if j == 0 and g >= 2:
                    pe.wait_ge(o_copied, g - 1)
                p = (probsT0 if l == 0 else probsT1)[:, hc % 3, :]
                blocks = prob_blocks(hc)
                for n, (qt, kt) in enumerate(blocks):
                    if kind == "mla":
                        v = v_rows[:, kt, h, :]
                    elif kind == "swa":
                        v = swa_v[:, kt, h // SWA_GROUP * HD:(h // SWA_GROUP + 1) * HD]
                    else:
                        v = (mem_v0 if l == 0 else mem_v1)[:, kt, h * HD:(h + 1) * HD]
                    ins = nc.tensor.matmul(ps[:, 6 + g % 2, qt * T + j * HD:qt * T + (j + 1) * HD], p[:, n * P:(n + 1) * P], v,
                                           start=j == 0 and n == 0, stop=j == 3 and n == len(blocks) - 1, skip_group_check=True)
                ins.then_inc(heads_done, 1)

            def heads(first, last):
                score_head(first)
                score_head(first + 1)
                for hc in range(first, last + 1):
                    if hc + 2 < last:
                        score_head(hc + 2)
                    if hc < last:
                        turn_probs(hc)
                    if hc > first:
                        values_head(hc - 1)

            def mix_turn(n, rows_from, copied):
                pe.wait_ge(o_copied, copied)
                for q in range(4):
                    turn_pair(2 + q, lambda ch, t: rows_from[:, t, (2 * q + ch) * P:(2 * q + ch + 1) * P]).then_inc(mix_turned, 1)

            pe.wait_ge(q_out, 6)
            pe.wait_ge(k_out, 6)
            heads(0, 16)
            mix_turn(0, o_rows0, 4)
            as_chunks_arrive("w_o0", 0)
            two_bank_slot("w_o0", 1)

            def ada_reduce(group, col):
                pe.wait_ge(ada_step, group * 8 + 8)
                for q in range(4):
                    to = ps[:, ADA_BANK, col + q:col + q + 1] if isinstance(col, int) else ps[:, ADA_BANK, bass.ds(col + q, 1)]
                    ins = nc.tensor.matmul(to, scratch[:, q // 2, (q % 2) * P:(q % 2 + 1) * P], ones[:, 0:1],
                                           start=True, stop=True)
                ins.then_inc(ada_reduced, 1)

            def mlp(l):
                norm_sum_all(f"mlp{l}")
                as_chunks_arrive(f"up{l}", f"mlp{l}")
                two_bank_slot(f"up{l}", 1)
                with pe.Fori(1, 4) as i:
                    two_bank_slot(f"up{l}", 0, i, 2, reduce=(i + (8 * l - 1), i * 4 - 4))
                    two_bank_slot(f"up{l}", 1, i, 2)
                for i in range(2):
                    for j in range(4):
                        s = Slot(f"down{l}", 4 * i + j)
                        pe.wait_ge(hid_lo, HIDDEN_BEFORE[str(l)] + 4 * (j + 1))
                        pe.wait_ge(split_lo, s.split + 2)
                        for b in range(2):
                            if j == 0:
                                wait_acc(b, turn(f"down{l}", i))
                            if b == 1 and j % 2 == 0:
                                before = 3 + 2 * i + j // 2
                                ada_reduce(8 * l + before, 4 * before)
                            features(s, b, [at_col((2 * b + q) * P) for q in range(2)], a_hi, a_lo, first=j == 0, last=j == 3,
                                     chunk=KD * j).then_inc(parts_done, 1)
                ada_reduce(8 * l + 7, 28)

            mlp(0)

            norm_sum_all("attn1")
            as_chunks_arrive("swa", "attn1", [("features", (0, P)), ("features", (2 * P,))])
            for j in range(1, 4):
                s, t = Slot("swa", j), turn("swa", j)
                pe.wait_ge(split_lo, s.split + 2)

                wait_acc(0, t)
                blocks = [at_col(0), at_col(P)] if j < 3 else [at_col(P), at_col(2 * P)]
                features(s, 0, blocks, h_hi, h_lo).then_inc(parts_done, 1)
                wait_acc(1, t)
                if j < 2:
                    features(s, 1, [at_col(2 * P)], h_hi, h_lo).then_inc(parts_done, 1)
                else:
                    col = 2 * P if j == 2 else 0
                    token_rows(s, ps[:, 1, 0:P], 0, col, P, h_hi, h_lo, last=False)
                    token_rows(s, ps[:, 1, P:2 * P], 1, col, P, h_hi, h_lo, first=False).then_inc(parts_done, 1)
            for c in range(2):
                pe.wait_ge(acc_out[c], turn("swa", 3) + 1)
            heads(16, 32)
            mix_turn(1, o_rows1, 8)
            as_chunks_arrive("w_o1", 1)
            two_bank_slot("w_o1", 1)
            mlp(1)

            norm_sum_all("final")
            norm_sum_all("mix0")
            as_chunks_arrive("lru_in", "mix0")
            four_blocks("lru_in", 3, first=1)
            pe.wait_ge(rg_loaded, 64)
            pe.wait_ge(xr_ready, 1)
            for g in range(2):
                for c in range(4):
                    ins = nc.tensor.matmul(ps[:, 2 + 2 * g + c // 2, c % 2 * T:(c % 2 + 1) * T], rg_w[:, g, c, :], xr[:, c, :],
                                           start=c % 2 == 0, stop=c % 2 == 1, skip_group_check=True)
                    if c % 2:
                        ins.then_inc(gates, 1)
            four_blocks("lru_in", 5, first=3)
            as_chunks_arrive("lru_out", 2, order=LRU_PAIRS)
            two_bank_slot("lru_out", 1)

            def ffn(l):
                norm_sum_all(f"ffn{l}")
                as_chunks_arrive(f"gate_up{l}", f"ffn{l}")
                two_bank_slot(f"gate_up{l}", 1)
                with pe.Fori(1, 5) as i:
                    two_bank_slot(f"gate_up{l}", 0, i, 2, reduce=(i + 15, i * 4 - 4) if l == 0 else None)
                    two_bank_slot(f"gate_up{l}", 1, i, 2)
                two_bank_slot(f"gate_up{l}", 10, reduce=(20, 16) if l == 0 else None)

                def down(i, reduce=None):
                    for j in range(2):
                        s = Slot(f"ffn_down{l}", 2 * i + j) if isinstance(i, int) else Slot(f"ffn_down{l}", j, i, 2)
                        pe.wait_ge(hid_lo, HIDDEN_BEFORE[f"ffn{l}"] + (6 if j == 0 else 11))
                        pe.wait_ge(split_lo, s.split + 2)
                        for b in range(2):
                            if j == 0:
                                wait_acc(b, i + turn(f"ffn_down{l}", 0))
                            if j == 0 and b == 1 and reduce and l == 0:
                                ada_reduce(*reduce)
                            features(s, b, [at_col(b * P)], a_hi, a_lo, first=j == 0, last=j == 1, chunk=11 * j).then_inc(parts_done, 1)

                down(0)
                with pe.Fori(1, 3) as i:
                    down(i, reduce=(i + 20, i * 4 + 16))
                down(3, reduce=(23, 28))

            ffn(0)
            norm_sum_all("mix1")

            def turn_qk(j):
                pe.wait_ge(qk_scaled, j + 1)
                for q in range(2):
                    if j >= 2:
                        pe.wait_ge(qk_out, 2 * (j - 2) + q + 1)
                    turn_pair(2 + 2 * (j % 2) + q, lambda ch, t: sb_rows[:, j // 2, t, (4 * (j % 2) + 2 * q + ch) * P:
                                                                         (4 * (j % 2) + 2 * q + ch + 1) * P]).then_inc(qk_turned, 1)

            def z_head(h):
                rows_of, c = slice(h % 2 * HD, (h % 2 + 1) * HD), h // 2
                if h >= 3:
                    pe.wait_ge(u_ready, h - 2)
                z = ps[:, SCORE_BANKS[h % 3], :]
                nc.tensor.matmul(z[:, 0:T], sb_kT[rows_of, c, 0:P], sb_qT[rows_of, c, :], start=True, stop=False,
                                 skip_group_check=True)
                nc.tensor.matmul(z[:, T:T + P], sb_kT[rows_of, c, P:T], sb_qT[rows_of, c, P:T], start=False, stop=True,
                                 skip_group_check=True).then_inc(z_ready, 1)

            as_chunks_arrive("qkv", "mix1", [("rows", 0, BANK, [(b, 0)]) for b in range(2)])
            for j in range(1, 6):
                s, t = Slot("qkv", j), turn("qkv", j)
                pe.wait_ge(split_lo, s.split + 2)
                for b in range(2):
                    if (j, b) == (5, 1):
                        pe.wait_ge(qk_out, 8)
                        z_head(0)
                        z_head(1)
                    wait_acc(b, t)
                    token_rows(s, ps[:, b, :], b, 0, BANK, h_hi, h_lo).then_inc(parts_done, 1)
                if 1 <= j < 5:
                    turn_qk(j - 1)
            for c in range(2):
                pe.wait_ge(acc_out[c], turn("qkv", 5) + 1)
            pe.wait_ge(pool_step, 12)

            def sum_head(h):
                pe.wait_ge(sp_masked, h + 1)
                if h >= 3:
                    pe.wait_ge(logw_ready, h - 2)
                to, sp_of = ps[:, TURNED_BANKS[h % 3], :], sb_sp[:, h % 3, :]
                nc.tensor.matmul(to[:, 0:384], suffix[:, :], sp_of, start=True, stop=False, skip_group_check=True)
                nc.tensor.matmul(to[:, P:T], ones[:, :], sp_of[:, T:T + P], start=False, stop=True,
                                 skip_group_check=True).then_inc(sums_ready, 1)

            def sb_values(h):
                g, j = h // 4, h % 4
                pe.wait_ge(w_masked, h + 1)
                if j == 0 and g >= 2:
                    pe.wait_ge(o_copied, len(HEADS) // 4 + g - 1)
                for n, (qt, kt) in enumerate(((0, 0), (1, 0), (1, 1))):
                    ins = nc.tensor.matmul(ps[:, 6 + g % 2, qt * T + j * HD:qt * T + (j + 1) * HD],
                                           sb_u[:, h % 3, n * P:(n + 1) * P], sb_rows[:, 2, kt, h * HD:(h + 1) * HD],
                                           start=j == 0 and n == 0, stop=j == 3 and n == 2, skip_group_check=True)
                ins.then_inc(heads_done, 1)

            for h in range(SB_HEADS + 2):
                if h + 2 < SB_HEADS:
                    z_head(h + 2)
                if h < SB_HEADS:
                    sum_head(h)
                if h >= 2:
                    sb_values(h - 2)
            mix_turn(2, sb_o, 12)
            as_chunks_arrive("sb_out", 3)
            two_bank_slot("sb_out", 1)
            ffn(1)
            wait_source(pe, "out")
            for t in range(NT):
                for q in range(2):
                    for ch in range(4):
                        ins = nc.tensor.transpose(ps[:, 2 + 2 * t + q, ch * P:(ch + 1) * P],
                                                  xT[:, 4 * q + ch, t * P:(t + 1) * P], ident[:, :])
                    ins.then_inc(turned, 1)


_OUT = ((1, T, D), "float32")


def kernel(**inputs):
    import numpy as np
    import concourse.bacc as bacc
    from concourse.bass_utils import run_bass_kernel_spmd as run

    nc = bacc.Bacc("TRN2", target_bir_lowering=False, num_devices=1)
    arrays, args = {}, {}
    for name, value in inputs.items():
        v = np.ascontiguousarray(value)
        arrays[f"in_{name}"] = v
        args[name] = nc.dram_tensor(f"in_{name}", v.shape, mybir.dt.from_np(v.dtype), kind="ExternalInput").ap()
    out = nc.dram_tensor("out_0", _OUT[0], F32, kind="ExternalOutput").ap()
    build(nc, args, out)
    r = run(nc, [arrays], core_ids=[0])
    return r.results[0]["out_0"]
```
